# Optimizing a Trainium2 kernel written in Bass

```python
import math
import jax
import jax.numpy as jnp
from jax import lax
import numpy as np
import jax, jax.numpy as jnp

D_MODEL = 1024
BATCH = 1
SEQ = 512
DEPTH = 1

CTX_LEN = 256
GRID_W = 64
EPS = 1e-6

N_ATTN_HEADS = 8
ATTN_DH = 64
ATTN_DV = 2 * ATTN_DH
ATTN_QK_DIM = N_ATTN_HEADS * 2 * ATTN_DH
ATTN_V_DIM = N_ATTN_HEADS * ATTN_DV
ATTN_SCALE = ATTN_DH ** -0.5
ATTN_QBLOCK = 128
ROPE_THETA = 10000.0
ROPE_AXIS_DIM = ATTN_DH // 2

D_SSD = D_MODEL
SSD_HEADDIM = 64
SSD_HEADS = D_SSD // SSD_HEADDIM
SSD_GROUPS = 4
SSD_HPG = SSD_HEADS // SSD_GROUPS
SSD_STATE = 128
SSD_CONV_W = 3
SSD_CHUNK = 64
XBC_DIM = D_SSD + 2 * SSD_GROUPS * SSD_STATE

IN_SPLITS = (ATTN_QK_DIM, 2 * ATTN_QK_DIM, 2 * ATTN_QK_DIM + ATTN_V_DIM, 2 * ATTN_QK_DIM + ATTN_V_DIM + D_SSD, 2 * ATTN_QK_DIM + ATTN_V_DIM + D_SSD + XBC_DIM, 2 * ATTN_QK_DIM + ATTN_V_DIM + D_SSD + XBC_DIM + 2 * SSD_HEADS)
IN_COLS = IN_SPLITS[-1] + 2 * D_MODEL

N_EXPERTS = 64
EXPERT_FF = 256
SHARED_FF = 256
TOP_K = 8
N_EXPERT_GROUPS = 8
TOPK_GROUPS = 4
ROUTED_SCALE = 2.5
MOE_BLOCK = 128


def rmsnorm(u, g):
    uf = u.astype(jnp.float32)
    y = uf * lax.rsqrt(jnp.mean(uf * uf, axis=-1, keepdims=True) + EPS)
    return (y * g.astype(jnp.float32)).astype(u.dtype)

def modulate(u, shift, scale):
    return u * (1 + scale) + shift

def rev(t):
    return jnp.flip(t, axis=1)

def axial_rope_tables(n_tok):
    rows = n_tok // GRID_W
    row = jnp.repeat(jnp.arange(rows, dtype=jnp.float32), GRID_W)
    col = jnp.broadcast_to(jnp.arange(GRID_W, dtype=jnp.float32)[None, :], (rows, GRID_W)).reshape(-1)
    inv_freq = ROPE_THETA ** (-jnp.arange(0, ROPE_AXIS_DIM, 2, dtype=jnp.float32) / ROPE_AXIS_DIM)
    ang = jnp.concatenate([row[:, None] * inv_freq, col[:, None] * inv_freq], axis=-1)
    ang = jnp.concatenate([ang, ang], axis=-1)
    return jnp.cos(ang), jnp.sin(ang)

def apply_rope(u, cos, sin):
    half = ATTN_DH // 2
    uf = u.astype(jnp.float32)
    rot = jnp.concatenate([-uf[..., half:], uf[..., :half]], axis=-1)
    return (uf * cos[:, None, None, :] + rot * sin[:, None, None, :]).astype(u.dtype)

def diff_attend(q, k, v, lam, g_subln, lam_init):
    s = jnp.einsum('bqhcd,bkhcd->bchqk', q.astype(jnp.float32), k.astype(jnp.float32)) * ATTN_SCALE
    p = jax.nn.softmax(s, axis=-1)
    w = p[:, 0] - lam * p[:, 1]
    o = jnp.einsum('bhqk,bkhd->bqhd', w, v.astype(jnp.float32))
    o = o * lax.rsqrt(jnp.mean(o * o, axis=-1, keepdims=True) + EPS) * g_subln.astype(jnp.float32)
    return (o * (1.0 - lam_init)).astype(v.dtype)

def centred_dwconv(u, w, b):
    pad = SSD_CONV_W // 2
    n = u.shape[1]
    up = jnp.pad(u, ((0, 0), (pad, pad), (0, 0)))
    out = b
    for i in range(SSD_CONV_W):
        out = out + up[:, i:i + n] * w[i]
    return out

def ssd_inputs(xbc, dt_raw, conv_w, conv_b, dt_bias):
    nb, nl, _ = xbc.shape
    u = jax.nn.silu(centred_dwconv(xbc, conv_w, conv_b)).astype(jnp.float32)
    xs, bm, cm = jnp.split(u, (D_SSD, D_SSD + SSD_GROUPS * SSD_STATE), axis=-1)
    xh = xs.reshape(nb, nl, SSD_GROUPS, SSD_HPG, SSD_HEADDIM)
    bm = bm.reshape(nb, nl, SSD_GROUPS, SSD_STATE)
    cm = cm.reshape(nb, nl, SSD_GROUPS, SSD_STATE)
    dt = jax.nn.softplus(dt_raw.astype(jnp.float32).reshape(nb, nl, 2, SSD_GROUPS, SSD_HPG) + dt_bias.astype(jnp.float32).reshape(2, SSD_GROUPS, SSD_HPG))
    return xh, bm, cm, dt[:, :, 0], dt[:, :, 1]

def ssd_chunked(xh, dt, a, bm, cm, h0, with_output):
    nb, nl, ng, nr, npd = xh.shape
    nn = bm.shape[-1]
    nc = nl // SSD_CHUNK
    xc = xh.reshape(nb, nc, SSD_CHUNK, ng, nr, npd)
    dtc = dt.reshape(nb, nc, SSD_CHUNK, ng, nr)
    bc = bm.reshape(nb, nc, SSD_CHUNK, ng, nn)
    acum = jnp.cumsum(dtc * a, axis=2)
    to_end = jnp.exp(acum[:, :, -1:] - acum)
    states = jnp.einsum('bcqgn,bcqgr,bcqgrp->bcgrpn', bc, to_end * dtc, xc)
    chunk_decay = jnp.exp(acum[:, :, -1])

    def step(h, inp):
        st, dec = inp
        return h * dec[..., None, None] + st, (h if with_output else None)

    h_last, h_prev = lax.scan(step, h0, (jnp.moveaxis(states, 1, 0), jnp.moveaxis(chunk_decay, 1, 0)))
    if not with_output:
        return None, h_last
    cc = cm.reshape(nb, nc, SSD_CHUNK, ng, nn)
    seg = acum[:, :, :, None] - acum[:, :, None]
    lower = (jnp.arange(SSD_CHUNK)[:, None] >= jnp.arange(SSD_CHUNK)[None, :])[:, :, None, None]
    decay = jnp.where(lower, jnp.exp(jnp.where(lower, seg, 0.0)), 0.0)
    cb = jnp.einsum('bcign,bcjgn->bcijg', cc, bc)
    y_diag = jnp.einsum('bcijg,bcijgr,bcjgr,bcjgrp->bcigrp', cb, decay, dtc, xc)
    y_off = jnp.einsum('bcign,cbgrpn,bcigr->bcigrp', cc, h_prev, jnp.exp(acum))
    y = (y_diag + y_off).reshape(nb, nl, ng, nr, npd)
    return y, h_last

def merge_branches(o_attn, y_ssd, z, gates, g_ssd_norm, w_branch_attn, w_branch_ssd, w_out):
    out_dtype = z.dtype
    y = y_ssd * jax.nn.silu(z.astype(jnp.float32))
    shp = y.shape
    yg = y.reshape(shp[:-1] + (SSD_GROUPS, D_SSD // SSD_GROUPS))
    yg = yg * lax.rsqrt(jnp.mean(yg * yg, axis=-1, keepdims=True) + EPS)
    y = (yg.reshape(shp) * g_ssd_norm.astype(jnp.float32)).astype(out_dtype)
    ya = o_attn @ w_branch_attn
    ys = y @ w_branch_ssd
    g_a, g_s = jnp.split(jax.nn.sigmoid(gates), 2, axis=-1)
    return (g_a * ya + g_s * ys) @ w_out

def token_mixer(h, hc, update_ctx, lam_init, w_in, lam_q1, lam_k1, lam_q2, lam_k2, g_attn_subln, conv_w, conv_b, dt_bias, a_log, d_skip, g_ssd_norm, w_branch_attn, w_branch_ssd, w_out):
    nb, ns, _ = h.shape
    nl = hc.shape[1]
    w_q, w_k, w_v, w_z, w_xbc, w_dt, w_g = jnp.split(w_in, IN_SPLITS, axis=1)
    q, k, v, z, xbc, dt_raw, gates = jnp.split(h @ w_in, IN_SPLITS, axis=-1)

    lam = (jnp.exp(jnp.sum(lam_q1.astype(jnp.float32) * lam_k1.astype(jnp.float32)))
           - jnp.exp(jnp.sum(lam_q2.astype(jnp.float32) * lam_k2.astype(jnp.float32))) + lam_init)
    cos, sin = axial_rope_tables(ns)
    q = apply_rope(q.reshape(nb, ns, N_ATTN_HEADS, 2, ATTN_DH), cos, sin)
    k = apply_rope(k.reshape(nb, ns, N_ATTN_HEADS, 2, ATTN_DH), cos, sin)
    v = v.reshape(nb, ns, N_ATTN_HEADS, ATTN_DV)
    kc = (hc @ w_k).reshape(nb, nl, N_ATTN_HEADS, 2, ATTN_DH)
    vc = (hc @ w_v).reshape(nb, nl, N_ATTN_HEADS, ATTN_DV)
    k_all = jnp.concatenate([kc, k], axis=1)
    v_all = jnp.concatenate([vc, v], axis=1)
    n_qb = ns // ATTN_QBLOCK
    q_blocks = jnp.swapaxes(q.reshape(nb, n_qb, ATTN_QBLOCK, N_ATTN_HEADS, 2, ATTN_DH), 0, 1)
    o = lax.map(lambda qb: diff_attend(qb, k_all, v_all, lam, g_attn_subln, lam_init), q_blocks)
    o_lat = jnp.swapaxes(o, 0, 1).reshape(nb, ns, ATTN_V_DIM)

    a = -jnp.exp(a_log.astype(jnp.float32)).reshape(2, SSD_GROUPS, SSD_HPG)
    d = d_skip.astype(jnp.float32).reshape(SSD_GROUPS, SSD_HPG, 1)
    xh_c, bm_c, cm_c, dtf_c, dtb_c = ssd_inputs(hc @ w_xbc, hc @ w_dt, conv_w, conv_b, dt_bias)
    h0 = jnp.zeros((nb, SSD_GROUPS, SSD_HPG, SSD_HEADDIM, SSD_STATE), jnp.float32)
    yf_c, hf = ssd_chunked(xh_c, dtf_c, a[0], bm_c, cm_c, h0, update_ctx)
    yb_c, hb = ssd_chunked(rev(xh_c), rev(dtb_c), a[1], rev(bm_c), rev(cm_c), h0, update_ctx)
    xh, bm, cm, dtf, dtb = ssd_inputs(xbc, dt_raw, conv_w, conv_b, dt_bias)
    yf, _ = ssd_chunked(xh, dtf, a[0], bm, cm, hf, True)
    yb, _ = ssd_chunked(rev(xh), rev(dtb), a[1], rev(bm), rev(cm), hb, True)
    y_lat = (yf + rev(yb) + d * xh).reshape(nb, ns, D_SSD)

    out_lat = merge_branches(o_lat, y_lat, z, gates, g_ssd_norm, w_branch_attn, w_branch_ssd, w_out)
    if not update_ctx:
        return out_lat, None
    qc = (hc @ w_q).reshape(nb, nl, N_ATTN_HEADS, 2, ATTN_DH)
    o_ctx = diff_attend(qc, kc, vc, lam, g_attn_subln, lam_init).reshape(nb, nl, ATTN_V_DIM)
    y_ctx = (yf_c + rev(yb_c) + d * xh_c).reshape(nb, nl, D_SSD)
    out_ctx = merge_branches(o_ctx, y_ctx, hc @ w_z, hc @ w_g, g_ssd_norm, w_branch_attn, w_branch_ssd, w_out)
    return out_lat, out_ctx

def moe_ffn(h, w_router, router_bias, w_e_gate, w_e_up, w_e_down, w_sh_gate, w_sh_up, w_sh_down):
    n_tok, d = h.shape
    scores = jax.nn.sigmoid((h @ w_router).astype(jnp.float32))
    sel = scores + router_bias.astype(jnp.float32)
    grp = sel.reshape(n_tok, N_EXPERT_GROUPS, N_EXPERTS // N_EXPERT_GROUPS)
    grp_score = lax.top_k(grp, 2)[0].sum(-1)
    top_g = lax.top_k(grp_score, TOPK_GROUPS)[1]
    gmask = jax.nn.one_hot(top_g, N_EXPERT_GROUPS, dtype=jnp.float32).sum(1) > 0
    emask = jnp.repeat(gmask, N_EXPERTS // N_EXPERT_GROUPS, axis=1)
    top_e = lax.top_k(jnp.where(emask, sel, -jnp.inf), TOP_K)[1]
    wts = jnp.take_along_axis(scores, top_e, axis=1)
    wts = wts / jnp.sum(wts, axis=-1, keepdims=True) * ROUTED_SCALE

    n_assign = n_tok * TOP_K
    n_blocks = -(-n_assign // MOE_BLOCK) + N_EXPERTS
    n_pad = n_blocks * MOE_BLOCK
    e_flat = top_e.reshape(-1)
    order = jnp.argsort(e_flat)
    e_sorted = e_flat[order]
    tok_sorted = (jnp.arange(n_assign, dtype=jnp.int32) // TOP_K)[order]
    w_sorted = wts.reshape(-1)[order]
    counts = jnp.bincount(e_flat, length=N_EXPERTS)
    start = jnp.cumsum(counts) - counts
    padded = (counts + MOE_BLOCK - 1) // MOE_BLOCK * MOE_BLOCK
    pend = jnp.cumsum(padded)
    pstart = pend - padded
    dest = pstart[e_sorted] + jnp.arange(n_assign, dtype=jnp.int32) - start[e_sorted]
    buf_tok = jnp.zeros((n_pad,), jnp.int32).at[dest].set(tok_sorted)
    buf_w = jnp.zeros((n_pad,), jnp.float32).at[dest].set(w_sorted)
    block_e = jnp.minimum(jnp.searchsorted(pend, jnp.arange(n_blocks, dtype=jnp.int32) * MOE_BLOCK, side='right'), N_EXPERTS - 1)

    def expert_block(args):
        tok_b, w_b, e = args
        xb = h[tok_b]
        hid = jax.nn.silu(xb @ w_e_gate[e]) * (xb @ w_e_up[e])
        return (hid @ w_e_down[e]) * w_b[:, None].astype(h.dtype)

    out = lax.map(expert_block, (buf_tok.reshape(n_blocks, MOE_BLOCK), buf_w.reshape(n_blocks, MOE_BLOCK), block_e))
    routed = jax.ops.segment_sum(out.reshape(n_pad, d), buf_tok, num_segments=n_tok)
    shared = (jax.nn.silu(h @ w_sh_gate) * (h @ w_sh_up)) @ w_sh_down
    return routed + shared

def first_inputs(seed: int = 0) -> dict:
    key = jax.random.key(seed)
    ks = jax.random.split(key, 40)
    f32 = jnp.float32

    def nrm(k, shape, scale):
        return jax.random.normal(k, shape, f32) * scale

    def gain(k, shape):
        return 1.0 + 0.05 * jax.random.normal(k, shape, f32)

    u_dt = jax.random.uniform(ks[18], (DEPTH, 2, SSD_HEADS), f32)
    dt0 = jnp.exp(u_dt * (math.log(0.1) - math.log(0.001)) + math.log(0.001))
    return {
        'x': nrm(ks[0], (BATCH, SEQ, D_MODEL), 1.0),
        'c': nrm(ks[1], (BATCH, D_MODEL), 1.0),
        'ctx': nrm(ks[2], (BATCH, CTX_LEN, D_MODEL), 1.0),
        'c_ctx': nrm(ks[3], (D_MODEL,), 1.0),
        'w_ada': nrm(ks[4], (DEPTH, D_MODEL, 6 * D_MODEL), 0.5 * D_MODEL ** -0.5),
        'b_ada': nrm(ks[5], (DEPTH, 6 * D_MODEL), 0.02),
        'g_pre_mix': gain(ks[6], (DEPTH, D_MODEL)),
        'g_post_mix': gain(ks[7], (DEPTH, D_MODEL)),
        'g_pre_ffn': gain(ks[8], (DEPTH, D_MODEL)),
        'g_post_ffn': gain(ks[9], (DEPTH, D_MODEL)),
        'w_in': nrm(ks[10], (DEPTH, D_MODEL, IN_COLS), D_MODEL ** -0.5),
        'lam_q1': nrm(ks[11], (DEPTH, ATTN_DH), 0.1),
        'lam_k1': nrm(ks[12], (DEPTH, ATTN_DH), 0.1),
        'lam_q2': nrm(ks[13], (DEPTH, ATTN_DH), 0.1),
        'lam_k2': nrm(ks[14], (DEPTH, ATTN_DH), 0.1),
        'g_attn_subln': gain(ks[15], (DEPTH, ATTN_DV)),
        'conv_w': nrm(ks[16], (DEPTH, SSD_CONV_W, XBC_DIM), SSD_CONV_W ** -0.5),
        'conv_b': nrm(ks[17], (DEPTH, XBC_DIM), 0.02),
        'dt_bias': dt0 + jnp.log(-jnp.expm1(-dt0)),
        'a_log': jnp.log(jax.random.uniform(ks[19], (DEPTH, 2, SSD_HEADS), f32, 1.0, 16.0)),
        'd_skip': gain(ks[20], (DEPTH, SSD_HEADS)),
        'g_ssd_norm': gain(ks[21], (DEPTH, D_SSD)),
        'w_branch_attn': nrm(ks[22], (DEPTH, ATTN_V_DIM, D_MODEL), ATTN_V_DIM ** -0.5),
        'w_branch_ssd': nrm(ks[23], (DEPTH, D_SSD, D_MODEL), D_SSD ** -0.5),
        'w_out': nrm(ks[24], (DEPTH, D_MODEL, D_MODEL), D_MODEL ** -0.5),
        'w_router': nrm(ks[25], (DEPTH, D_MODEL, N_EXPERTS), D_MODEL ** -0.5),
        'router_bias': nrm(ks[26], (DEPTH, N_EXPERTS), 0.01),
        'w_e_gate': nrm(ks[27], (DEPTH, N_EXPERTS, D_MODEL, EXPERT_FF), D_MODEL ** -0.5),
        'w_e_up': nrm(ks[28], (DEPTH, N_EXPERTS, D_MODEL, EXPERT_FF), D_MODEL ** -0.5),
        'w_e_down': nrm(ks[29], (DEPTH, N_EXPERTS, EXPERT_FF, D_MODEL), EXPERT_FF ** -0.5),
        'w_sh_gate': nrm(ks[30], (DEPTH, D_MODEL, SHARED_FF), D_MODEL ** -0.5),
        'w_sh_up': nrm(ks[31], (DEPTH, D_MODEL, SHARED_FF), D_MODEL ** -0.5),
        'w_sh_down': nrm(ks[32], (DEPTH, SHARED_FF, D_MODEL), SHARED_FF ** -0.5),
    }

def first_block(x, c, ctx, c_ctx, w_ada, b_ada, g_pre_mix, g_post_mix, g_pre_ffn, g_post_ffn, w_in, lam_q1, lam_k1, lam_q2, lam_k2, g_attn_subln, conv_w, conv_b, dt_bias, a_log, d_skip, g_ssd_norm, w_branch_attn, w_branch_ssd, w_out, w_router, router_bias, w_e_gate, w_e_up, w_e_down, w_sh_gate, w_sh_up, w_sh_down):
    nb, ns, d = x.shape
    for li in range(DEPTH):
        update_ctx = li < DEPTH - 1
        lam_init = 0.8 - 0.6 * math.exp(-0.3 * li)
        mod = jax.nn.silu(c) @ w_ada[li] + b_ada[li]
        sh1, sc1, gt1, sh2, sc2, gt2 = jnp.split(mod[:, None, :], 6, axis=-1)
        mod_c = jax.nn.silu(c_ctx) @ w_ada[li] + b_ada[li]
        sh1c, sc1c, gt1c, sh2c, sc2c, gt2c = jnp.split(mod_c, 6)

        h = modulate(rmsnorm(x, g_pre_mix[li]), sh1, sc1)
        hc = modulate(rmsnorm(ctx, g_pre_mix[li]), sh1c, sc1c)
        mix, mix_c = token_mixer(h, hc, update_ctx, lam_init, w_in[li], lam_q1[li], lam_k1[li], lam_q2[li], lam_k2[li], g_attn_subln[li], conv_w[li], conv_b[li], dt_bias[li], a_log[li], d_skip[li], g_ssd_norm[li], w_branch_attn[li], w_branch_ssd[li], w_out[li])
        x = x + gt1 * rmsnorm(mix, g_post_mix[li])

        h = modulate(rmsnorm(x, g_pre_ffn[li]), sh2, sc2)
        moe_w = (w_router[li], router_bias[li], w_e_gate[li], w_e_up[li], w_e_down[li], w_sh_gate[li], w_sh_up[li], w_sh_down[li])
        if update_ctx:
            ctx = ctx + gt1c * rmsnorm(mix_c, g_post_mix[li])
            hc = modulate(rmsnorm(ctx, g_pre_ffn[li]), sh2c, sc2c)
            f = moe_ffn(jnp.concatenate([h.reshape(-1, d), hc.reshape(-1, d)], axis=0), *moe_w)
            f_lat = f[: nb * ns]
            ctx = ctx + gt2c * rmsnorm(f[nb * ns:].reshape(ctx.shape), g_post_ffn[li])
        else:
            f_lat = moe_ffn(h.reshape(-1, d), *moe_w)
        x = x + gt2 * rmsnorm(f_lat.reshape(x.shape), g_post_ffn[li])
    return x


DEPTH_2 = 2

N_MIXERS = 2
N_A_LAYERS = (DEPTH_2 + 1) // 2
N_B_LAYERS = DEPTH_2 // 2
RMS_EPS = 1e-6
NEG_INF = -1e30

A_GROUPS = ((128, 1), (512, 4), (2048, 16))
A_N_GROUPS = len(A_GROUPS)
A_HEADS = 16
A_HEAD_DIM = D_MODEL // A_HEADS
A_WIDTH = A_HEADS * A_HEAD_DIM
A_IN_WIDTH = A_N_GROUPS * 3 * A_WIDTH

B_HEADS = 4
B_KEY_DIM = D_MODEL // 2 // B_HEADS
B_VAL_DIM = D_MODEL // B_HEADS
B_QK_WIDTH = B_HEADS * B_KEY_DIM
B_V_WIDTH = B_HEADS * B_VAL_DIM
B_GATE_RANK = 16
B_GATE_TAU = 16.0
B_CHUNK = 64
B_IN_WIDTH = 2 * B_QK_WIDTH + 2 * B_V_WIDTH + 2 * B_GATE_RANK

FFN_HIDDEN = -(-8 * D_MODEL // (3 * 256)) * 256


def rms_norm(x, gain):
    xf = x.astype(jnp.float32)
    y = xf * lax.rsqrt(jnp.mean(xf * xf, axis=-1, keepdims=True) + RMS_EPS)
    return (y * gain.astype(jnp.float32)).astype(x.dtype)

def rope(x, positions):
    half = x.shape[-1] // 2
    inv_freq = ROPE_THETA ** (-jnp.arange(half, dtype=jnp.float32) / half)
    ang = positions.astype(jnp.float32)[:, None] * inv_freq[None, :]
    cos = jnp.cos(ang)[:, None, :]
    sin = jnp.sin(ang)[:, None, :]
    xf = x.astype(jnp.float32)
    x1, x2 = xf[..., :half], xf[..., half:]
    return jnp.concatenate([x1 * cos - x2 * sin, x2 * cos + x1 * sin], axis=-1).astype(x.dtype)

def dilated_window_attention(q, k, v, window, dilation):
    bsz, seq, nh, dh = q.shape
    half = window // (2 * dilation)
    L = seq // dilation
    nb = -(-L // half)
    Lp = nb * half

    def to_phase(t):
        t = t.reshape(bsz, L, dilation, nh, dh)
        return jnp.moveaxis(t, 2, 1).reshape(bsz * dilation, L, nh, dh)

    n = bsz * dilation
    qp = jnp.pad(to_phase(q), ((0, 0), (0, Lp - L), (0, 0), (0, 0))).reshape(n, nb, half, nh, dh)

    def key_blocks(t):
        t = jnp.pad(to_phase(t), ((0, 0), (half, Lp - L + half), (0, 0), (0, 0)))
        t = t.reshape(n, nb + 2, half, nh, dh)
        return jnp.concatenate([t[:, :-2], t[:, 1:-1], t[:, 2:]], axis=2)

    kb = key_blocks(k)
    vb = key_blocks(v)
    tq = jnp.arange(nb)[:, None] * half + jnp.arange(half)[None, :]
    tk = jnp.arange(nb)[:, None] * half + jnp.arange(3 * half)[None, :] - half
    dist = tk[:, None, :] - tq[:, :, None]
    valid = (tk[:, None, :] >= 0) & (tk[:, None, :] < L) & (jnp.abs(dist) <= half)

    scores = jnp.einsum("nbqhd,nbkhd->nbhqk", qp.astype(jnp.float32), kb.astype(jnp.float32)) * (dh ** -0.5)
    scores = jnp.where(valid[None, :, None], scores, NEG_INF)
    m = jnp.max(scores, axis=-1, keepdims=True)
    p = jnp.exp(scores - m)
    l = jnp.sum(p, axis=-1)
    o = jnp.einsum("nbhqk,nbkhd->nbqhd", p, vb.astype(jnp.float32))
    o = o / jnp.moveaxis(l, 2, 3)[..., None]
    lse = jnp.moveaxis(m[..., 0] + jnp.log(l), 2, 3)

    def from_phase(t):
        rest = t.shape[4:]
        t = t.reshape(bsz, dilation, Lp, nh, *rest)[:, :, :L]
        return jnp.moveaxis(t, 1, 2).reshape(bsz, seq, nh, *rest)

    return from_phase(o), from_phase(lse)

def dilated_attention_mixer(h, w_in, q_gain, k_gain, w_out, positions):
    bsz, seq, _ = h.shape
    qkv = (h @ w_in).reshape(bsz, seq, A_N_GROUPS, 3, A_HEADS, A_HEAD_DIM)
    outs, lses = [], []
    for g, (window, dilation) in enumerate(A_GROUPS):
        q = rope(rms_norm(qkv[:, :, g, 0], q_gain[g]), positions)
        k = rope(rms_norm(qkv[:, :, g, 1], k_gain[g]), positions)
        v = qkv[:, :, g, 2]
        o, lse = dilated_window_attention(q, k, v, window, dilation)
        outs.append(o)
        lses.append(lse)
    alpha = jax.nn.softmax(jnp.stack(lses, axis=0), axis=0)
    out = jnp.sum(alpha[..., None] * jnp.stack(outs, axis=0), axis=0)
    return out.reshape(bsz, seq, A_WIDTH).astype(h.dtype) @ w_out

def gla_chunk(q, k, v, log_a, strict):
    bsz, nh, seq, dk = q.shape
    dv = v.shape[-1]
    nc = seq // B_CHUNK
    q = q.astype(jnp.float32).reshape(bsz, nh, nc, B_CHUNK, dk)
    k = k.astype(jnp.float32).reshape(bsz, nh, nc, B_CHUNK, dk)
    v = v.astype(jnp.float32).reshape(bsz, nh, nc, B_CHUNK, dv)
    b = jnp.cumsum(log_a.astype(jnp.float32).reshape(bsz, nh, nc, B_CHUNK, dk), axis=3)
    b_last = b[..., -1:, :]
    q_t = q * jnp.exp(b)
    k_t = k * jnp.exp(-b)
    k_end = k * jnp.exp(b_last - b)
    mask = jnp.tril(jnp.ones((B_CHUNK, B_CHUNK), dtype=bool), k=-1 if strict else 0)
    attn = jnp.where(mask, jnp.einsum("bhncd,bhnsd->bhncs", q_t, k_t), 0.0)
    o_intra = jnp.einsum("bhncs,bhnse->bhnce", attn, v)
    chunk_kv = jnp.einsum("bhncd,bhnce->bhnde", k_end, v)
    decay = jnp.exp(b_last[..., 0, :])

    def step(state, inp):
        kv_n, dec_n = inp
        return dec_n[..., None] * state + kv_n, state

    init = jnp.zeros((bsz, nh, dk, dv), jnp.float32)
    _, s_in = lax.scan(step, init, (jnp.moveaxis(chunk_kv, 2, 0), jnp.moveaxis(decay, 2, 0)))
    s_in = jnp.moveaxis(s_in, 0, 2)
    o_inter = jnp.einsum("bhncd,bhnde->bhnce", q_t, s_in)
    return (o_intra + o_inter).reshape(bsz, nh, seq, dv)

def _heads(t, nh):
    bsz, seq, _ = t.shape
    return t.reshape(bsz, seq, nh, -1).transpose(0, 2, 1, 3)

def gla_mixer(h, w_in, w_gate_f, bias_gate_f, w_gate_b, bias_gate_b, out_gain, w_out):
    bsz, seq, _ = h.shape
    proj = h @ w_in
    cuts = np.cumsum([B_QK_WIDTH, B_QK_WIDTH, B_V_WIDTH, B_V_WIDTH, B_GATE_RANK]).tolist()
    q, k, v, r, zf, zb = jnp.split(proj, cuts, axis=-1)
    q = _heads(q, B_HEADS) * (B_KEY_DIM ** -0.5)
    k = _heads(k, B_HEADS)
    v = _heads(v, B_HEADS)
    log_af = jax.nn.log_sigmoid((zf @ w_gate_f + bias_gate_f).astype(jnp.float32)) / B_GATE_TAU
    log_ab = jax.nn.log_sigmoid((zb @ w_gate_b + bias_gate_b).astype(jnp.float32)) / B_GATE_TAU
    log_af = _heads(log_af, B_HEADS)
    log_ab = _heads(log_ab, B_HEADS)
    o_f = gla_chunk(q, k, v, log_af, strict=False)
    flip = lambda t: jnp.flip(t, axis=2)
    o_b = flip(gla_chunk(flip(q), flip(k), flip(v), flip(log_ab), strict=True))
    o = (o_f + o_b).transpose(0, 2, 1, 3)
    o = rms_norm(o, out_gain).reshape(bsz, seq, B_V_WIDTH)
    o = o * jax.nn.silu(r.astype(jnp.float32))
    return o.astype(h.dtype) @ w_out

def swiglu(h, w_gate_up, w_down):
    g, u = jnp.split(h @ w_gate_up, 2, axis=-1)
    return (jax.nn.silu(g) * u) @ w_down

def second_inputs(seed: int = 0) -> dict:
    key = jax.random.key(seed)
    ks = jax.random.split(key, 16)

    def nrm(k, shape, scale):
        return jax.random.normal(k, shape, jnp.float32) * scale

    return {
        "x": nrm(ks[0], (BATCH, SEQ, D_MODEL), 1.0),
        "attn_norm": 1.0 + nrm(ks[1], (DEPTH_2, D_MODEL), 0.02),
        "ffn_norm": 1.0 + nrm(ks[2], (DEPTH_2, D_MODEL), 0.02),
        "a_w_in": nrm(ks[3], (N_A_LAYERS, D_MODEL, A_IN_WIDTH), D_MODEL ** -0.5),
        "a_q_norm": 1.0 + nrm(ks[4], (N_A_LAYERS, A_N_GROUPS, A_HEAD_DIM), 0.02),
        "a_k_norm": 1.0 + nrm(ks[5], (N_A_LAYERS, A_N_GROUPS, A_HEAD_DIM), 0.02),
        "a_w_out": nrm(ks[6], (N_A_LAYERS, A_WIDTH, D_MODEL), A_WIDTH ** -0.5),
        "b_w_in": nrm(ks[7], (N_B_LAYERS, D_MODEL, B_IN_WIDTH), D_MODEL ** -0.5),
        "b_w_gate_f": nrm(ks[8], (N_B_LAYERS, B_GATE_RANK, B_QK_WIDTH), B_GATE_RANK ** -0.5),
        "b_gate_bias_f": nrm(ks[9], (N_B_LAYERS, B_QK_WIDTH), 0.1),
        "b_w_gate_b": nrm(ks[10], (N_B_LAYERS, B_GATE_RANK, B_QK_WIDTH), B_GATE_RANK ** -0.5),
        "b_gate_bias_b": nrm(ks[11], (N_B_LAYERS, B_QK_WIDTH), 0.1),
        "b_out_norm": 1.0 + nrm(ks[12], (N_B_LAYERS, B_HEADS, B_VAL_DIM), 0.02),
        "b_w_out": nrm(ks[13], (N_B_LAYERS, B_V_WIDTH, D_MODEL), B_V_WIDTH ** -0.5),
        "ffn_w_gate_up": nrm(ks[14], (DEPTH_2, D_MODEL, 2 * FFN_HIDDEN), D_MODEL ** -0.5),
        "ffn_w_down": nrm(ks[15], (DEPTH_2, FFN_HIDDEN, D_MODEL), FFN_HIDDEN ** -0.5),
    }

def second_block(x, attn_norm, ffn_norm, a_w_in, a_q_norm, a_k_norm, a_w_out, b_w_in, b_w_gate_f, b_gate_bias_f, b_w_gate_b, b_gate_bias_b, b_out_norm, b_w_out, ffn_w_gate_up, ffn_w_down):
    positions = jnp.arange(x.shape[1])
    h = x
    for i in range(DEPTH_2):
        j = i // N_MIXERS
        hn = rms_norm(h, attn_norm[i])
        if i % N_MIXERS == 0:
            mix = dilated_attention_mixer(hn, a_w_in[j], a_q_norm[j], a_k_norm[j], a_w_out[j], positions)
        else:
            mix = gla_mixer(hn, b_w_in[j], b_w_gate_f[j], b_gate_bias_f[j], b_w_gate_b[j], b_gate_bias_b[j], b_out_norm[j], b_w_out[j])
        h = h + mix.astype(h.dtype)
        h = h + swiglu(rms_norm(h, ffn_norm[i]), ffn_w_gate_up[i], ffn_w_down[i]).astype(h.dtype)
    return h


def setup_inputs(seed=0):
    out = dict(first_inputs(seed))
    for name, value in second_inputs(seed + 1).items():
        if name != "x":
            out[name + "_2"] = value
    return out


def reference(
    x, c, ctx, c_ctx, w_ada, b_ada, g_pre_mix, g_post_mix, g_pre_ffn, g_post_ffn, w_in, lam_q1,
    lam_k1, lam_q2, lam_k2, g_attn_subln, conv_w, conv_b, dt_bias, a_log, d_skip, g_ssd_norm,
    w_branch_attn, w_branch_ssd, w_out, w_router, router_bias, w_e_gate, w_e_up, w_e_down,
    w_sh_gate, w_sh_up, w_sh_down, attn_norm_2, ffn_norm_2, a_w_in_2, a_q_norm_2, a_k_norm_2,
    a_w_out_2, b_w_in_2, b_w_gate_f_2, b_gate_bias_f_2, b_w_gate_b_2, b_gate_bias_b_2,
    b_out_norm_2, b_w_out_2, ffn_w_gate_up_2, ffn_w_down_2,
):
    x = first_block(
        x, c, ctx, c_ctx, w_ada, b_ada, g_pre_mix, g_post_mix, g_pre_ffn, g_post_ffn, w_in,
        lam_q1, lam_k1, lam_q2, lam_k2, g_attn_subln, conv_w, conv_b, dt_bias, a_log, d_skip,
        g_ssd_norm, w_branch_attn, w_branch_ssd, w_out, w_router, router_bias, w_e_gate, w_e_up,
        w_e_down, w_sh_gate, w_sh_up, w_sh_down,
    )
    return second_block(
        x, attn_norm_2, ffn_norm_2, a_w_in_2, a_q_norm_2, a_k_norm_2, a_w_out_2, b_w_in_2,
        b_w_gate_f_2, b_gate_bias_f_2, b_w_gate_b_2, b_gate_bias_b_2, b_out_norm_2, b_w_out_2,
        ffn_w_gate_up_2, ffn_w_down_2,
    )


_drawn_inputs = setup_inputs


def setup_inputs(seed=0):
    import zlib

    import numpy as np

    out = dict(_drawn_inputs(seed))
    spreads = {}
    factors = {'lam_k2': 2.834,
     'd_skip': 2.707,
     'attn_norm_2': 2.748,
     'ffn_norm_2': 2.686,
     'a_q_norm_2': 8.0,
     'a_k_norm_2': 8.0,
     'b_gate_bias_f_2': 4.282,
     'b_gate_bias_b_2': 3.745,
     'b_out_norm_2': 6.084}
    for name, (base, spread) in spreads.items():
        noise = np.random.default_rng([zlib.crc32(name.encode()), seed]).standard_normal(out[name].shape)
        drawn = base * np.exp(spread * noise) if base else spread * noise
        out[name] = jnp.asarray(drawn.astype(out[name].dtype))
    for name, factor in factors.items():
        out[name] = (out[name] * factor).astype(out[name].dtype)
    return out
```

```python
from contextlib import ExitStack

import concourse.bass as bass
from concourse import mybir
from concourse.alu_op_type import AluOpType as ALU

ACT = mybir.ActivationFunctionType
AX = mybir.AxisListType
F32 = mybir.dt.float32
BF16 = mybir.dt.bfloat16
I32 = mybir.dt.int32
U32 = mybir.dt.uint32

P = 128
D = 1024
KT = D // P
T = 512
TC = 256
TA = T + TC
TT = T // P
AT = TA // P
EPS = 1e-6
H1 = 8
SSD_H, SSD_G = 16, 4
E_N, E_F = 64, 256
MAXBLK = T * 8 // P + E_N
FF_T = 2816 // P
GH = 4
GC = 64
LAM_INIT = 0.8 - 0.6
NSLOT = 4
CHW = 2048

CH_ADA = 0
CH_QKV = CH_ADA + 6 * D // 256
CH_XBC = CH_QKV + 12
CH_Z = CH_XBC + 8
CH_MERGE = CH_Z + 4
CH_OUT = CH_MERGE + 16
CH_SH = CH_OUT + 4
CH_DIL = CH_SH + 3
CH_DILO = CH_DIL + 36
CH_FF0 = CH_DILO + 4
CH_GLA = CH_FF0 + 33
CH_GLAR = CH_GLA + 8
CH_GLAO = CH_GLAR + 4
CH_FF1 = CH_GLAO + 4
CH_END = CH_FF1 + 33

VEC = {}


def _cols():
    at = 0
    for name, n in [("cc", 16), ("b_ada", 48), ("g_pre_mix", 8), ("g_post_mix", 8), ("g_pre_ffn", 8),
                    ("g_post_ffn", 8), ("g_subln", 1), ("conv_w", 48), ("conv_b", 16), ("d_skip", 8),
                    ("g_ssd", 8), ("attn_norm", 16), ("ffn_norm", 16), ("a_q_norm", 3), ("a_k_norm", 3),
                    ("b_out_norm", 8), ("lam", 256), ("dt_bias", 32), ("a_log", 32), ("router_bias", 64)]:
        VEC[name] = (at, n)
        at += n
    return at


NVEC = _cols()
CONSTS = ["ident", "ones", "rot", "pair", "triu", "tril", "triu_strict", "gtriu", "gtril"]


BLOCK1_SEMS = (
    "da_bias", "da_diff", "da_exp", "da_head", "da_ln", "da_max", "da_norm", "da_recip", "da_rstd",
    "da_scores", "da_sq", "da_ss", "da_turn", "da_turned", "da_values", "dt_abs", "dt_diff", "dt_ln",
    "dt_raw", "dt_sums", "dta", "qk_cos", "qk_out", "qk_raw", "qk_rot", "qk_sin", "ssd_btok", "ssd_bturn",
    "ssd_cb", "ssd_cbmm", "ssd_ce", "ssd_decay", "ssd_decayed", "ssd_erow", "ssd_exp", "ssd_rows", "ssd_seg",
    "ssd_state", "ssd_statemm", "ssd_sub", "ssd_tridta", "ssd_xdt", "ssd_xturn", "ssd_xw", "ssd_y", "ssd_ymm",
    "xbc_mid", "xbc_silu", "xbc_taps", "z_gated", "z_ln",
)
BLOCK2_SEMS = (
    "dil_bias", "dil_cos", "dil_evac", "dil_exp", "dil_ln", "dil_max", "dil_o", "dil_out", "dil_prob",
    "dil_pv", "dil_qn", "dil_recip", "dil_rot", "dil_rstd", "dil_scores", "dil_sin", "dil_ss", "dil_turn",
    "dil_turned", "gla_attn", "gla_b", "gla_diff", "gla_eb", "gla_ekend", "gla_enb", "gla_k", "gla_kend",
    "gla_kturn", "gla_kturned", "gla_kv", "gla_last", "gla_masked", "gla_o", "gla_omm", "gla_q", "gla_state",
    "gla_zeroed", "lg_ln", "lg_out", "lg_rstd", "lg_silu", "lg_sq", "lg_sums", "lin_abs", "lin_evac",
    "lin_exp", "lin_gate", "lin_ln", "lin_raw", "lin_z", "lin_zt",
)


def two_blocks(nc, wstream, x_t, ctx_t, vecs, consts, rope_t, gmask_t, dmask_t, iota_t, w_dt, w_router,
               we_gu, we_down, w_z, w_gate_fb, xs, ys, out_t, dbg, stop):
    ctx = ExitStack()
    with ctx:
        def sb(name, shape, dt=F32):
            return ctx.enter_context(nc.sbuf_tensor(name, shape, dt))

        made = {}

        def sem(name):
            if name in BLOCK2_SEMS:
                name = BLOCK1_SEMS[BLOCK2_SEMS.index(name)]
            if name not in made:
                made[name] = ctx.enter_context(nc.semaphore(name))
            return made[name]

        ring = sb("ring", [P, NSLOT, CHW])
        arena = sb("arena", [P, 40960])
        vec = sb("vec", [P, NVEC])
        cst = sb("cst", [P, len(CONSTS), P])
        rope = sb("rope", [P, 2, T])
        gmask = sb("gmask", [P, 2, 64], U32)
        identb = sb("identb", [P, P], BF16)
        wdt = sb("wdt", [P, KT, 32])
        wrt = sb("wrt", [P, KT, E_N])
        mod = sb("mod", [P, 48, 2])
        cs = sb("cs", [P, KT, 2])
        gain = sb("gain", [P, 40])
        small = sb("small", [P, 64])
        epst = sb("epst", [P, 1])
        ps = ctx.enter_context(nc.psum_tensor("ps", [P, 8, 512], F32))
        pf = ps[:, :, :].rearrange("p b n -> p (b n)")

        def bank(b, n=512, off=0):
            return pf[:, b * 512 + off:b * 512 + off + n]

        def view(at, *dims):
            n = 1
            for d in dims:
                n *= d
            ap = arena[:, at:at + n]
            if len(dims) == 2:
                return ap.rearrange("p (a b) -> p a b", b=dims[1])
            if len(dims) == 3:
                return ap.rearrange("p (a b c) -> p a b c", b=dims[1], c=dims[2])
            return ap

        def split(ap, *dims):
            if len(dims) == 2:
                return ap.rearrange("p (a b) -> p a b", b=dims[1])
            return ap.rearrange("p (a b c) -> p a b c", b=dims[1], c=dims[2])

        def v(name, a=0, n=None):
            at, m = VEC[name]
            return vec[:, at + a:at + a + (m if n is None else n)]

        C = {name: cst[:, i, :] for i, name in enumerate(CONSTS)}
        XT = view(0, KT, T)
        HT = view(4096, KT, T)
        R = 8192

        A1, A2, G1, G2 = 0, 16, 24, 32

        phases = []

        class Link:

            def __init__(self, eng, name):
                self.eng, self.sem, self.n = eng, sem(name), 0

            def __call__(self, ins):
                ins.then_inc(self.sem, 1)
                self.n += 1
                self.eng.wait_ge(self.sem, self.n)

        def arrived(pe, c):
            pe.wait_ge(sem(f"slot{c % NSLOT}_full"), 16 * (c // NSLOT + 1))

        def wtile(c, k, j, n=P):
            return ring[:, c % NSLOT, k * 256 + j * P:k * 256 + j * P + n]

        def chunk_done(ins):
            ins.then_inc(sem("chunk_done"), 1)

        NLOAD = 9

        def ada_sync(sp):
            for dst, src in ((vec[:, :], vecs), (cst[:, :, :], consts), (XT, x_t), (view(R, KT, TC), ctx_t),
                             (rope[:, :, :], rope_t[0]), (gmask[:, :, :], gmask_t),
                             (identb[:, :], dmask_t[:, 2304:2432]), (wdt[:, :, :], w_dt),
                             (wrt[:, :, :], w_router)):
                sp.dma_start(dst, src).then_inc(sem("loaded"), 16)

        def ada_scalar(act):
            act.wait_ge(sem("loaded"), 16 * NLOAD)
            act.activation(cs[:, :, :], split(v("cc"), KT, 2), ACT.Silu).then_inc(sem("ada_silu"), 1)
            act.wait_ge(sem("lam_dots"), 1)
            act.activation(small[:, 2:4], small[:, 0:2], ACT.Exp).then_inc(sem("lam_exp"), 1)

        def ada_tensor(pe):
            pe.wait_ge(sem("ada_silu"), 1)
            for c in range(24):
                arrived(pe, CH_ADA + c)
                for j in range(2):
                    m = 2 * c + j
                    for k in range(KT):
                        mm = pe.matmul(bank(7, 2, 2 * m), wtile(CH_ADA + c, k, j), cs[:, k, :],
                                       start=(k == 0), stop=(k == KT - 1))
                chunk_done(mm)

        def ada_vector(dve):
            link = Link(dve, "ada_link")
            dve.memset(epst[:, :], EPS)
            dve.wait_ge(sem("loaded"), 16 * NLOAD)
            lam = split(v("lam"), 4, 64)
            prod = split(view(R + 2048, 128), 2, 64)
            link(dve.tensor_tensor(prod, lam[:, 0:4:2, :], lam[:, 1:4:2, :], ALU.mult))
            dve.tensor_reduce(small[:, 0:2], prod, AX.X, ALU.add).then_inc(sem("lam_dots"), 1)
            dve.wait_ge(sem("lam_exp"), 1)
            link(dve.tensor_tensor(small[:, 4:5], small[:, 3:4], small[:, 2:3], ALU.subtract))
            link(dve.tensor_scalar(small[:, 5:6], small[:, 4:5], -LAM_INIT, None, ALU.add))
            link(dve.tensor_scalar(small[:, 6:7], v("g_subln"), 1.0 - LAM_INIT, None, ALU.mult))
            dve.wait_ge(sem("chunk_done"), CH_ADA + 24)
            link(dve.tensor_tensor(mod[:, :, :], split(bank(7, 96), 48, 2),
                                   v("b_ada").unsqueeze(2).to_broadcast([P, 48, 2]), ALU.add))
            for s in range(2):
                dve.scalar_tensor_tensor(gain[:, A1 + 8 * s:A1 + 8 * s + 8], mod[:, 8:16, s], 1.0, v("g_pre_mix"),
                                         ALU.add, ALU.mult)
            dve.scalar_tensor_tensor(gain[:, A2:A2 + 8], mod[:, 32:40, 0], 1.0, v("g_pre_ffn"), ALU.add, ALU.mult)
            dve.tensor_tensor(gain[:, G1:G1 + 8], mod[:, 16:24, 0], v("g_post_mix"), ALU.mult)
            dve.tensor_tensor(gain[:, G2:G2 + 8], mod[:, 40:48, 0], v("g_post_ffn"), ALU.mult)

        phases.append(dict(scalar=ada_scalar, tensor=ada_tensor, vector=ada_vector))

        norms = [0]
        SQ = R + 32768 - 1024

        def norm(src, n, dst=None, scale=None, shift=None, residual=None):
            m = norms[0]
            norms[0] += 1
            sq = [view(SQ + 512 * i, 512)[:, 0:n] for i in range(2)]
            tmp = [view(SQ - 1024 + 512 * i, 512)[:, 0:n] for i in range(2)]
            ss, rs = bank(6, n), bank(7, n)

            def scalar(act):
                for k in range(KT):
                    if k >= 2:
                        act.wait_ge(sem("norm_summed"), 8 * m + k - 1)
                    act.activation(sq[k % 2], src[:, k, :], ACT.Square).then_inc(sem("norm_sq"), 1)
                act.wait_ge(sem("norm_summed"), 8 * m + 8)
                act.activation(rs, ss, ACT.Ln, scale=1.0 / D, bias=epst[:, :]).then_inc(sem("norm_ln"), 1)
                act.wait_ge(sem("norm_ln"), m + 1)
                act.activation(rs, rs, ACT.Exp, scale=-0.5).then_inc(sem("norm_rstd"), 1)
                if dst is not None:
                    for k in range(KT):
                        act.wait_ge(sem("norm_scaled"), 8 * m + k + 1)
                        if shift is None:
                            act.activation(dst[:, k, :], tmp[k % 2], ACT.Copy).then_inc(sem("norm_out"), 1)
                        else:
                            act.activation(dst[:, k, :], tmp[k % 2], ACT.Identity, scale=scale(k),
                                           bias=shift(k)).then_inc(sem("norm_out"), 1)
                else:
                    for k in range(KT):
                        act.sem_inc(sem("norm_out"), 1)

            def tensor(pe):
                for k in range(KT):
                    pe.wait_ge(sem("norm_sq"), 8 * m + k + 1)
                    pe.matmul(ss, C["ones"], sq[k % 2], start=(k == 0),
                              stop=(k == KT - 1)).then_inc(sem("norm_summed"), 1)

            def vector(dve):
                dve.wait_ge(sem("norm_rstd"), m + 1)
                for k in range(KT):
                    if dst is not None:
                        if k >= 2:
                            dve.wait_ge(sem("norm_out"), 8 * m + k - 1)
                        if shift is None:
                            dve.scalar_tensor_tensor(tmp[k % 2], src[:, k, :], scale(k), rs, ALU.mult,
                                                     ALU.mult).then_inc(sem("norm_scaled"), 1)
                        else:
                            dve.tensor_tensor(tmp[k % 2], src[:, k, :], rs, ALU.mult).then_inc(sem("norm_scaled"), 1)
                    else:
                        dve.scalar_tensor_tensor(tmp[k % 2], src[:, k, :], scale(k), rs, ALU.mult,
                                                 ALU.mult).then_inc(sem("norm_scaled"), 1)
                        dve.wait_ge(sem("norm_scaled"), 8 * m + k + 1)
                        dve.tensor_tensor(residual[:, k, :], residual[:, k, :], tmp[k % 2], ALU.add)

            phases.append(dict(scalar=scalar, tensor=tensor, vector=vector))

        HC = view(R, KT, TC)
        norm(XT, T, HT, lambda k: gain[:, A1 + k:A1 + k + 1], lambda k: mod[:, k, 0:1])
        norm(HC, TC, HC, lambda k: gain[:, A1 + 8 + k:A1 + 9 + k], lambda k: mod[:, k, 1:2])

        O1 = view(R + 2048, H1, T)
        Q = view(R + 6144, H1, T)
        K = view(R + 10240, H1, TA)
        V = view(R + 16384, AT, D)
        W0 = R + 22528

        def acc(n):
            return pf[:, (n % 2) * 1536:(n % 2) * 1536 + 1536]

        def qkv_tensor(pe):
            def rotate(ch):
                pe.wait_ge(sem("qk_raw"), ch + 1)
                if ch >= 1:
                    pe.wait_ge(sem("qk_out"), ch)
                for j in range(2):
                    mm = pe.matmul(bank(6 + j), C["rot"], view(W0 + (ch % 2) * 1024 + j * 512, 512),
                                   start=True, stop=True)
                mm.then_inc(sem("qk_rot"), 1)

            for ch in range(12):
                c = CH_QKV + ch
                a = acc(ch)
                arrived(pe, c)
                if ch >= 2:
                    pe.wait_ge(sem("qk_raw"), ch - 1)
                if ch < 8:
                    for j in range(2):
                        for k in range(KT):
                            mm = pe.matmul(a[:, j * 512:j * 512 + 512], wtile(c, k, j), HT[:, k, :],
                                           start=(k == 0), stop=(k == KT - 1))
                        if ch >= 4:
                            for k in range(KT):
                                mm = pe.matmul(a[:, 1024 + j * 256:1280 + j * 256], wtile(c, k, j), HC[:, k, :],
                                               start=(k == 0), stop=(k == KT - 1))
                else:
                    for t in range(AT):
                        for k in range(KT):
                            lhs = HC[:, k, t * P:t * P + P] if t < 2 else HT[:, k, (t - 2) * P:(t - 1) * P]
                            mm = pe.matmul(a[:, t * 256:t * 256 + 256], lhs, wtile(c, k, 0, 256),
                                           start=(k == 0), stop=(k == KT - 1))
                chunk_done(mm)
                if 1 <= ch < 9:
                    rotate(ch - 1)

        def qkv_scalar(act):
            for ch in range(12):
                a = acc(ch)
                act.wait_ge(sem("chunk_done"), CH_QKV + ch + 1)
                if ch < 8:
                    if ch >= 2:
                        act.wait_ge(sem("qk_rot"), ch - 1)
                        act.wait_ge(sem("qk_cos"), ch - 1)
                    if ch >= 4:
                        act.activation(K[:, 2 * (ch - 4):2 * (ch - 4) + 2, 0:TC], split(a[:, 1024:1536], 2, 256),
                                       ACT.Copy)
                    act.activation(view(W0 + (ch % 2) * 1024, 1024), a[:, 0:1024], ACT.Copy).then_inc(sem("qk_raw"), 1)
                else:
                    act.activation(V[:, :, (ch - 8) * 256:(ch - 7) * 256], split(a, AT, 256),
                                   ACT.Copy).then_inc(sem("qk_raw"), 1)

        def qkv_gpsimd(pool):
            cos = rope[:, 0:1, :].to_broadcast([P, 2, T])
            for ch in range(8):
                pool.wait_ge(sem("qk_raw"), ch + 1)
                if ch >= 2:
                    pool.wait_ge(sem("qk_out"), ch - 1)
                pool.tensor_tensor(view(W0 + 2048 + (ch % 2) * 1024, 2, 512), view(W0 + (ch % 2) * 1024, 2, 512),
                                   cos, ALU.mult).then_inc(sem("qk_cos"), 1)

        def qkv_vector(dve):
            sin = rope[:, 1:2, :].to_broadcast([P, 2, T])
            rot = split(pf[:, 3072:4096], 2, 512)
            for ch in range(8):
                dve.wait_ge(sem("qk_rot"), ch + 1)
                dve.tensor_tensor(rot, rot, sin, ALU.mult).then_inc(sem("qk_sin"), 1)
                dve.wait_ge(sem("qk_cos"), ch + 1)
                dve.wait_ge(sem("qk_sin"), ch + 1)
                dst = Q[:, 2 * ch:2 * ch + 2, :] if ch < 4 else K[:, 2 * (ch - 4):2 * (ch - 4) + 2, TC:TA]
                dve.tensor_tensor(dst, rot, view(W0 + 2048 + (ch % 2) * 1024, 2, 512),
                                  ALU.add).then_inc(sem("qk_out"), 1)

        phases.append(dict(tensor=qkv_tensor, scalar=qkv_scalar, gpsimd=qkv_gpsimd, vector=qkv_vector))

        NU = H1 * TT

        def prob(n, c):
            return view(W0 + ((n % 2) * 2 + c) * TA, TA)

        def wT(h):
            return view(W0 + 4 * TA + (h % 2) * AT * T, AT, T)

        SC = small[:, 8:40]

        def da_tensor(pe):
            def scores(n):
                h, qt = divmod(n, TT)
                for c in range(2):
                    if n >= 1:
                        pe.wait_ge(sem("da_exp"), 2 * (n - 1) + c + 1)
                    q = Q[64 * c:64 * c + 64, h, qt * P:qt * P + P]
                    pe.matmul(bank(2 * c), q, K[64 * c:64 * c + 64, h, 0:512], start=True, stop=True)
                    pe.matmul(bank(2 * c + 1, 256), q, K[64 * c:64 * c + 64, h, 512:TA], start=True,
                              stop=True).then_inc(sem("da_scores"), 1)

            def turn(n):
                pe.wait_ge(sem("da_diff"), n + 1)
                if n >= 1:
                    pe.wait_ge(sem("da_turned"), n)
                for t in range(AT):
                    mm = pe.transpose(bank(4, P, t * P), prob(n, 0)[:, t * P:t * P + P], C["ident"])
                mm.then_inc(sem("da_turn"), 1)

            def values(h):
                pe.wait_ge(sem("da_turned"), 4 * h + 4)
                if h >= 1:
                    pe.wait_ge(sem("da_head"), h)
                for t in range(AT):
                    mm = pe.matmul(bank(6), V[:, t, h * P:h * P + P], wT(h)[:, t, :], start=(t == 0),
                                   stop=(t == AT - 1))
                mm.then_inc(sem("da_values"), 1)

            def square_sum(h):
                pe.wait_ge(sem("da_sq"), h + 1)
                pe.matmul(bank(7), C["ones"], view(SQ, 512), start=True, stop=True).then_inc(sem("da_ss"), 1)

            scores(0)
            for n in range(NU):
                if n + 1 < NU:
                    scores(n + 1)
                turn(n)
                if n % 4 == 0 and n:
                    values(n // 4 - 1)
                if n % 4 == 1 and n > 4:
                    square_sum(n // 4 - 1)
            values(H1 - 1)
            square_sum(H1 - 1)

        def da_vector(dve):
            def row_max(n):
                s = SC[:, 16 * (n % 2):16 * (n % 2) + 16]
                for c in range(2):
                    dve.wait_ge(sem("da_scores"), 2 * n + c + 1)
                    dve.reduce_max(s[:, c:c + 1], pf[:, 1024 * c:1024 * c + TA], AX.X).then_inc(sem("da_max"), 1)
                    dve.wait_ge(sem("da_max"), 2 * n + c + 1)
                    dve.tensor_scalar(s[:, 2 + c:3 + c], s[:, c:c + 1], -0.125, None,
                                      ALU.mult).then_inc(sem("da_bias"), 1)

            def diff(n):
                s = SC[:, 16 * (n % 2):16 * (n % 2) + 16]
                dve.wait_ge(sem("da_exp"), 2 * n + 2)
                dve.reciprocal(s[:, 6:8], s[:, 4:6]).then_inc(sem("da_recip"), 1)
                dve.wait_ge(sem("da_recip"), n + 1)
                dve.tensor_tensor(s[:, 8:9], s[:, 7:8], small[:, 5:6], ALU.mult)
                dve.tensor_scalar(prob(n, 0), prob(n, 0), s[:, 6:7], None, ALU.mult).then_inc(sem("da_norm"), 1)
                dve.wait_ge(sem("da_norm"), n + 1)
                dve.scalar_tensor_tensor(prob(n, 0), prob(n, 1), s[:, 8:9], prob(n, 0), ALU.mult,
                                         ALU.add).then_inc(sem("da_diff"), 1)

            def head(h):
                dve.wait_ge(sem("da_rstd"), h + 1)
                dve.scalar_tensor_tensor(O1[:, h, :], bank(6), small[:, 6:7], view(SQ + 512, 512), ALU.mult,
                                         ALU.mult).then_inc(sem("da_head"), 1)

            for n in range(NU + 1):
                if n < NU:
                    row_max(n)
                if n >= 1:
                    diff(n - 1)
                if n % 4 == 3 and n > 4:
                    head(n // 4 - 1)
            head(H1 - 1)

        def da_scalar(act):
            def turned(n):
                h, qt = divmod(n, TT)
                act.wait_ge(sem("da_turn"), n + 1)
                if h >= 2 and qt == 0:
                    act.wait_ge(sem("da_values"), h - 1)
                act.activation(wT(h)[:, :, qt * P:qt * P + P], split(bank(4, TA), AT, P),
                               ACT.Copy).then_inc(sem("da_turned"), 1)

            def head(h):
                act.wait_ge(sem("da_values"), h + 1)
                act.activation(view(SQ, 512), bank(6), ACT.Square).then_inc(sem("da_sq"), 1)

            def rstd(h):
                act.wait_ge(sem("da_ss"), h + 1)
                if h >= 1:
                    act.wait_ge(sem("da_head"), h)
                act.activation(view(SQ + 512, 512), bank(7), ACT.Ln, scale=1.0 / P,
                               bias=epst[:, :]).then_inc(sem("da_ln"), 1)
                act.wait_ge(sem("da_ln"), h + 1)
                act.activation(view(SQ + 512, 512), view(SQ + 512, 512), ACT.Exp, scale=-0.5).then_inc(sem("da_rstd"), 1)

            for n in range(NU):
                s = SC[:, 16 * (n % 2):16 * (n % 2) + 16]
                for c in range(2):
                    act.wait_ge(sem("da_bias"), 2 * n + c + 1)
                    if n >= 2:
                        act.wait_ge(sem("da_turn"), n - 1)
                    act.activation(prob(n, c), pf[:, 1024 * c:1024 * c + TA], ACT.Exp, scale=0.125,
                                   bias=s[:, 2 + c:3 + c], accum_out=s[:, 4 + c:5 + c]).then_inc(sem("da_exp"), 1)
                if n >= 1:
                    turned(n - 1)
                if n % 4 == 1 and n > 4:
                    head(n // 4 - 1)
                if n % 4 == 2 and n > 4:
                    rstd(n // 4 - 1)
            turned(NU - 1)
            head(H1 - 1)
            rstd(H1 - 1)

        NFILL = 8

        def fill_gpsimd(pool):
            src = rope[:, :, :].rearrange("p a b -> p (a b)").unsqueeze(1).to_broadcast([P, NFILL, D])
            for buf in (xs, ys):
                for i in range(MAXBLK // NFILL):
                    pool.dma_start(buf[i * NFILL * P:(i + 1) * NFILL * P, :].rearrange("(b p) d -> p b d", p=P),
                                   src).then_inc(sem("filled"), 16)

        phases.append(dict(tensor=da_tensor, scalar=da_scalar, vector=da_vector, gpsimd=fill_gpsimd))

        XBC = view(R + 6144, 16, TA)
        Y = view(R + 18432, KT, T)
        SEGS = ((0, TC, 1024), (TC, T, 0))

        def xbc_tensor(pe):
            for t in range(AT):
                for k in range(KT):
                    lhs = HC[:, k, t * P:t * P + P] if t < 2 else HT[:, k, (t - 2) * P:(t - 1) * P]
                    mm = pe.matmul(bank(6, 32, t * 32), lhs, wdt[:, k, :], start=(k == 0), stop=(k == KT - 1))
            mm.then_inc(sem("dt_raw"), 1)
            for ch in range(8):
                c = CH_XBC + ch
                a = acc(ch)
                arrived(pe, c)
                if ch >= 2:
                    pe.wait_ge(sem("xbc_taps"), ch - 1)
                for j in range(2):
                    for k in range(KT):
                        pe.matmul(a[:, j * 512:j * 512 + 512], wtile(c, k, j), HT[:, k, :],
                                  start=(k == 0), stop=(k == KT - 1))
                    for k in range(KT):
                        mm = pe.matmul(a[:, 1024 + j * 256:1280 + j * 256], wtile(c, k, j), HC[:, k, :],
                                       start=(k == 0), stop=(k == KT - 1))
                chunk_done(mm)

        def part(a, j, base, n, lo, hi):
            at = base + j * n
            return a[:, at + lo:at + hi]

        def xbc_scalar(act):
            def silu(ch):
                act.wait_ge(sem("xbc_taps"), ch + 1)
                act.activation(XBC[:, 2 * ch:2 * ch + 2, :], XBC[:, 2 * ch:2 * ch + 2, :],
                               ACT.Silu).then_inc(sem("xbc_silu"), 1)

            for ch in range(8):
                act.wait_ge(sem("chunk_done"), CH_XBC + ch + 1)
                for j in range(2):
                    m = 2 * ch + j
                    for first, n, base in SEGS:
                        ins = act.activation(XBC[:, m, first:first + n], part(acc(ch), j, base, n, 0, n), ACT.Identity,
                                             scale=v("conv_w", 16 + m, 1), bias=v("conv_b", m, 1))
                ins.then_inc(sem("xbc_mid"), 1)
                if ch:
                    silu(ch - 1)
            silu(7)

        def xbc_vector(dve):
            link = Link(dve, "xbc_link")
            for ch in range(8):
                dve.wait_ge(sem("xbc_mid"), ch + 1)
                for lo, tap in ((0, 0), (1, 32)):
                    for j in range(2):
                        m = 2 * ch + j
                        for first, n, base in SEGS:
                            o = XBC[:, m, first + 1 - lo:first + n - lo]
                            ins = dve.scalar_tensor_tensor(o, part(acc(ch), j, base, n, lo, n - 1 + lo),
                                                           v("conv_w", tap + m, 1), o, ALU.mult, ALU.add)
                    if lo == 0:
                        link(ins)
                    else:
                        ins.then_inc(sem("xbc_taps"), 1)

        S0 = R + 22528 + 7168
        DT = view(S0, 2, AT, SSD_H)
        DTA = view(S0 + 192, 2, AT, SSD_H)
        ACOL = view(S0 + 384, 2, AT, SSD_H)
        TOEND = view(S0 + 576, 2, AT, SSD_H)
        DECAY = view(S0 + 768, 2, AT, SSD_H)

        def flat(ap):
            return ap.rearrange("p a b c -> p (a b c)")

        def dt_vector(dve):
            link = Link(dve, "dt_link")
            tmp = view(S0 + 384, AT, 32)
            dve.wait_ge(sem("dt_raw"), 1)
            link(dve.tensor_tensor(tmp, split(bank(6, 192), AT, 32),
                                   v("dt_bias").unsqueeze(1).to_broadcast([P, AT, 32]), ALU.add))
            dve.scalar_tensor_tensor(view(S0 + 576, AT, 32), tmp, -1.0, tmp, ALU.mult, ALU.min).then_inc(sem("dt_abs"), 1)
            dve.wait_ge(sem("dt_ln"), 1)
            for d in range(2):
                ins = dve.scalar_tensor_tensor(DT[:, d], tmp[:, :, 16 * d:16 * d + 16], 0.0,
                                               view(S0 + 576, AT, 32)[:, :, 16 * d:16 * d + 16], ALU.max, ALU.add)
            link(ins)
            for d in range(2):
                ins = dve.scalar_tensor_tensor(
                    DTA[:, d], DT[:, d], -1.0,
                    v("a_log", 16 * d, 16).unsqueeze(1).to_broadcast([P, AT, 16]), ALU.mult, ALU.mult)
            ins.then_inc(sem("dta"), 1)
            dve.wait_ge(sem("dt_sums"), 1)
            link(dve.tensor_copy(flat(ACOL), bank(6, 192)))
            dve.tensor_tensor(flat(TOEND), bank(7, 192), flat(ACOL), ALU.subtract).then_inc(sem("dt_diff"), 1)
            dve.wait_ge(sem("xbc_silu"), 4)
            for j in range(KT):
                dve.tensor_scalar(Y[:, j, :], XBC[:, j, TC:TA], v("d_skip", j, 1), None, ALU.mult)

        def dt_scalar(act):
            link = Link(act, "dt_act_link")
            link(act.activation(v("a_log"), v("a_log"), ACT.Exp))
            act.wait_ge(sem("dt_abs"), 1)
            link(act.activation(flat(TOEND), flat(TOEND), ACT.Exp))
            act.activation(flat(TOEND), flat(TOEND), ACT.Ln, bias=1.0).then_inc(sem("dt_ln"), 1)
            act.wait_ge(sem("dt_diff"), 1)
            act.activation(flat(TOEND), flat(TOEND), ACT.Exp)
            act.activation(flat(DECAY), bank(7, 192), ACT.Exp)

        def dt_tensor(pe):
            pe.wait_ge(sem("dta"), 1)
            pe.matmul(bank(6, 96), C["triu"], DTA[:, 0].rearrange("p a b -> p (a b)"), start=True, stop=True)
            pe.matmul(bank(6, 96, 96), C["tril"], DTA[:, 1].rearrange("p a b -> p (a b)"), start=True, stop=True)
            pe.matmul(bank(7, 192), C["ones"], flat(DTA), start=True, stop=True).then_inc(sem("dt_sums"), 1)

        def xbc_all_tensor(pe):
            xbc_tensor(pe)
            dt_tensor(pe)

        def xbc_all_scalar(act):
            xbc_scalar(act)
            dt_scalar(act)

        def xbc_all_vector(dve):
            xbc_vector(dve)
            dt_vector(dve)

        phases.append(dict(tensor=xbc_all_tensor, scalar=xbc_all_scalar, vector=xbc_all_vector))

        STEPS = [(0, 0), (1, 1), (0, 1), (1, 0), (0, 2), (1, 5), (0, 3), (1, 4), (0, 4), (1, 3), (0, 5), (1, 2)]
        NCTX = 4
        W1 = R + 22528
        DM = view(W1, SSD_H, P)
        EC = view(W1 + 2048, SSD_H, P)
        XDT = view(W1 + 4096, 1024)
        XW = view(W1 + 5120, 1024)
        BTOK = view(W1 + 6144, 512)
        CBM = view(W1 + 6656, SSD_G, P)
        STATE = [view(R + 1024 * d, 1024) for d in range(2)]
        TRI = (C["triu"], C["tril"])

        def hcol(ap):
            return ap.unsqueeze(2).to_broadcast([P, SSD_H, 64])

        def ssd_tensor(pe):
            for n, (d, t) in enumerate(STEPS):
                tok = slice(t * P, t * P + P)
                if n >= 1:
                    pe.wait_ge(sem("ssd_state"), n)
                    pe.wait_ge(sem("ssd_btok"), n)
                for j in range(KT):
                    mm = pe.transpose(bank(0, P, j * P), XBC[:, j, tok], C["ident"])
                mm.then_inc(sem("ssd_xturn"), 1)
                for g in range(SSD_G):
                    mm = pe.transpose(bank(2, P, g * P), XBC[:, 8 + g, tok], C["ident"])
                mm.then_inc(sem("ssd_bturn"), 1)
                if n >= NCTX:
                    m = n - NCTX
                    if m >= 1:
                        pe.wait_ge(sem("ssd_y"), m)
                        pe.wait_ge(sem("ssd_cb"), m)
                    for g in range(SSD_G):
                        mm = pe.matmul(bank(3, P, g * P), XBC[:, 8 + g, tok], XBC[:, 12 + g, tok],
                                       start=True, stop=True)
                    mm.then_inc(sem("ssd_cbmm"), 1)
                    pe.wait_ge(sem("ssd_tridta"), m + 1)
                    for q in range(4):
                        mm = pe.matmul(bank(4 + q), C["ones"], DM[:, 4 * q:4 * q + 4, :], start=True, stop=True)
                    mm.then_inc(sem("ssd_rows"), 1)
                    pe.wait_ge(sem("ssd_decay"), m + 1)
                    pe.wait_ge(sem("ssd_ce"), m + 1)
                    for h in range(SSD_H):
                        o = pf[64 * (h % 2):64 * (h % 2) + 64, 2048 + (h // 2) * P:2048 + (h // 2) * P + P]
                        pe.matmul(o, XDT[:, 64 * h:64 * h + 64], DM[:, h, :], start=True, stop=False)
                        mm = pe.matmul(o, STATE[d][:, 64 * h:64 * h + 64], EC[:, h, :], start=False, stop=True)
                    mm.then_inc(sem("ssd_ymm"), 1)
                pe.wait_ge(sem("ssd_xw"), n + 1)
                pe.wait_ge(sem("ssd_btok"), n + 1)
                for g in range(SSD_G):
                    mm = pe.matmul(bank(g // 2, 256, (g % 2) * 256), BTOK[:, g * P:g * P + P],
                                   XW[:, g * 256:g * 256 + 256], start=True, stop=True)
                mm.then_inc(sem("ssd_statemm"), 1)

        def ssd_vector(dve):
            for n, (d, t) in enumerate(STEPS):
                dve.wait_ge(sem("ssd_xturn"), n + 1)
                if n >= 1:
                    dve.wait_ge(sem("ssd_xw"), n)
                dve.tensor_tensor(split(XDT, SSD_H, 64), split(pf[:, 0:1024], SSD_H, 64), hcol(DT[:, d, t, :]),
                                  ALU.mult).then_inc(sem("ssd_xdt"), 1)
                if n >= NCTX:
                    m = n - NCTX
                    dve.wait_ge(sem("ssd_cbmm"), m + 1)
                    dve.tensor_tensor(CBM, split(bank(3), SSD_G, P), TRI[d].unsqueeze(1).to_broadcast([P, SSD_G, P]),
                                      ALU.mult).then_inc(sem("ssd_cb"), 1)
                    dve.wait_ge(sem("ssd_rows"), m + 1)
                    dve.wait_ge(sem("ssd_erow"), m + 1)
                    dve.tensor_tensor(DM, split(pf[:, 2048:4096], SSD_H, P),
                                      ACOL[:, d, t, :].unsqueeze(2).to_broadcast([P, SSD_H, P]),
                                      ALU.subtract).then_inc(sem("ssd_sub"), 1)
                    dve.wait_ge(sem("ssd_sub"), m + 1)
                    dve.tensor_scalar(DM, DM, 0.0, None, ALU.min).then_inc(sem("ssd_seg"), 1)
                    dve.wait_ge(sem("ssd_exp"), m + 1)
                    dve.wait_ge(sem("ssd_cb"), m + 1)
                    dve.tensor_tensor(DM.rearrange("p (g r) i -> p g r i", r=4),
                                      pf[:, 2048:4096].rearrange("p (g r i) -> p g r i", r=4, i=P),
                                      CBM.unsqueeze(2).to_broadcast([P, SSD_G, 4, P]),
                                      ALU.mult).then_inc(sem("ssd_decay"), 1)
                    dve.wait_ge(sem("ssd_ymm"), m + 1)
                    y = Y[:, :, (t - 2) * P:(t - 1) * P]
                    dve.tensor_tensor(y, y, split(pf[:, 2048:3072], KT, P), ALU.add).then_inc(sem("ssd_y"), 1)
                dve.wait_ge(sem("ssd_statemm"), n + 1)
                if n < 2:
                    dve.tensor_copy(STATE[d], pf[:, 0:1024]).then_inc(sem("ssd_state"), 1)
                else:
                    s = split(STATE[d], SSD_H, 64)
                    dve.tensor_tensor(s, s, hcol(DECAY[:, d, t, :]), ALU.mult).then_inc(sem("ssd_decayed"), 1)
                    dve.wait_ge(sem("ssd_decayed"), n - 1)
                    dve.tensor_tensor(STATE[d], STATE[d], pf[:, 0:1024], ALU.add).then_inc(sem("ssd_state"), 1)

        def ssd_scalar(act):
            for n, (d, t) in enumerate(STEPS):
                act.wait_ge(sem("ssd_bturn"), n + 1)
                if n >= 1:
                    act.wait_ge(sem("ssd_statemm"), n)
                act.activation(BTOK, bank(2), ACT.Copy).then_inc(sem("ssd_btok"), 1)
                if n >= NCTX:
                    m = n - NCTX
                    act.wait_ge(sem("ssd_rows"), m + 1)
                    if m >= 1:
                        act.wait_ge(sem("ssd_ymm"), m)
                    act.activation(EC.rearrange("p h i -> p (h i)"), pf[:, 2048:4096],
                                   ACT.Exp).then_inc(sem("ssd_erow"), 1)
                    act.wait_ge(sem("ssd_seg"), m + 1)
                    act.activation(pf[:, 2048:4096], DM.rearrange("p h i -> p (h i)"),
                                   ACT.Exp).then_inc(sem("ssd_exp"), 1)

        def ssd_gpsimd(pool):
            for n, (d, t) in enumerate(STEPS):
                if n >= NCTX:
                    m = n - NCTX
                    if m >= 1:
                        pool.wait_ge(sem("ssd_ymm"), m)
                    pool.tensor_tensor(DM, TRI[d].unsqueeze(1).to_broadcast([P, SSD_H, P]),
                                       DTA[:, d, t, :].unsqueeze(2).to_broadcast([P, SSD_H, P]),
                                       ALU.mult).then_inc(sem("ssd_tridta"), 1)
                    pool.wait_ge(sem("ssd_erow"), m + 1)
                    ec = EC.rearrange("p (g r) i -> p g r i", r=4)
                    pool.tensor_tensor(ec, ec, XBC[:, 12:16, t * P:t * P + P].unsqueeze(2).to_broadcast([P, 4, 4, P]),
                                       ALU.mult).then_inc(sem("ssd_ce"), 1)
                pool.wait_ge(sem("ssd_xdt"), n + 1)
                if n >= 1:
                    pool.wait_ge(sem("ssd_statemm"), n)
                pool.tensor_tensor(split(XW, SSD_H, 64), split(XDT, SSD_H, 64), hcol(TOEND[:, d, t, :]),
                                   ALU.mult).then_inc(sem("ssd_xw"), 1)

        phases.append(dict(tensor=ssd_tensor, vector=ssd_vector, scalar=ssd_scalar, gpsimd=ssd_gpsimd))

        ZS = [view(R + 6144 + 1024 * i, 2, T) for i in range(2)]
        ZQ = [view(R + 8192 + 1024 * i, 2, T) for i in range(2)]
        ZR = [view(R + 10240 + 512 * i, T) for i in range(2)]

        def z_tensor(pe):
            def sums(g):
                pe.wait_ge(sem("z_sq"), g + 1)
                if g >= 1:
                    pe.wait_ge(sem("z_ln"), g)
                for j in range(2):
                    mm = pe.matmul(bank(6), C["ones"], ZQ[g % 2][:, j, :], start=(j == 0), stop=(j == 1))
                mm.then_inc(sem("z_sums"), 1)

            for g in range(4):
                c = CH_Z + g
                arrived(pe, c)
                if g >= 2:
                    pe.wait_ge(sem("z_silu"), g - 1)
                for j in range(2):
                    for k in range(KT):
                        mm = pe.matmul(acc(g)[:, j * 512:j * 512 + 512], wtile(c, k, j), HT[:, k, :],
                                       start=(k == 0), stop=(k == KT - 1))
                chunk_done(mm)
                if g:
                    sums(g - 1)
            sums(3)

        def z_scalar(act):
            def rstd(g):
                act.wait_ge(sem("z_gated"), g + 1)
                act.activation(ZQ[g % 2], Y[:, 2 * g:2 * g + 2, :], ACT.Square).then_inc(sem("z_sq"), 1)
                act.wait_ge(sem("z_sums"), g + 1)
                if g >= 2:
                    act.wait_ge(sem("z_out"), g - 1)
                act.activation(ZR[g % 2], bank(6), ACT.Ln, scale=1.0 / 256, bias=epst[:, :]).then_inc(sem("z_ln"), 1)
                act.wait_ge(sem("z_ln"), g + 1)
                act.activation(ZR[g % 2], ZR[g % 2], ACT.Exp, scale=-0.5).then_inc(sem("z_rstd"), 1)

            for g in range(4):
                act.wait_ge(sem("chunk_done"), CH_Z + g + 1)
                if g >= 2:
                    act.wait_ge(sem("z_gated"), g - 1)
                act.activation(ZS[g % 2], split(acc(g)[:, 0:1024], 2, T), ACT.Silu).then_inc(sem("z_silu"), 1)
                if g:
                    rstd(g - 1)
            rstd(3)

        def z_vector(dve):
            for g in range(4):
                y = Y[:, 2 * g:2 * g + 2, :]
                dve.wait_ge(sem("z_silu"), g + 1)
                dve.tensor_tensor(y, y, ZS[g % 2], ALU.mult).then_inc(sem("z_gated"), 1)
                dve.wait_ge(sem("z_rstd"), g + 1)
                for j in range(2):
                    ins = dve.scalar_tensor_tensor(y[:, j, :], y[:, j, :], v("g_ssd", 2 * g + j, 1), ZR[g % 2],
                                                   ALU.mult, ALU.mult)
                ins.then_inc(sem("z_out"), 1)

        def fill_end_gpsimd(pool):
            pool.wait_ge(sem("filled"), 16 * 2 * (MAXBLK // NFILL))

        phases.append(dict(tensor=z_tensor, scalar=z_scalar, vector=z_vector))

        MERGED = view(R + 6144, KT, T)
        MG = [view(R + 10240 + 1024 * i, 1024) for i in range(2)]
        MT = view(R + 12288, 1024)
        MIX = view(R + 13312, KT, T)

        def merge_tensor(pe):
            for n in range(16):
                c = CH_MERGE + n
                src = (HT, O1, HT, Y)[n % 4]
                arrived(pe, c)
                if n >= 2 and n % 2 == 0:
                    pe.wait_ge(sem("merge_gate"), n // 2)
                if n >= 2 and n % 2 == 1:
                    pe.wait_ge(sem("merge_prod"), n // 2)
                for j in range(2):
                    for k in range(KT):
                        mm = pe.matmul(acc(n)[:, j * 512:j * 512 + 512], wtile(c, k, j), src[:, k, :],
                                       start=(k == 0), stop=(k == KT - 1))
                chunk_done(mm)
            for n in range(4):
                c = CH_OUT + n
                arrived(pe, c)
                if n == 0:
                    pe.wait_ge(sem("merge_sum"), 4)
                if n < 2:
                    pe.wait_ge(sem("merge_gate"), 8)
                    pe.wait_ge(sem("merge_prod"), 8)
                else:
                    pe.wait_ge(sem("mix_out"), n - 1)
                for j in range(2):
                    for k in range(KT):
                        mm = pe.matmul(acc(n)[:, j * 512:j * 512 + 512], wtile(c, k, j), MERGED[:, k, :],
                                       start=(k == 0), stop=(k == KT - 1))
                chunk_done(mm)

        def merge_scalar(act):
            for q in range(8):
                act.wait_ge(sem("chunk_done"), CH_MERGE + 2 * q + 1)
                if q >= 2:
                    act.wait_ge(sem("merge_prod"), q - 1)
                act.activation(MG[q % 2], acc(0)[:, 0:1024], ACT.Sigmoid).then_inc(sem("merge_gate"), 1)
            for n in range(4):
                act.wait_ge(sem("chunk_done"), CH_OUT + n + 1)
                act.activation(MIX[:, 2 * n:2 * n + 2, :], split(acc(n)[:, 0:1024], 2, T),
                               ACT.Copy).then_inc(sem("mix_out"), 1)

        def merge_vector(dve):
            for q in range(8):
                m = MERGED[:, 2 * (q // 2):2 * (q // 2) + 2, :].rearrange("p a b -> p (a b)")
                dve.wait_ge(sem("chunk_done"), CH_MERGE + 2 * q + 2)
                dve.wait_ge(sem("merge_gate"), q + 1)
                dst = m if q % 2 == 0 else MT
                dve.tensor_tensor(dst, acc(1)[:, 0:1024], MG[q % 2], ALU.mult).then_inc(sem("merge_prod"), 1)
                if q % 2 == 1:
                    dve.wait_ge(sem("merge_prod"), q + 1)
                    dve.tensor_tensor(m, m, MT, ALU.add).then_inc(sem("merge_sum"), 1)

        phases.append(dict(tensor=merge_tensor, scalar=merge_scalar, vector=merge_vector, gpsimd=fill_end_gpsimd))

        norm(MIX, T, None, lambda k: gain[:, G1 + k:G1 + k + 1], residual=XT)
        norm(XT, T, HT, lambda k: gain[:, A2 + k:A2 + k + 1], lambda k: mod[:, 24 + k, 0:1])

        H2TOK = view(R, TT, D)
        SHID = view(R + 4096, 2, T)
        WGU = [view(R + 5120 + 4096 * s, KT, 512) for s in range(2)]
        WD = [view(R + 13312 + 2048 * s, 2, D) for s in range(2)]
        XB = [view(R + 17408 + 1024 * s, D) for s in range(2)]
        XBT = [view(R + 19456 + 1024 * s, KT, P) for s in range(2)]
        YO = [view(R + 21504 + 1024 * s, D) for s in range(2)]
        HID = [view(R + 23552 + 256 * s, 256) for s in range(2)]
        HIDT = [view(R + 24064 + 256 * s, 2, P) for s in range(2)]
        SIL = [view(R + 24576 + 256 * s, 256) for s in range(2)]
        M0 = R + 25088
        SCO, SEL, MSK, REP, KEY = (view(M0 + 256 * i, TT, E_N) for i in range(5))
        WTS = view(M0 + 1280, TT, E_N)
        GS8 = view(M0 + 1536, TT, 8, 8)
        GSC = view(M0 + 1792, TT, 8)
        GMK = view(M0 + 1824, TT, 8)
        WSUM = view(M0 + 1856, TT)
        NB = view(M0 + 1860, E_N)
        INCL = view(M0 + 1924, E_N)
        START = view(M0 + 1988, E_N)
        DST8 = view(M0 + 2052, TT, 8)
        W8 = view(M0 + 2084, TT, 8)
        DSTI = view(M0 + 2116, 32).bitcast(U32)
        LOWER = view(M0 + 2148, 64)
        IOTA = view(M0 + 2212, MAXBLK)
        BEF = view(M0 + 2308, MAXBLK)
        BEI = view(M0 + 2404, MAXBLK).bitcast(I32)
        NPF = view(M0 + 2500, 1)
        NPI = view(M0 + 2501, 1).bitcast(I32)
        EVEN = view(M0 + 2502, MAXBLK // 2)
        CMP = view(R + 17408, MAXBLK, E_N)
        PICK = view(R + 17408, 32, E_N)
        CMPG = view(M0 + 2560, TT, 8, 8)
        CMPE = view(M0 + 2816, TT, 8, 8)

        def rt_sync_gpsimd(pool):
            pool.dma_start(view(M0 + 2148, 64 + MAXBLK), iota_t).then_inc(sem("iota_loaded"), 16)
            pool.wait_ge(sem("rt_dest"), 1)
            pool.wait_ge(sem("h2_tok"), 8)
            for t in range(TT):
                for k in range(8):
                    pool.indirect_dma_start(xs, bass.IndirectOffsetOnAxis(ap=DSTI[:, 8 * t + k:8 * t + k + 1], axis=0),
                                            H2TOK[:, t, :], None).then_inc(sem("scattered"), 16)
            pool.wait_ge(sem("scattered"), 16 * 32)

        def rt_tensor(pe):
            for t in range(TT):
                for k in range(KT):
                    mm = pe.matmul(bank(6, E_N, t * E_N), HT[:, k, t * P:t * P + P], wrt[:, k, :],
                                   start=(k == 0), stop=(k == KT - 1))
            mm.then_inc(sem("rt_logits"), 1)
            for c in range(2):
                arrived(pe, CH_SH + c)
                for j in range(2):
                    for k in range(KT):
                        mm = pe.matmul(acc(c)[:, j * 512:j * 512 + 512], wtile(CH_SH + c, k, j), HT[:, k, :],
                                       start=(k == 0), stop=(k == KT - 1))
                chunk_done(mm)
            for q in range(8):
                if q >= 2:
                    pe.wait_ge(sem("h2_tok"), q - 1)
                for i in range(4):
                    mm = pe.transpose(bank(2 + 3 * (q % 2), P, i * P), HT[:, 4 * (q % 2) + i, (q // 2) * P:(q // 2) * P + P],
                                      C["ident"])
                mm.then_inc(sem("h2_turn"), 1)
            pe.wait_ge(sem("rt_mask"), 1)
            for t in range(TT):
                for u in range(t + 1):
                    pe.matmul(bank(7, E_N, t * E_N), C["triu_strict"] if u == t else C["ones"], MSK[:, u, :],
                              start=(u == 0), stop=(u == t))
            for u in range(TT):
                mm = pe.matmul(bank(6, E_N, 256), C["ones"], MSK[:, u, :], start=(u == 0), stop=(u == TT - 1))
            mm.then_inc(sem("rt_pos"), 1)

        def rt_scalar(act):
            act.wait_ge(sem("rt_logits"), 1)
            act.activation(SCO.rearrange("p a b -> p (a b)"), bank(6, 256), ACT.Sigmoid).then_inc(sem("rt_scores"), 1)
            act.wait_ge(sem("chunk_done"), CH_SH + 1)
            act.activation(SHID, split(acc(0)[:, 0:1024], 2, T), ACT.Silu).then_inc(sem("sh_silu"), 1)
            for q in range(8):
                act.wait_ge(sem("h2_turn"), q + 1)
                act.activation(H2TOK[:, q // 2, 512 * (q % 2):512 * (q % 2) + 512], bank(2 + 3 * (q % 2)),
                               ACT.Copy).then_inc(sem("h2_tok"), 1)

        def rt_vector(dve):
            link = Link(dve, "rt_link")

            def spread(ap, n):
                return ap.unsqueeze(3).to_broadcast([P, TT, 8, n])

            def groups(ap):
                return ap.rearrange("p t (g e) -> p t g e", e=8)

            dve.wait_ge(sem("rt_scores"), 1)
            link(dve.tensor_tensor(SEL, SCO, v("router_bias").unsqueeze(1).to_broadcast([P, TT, E_N]), ALU.add))
            for t in range(TT):
                for g in range(8):
                    ins = dve.max(GS8[:, t, g, :], SEL[:, t, 8 * g:8 * g + 8])
            link(ins)
            link(dve.tensor_tensor(GSC, GS8[:, :, :, 0], GS8[:, :, :, 1], ALU.add))
            other = GSC.unsqueeze(2).to_broadcast([P, TT, 8, 8])
            this = spread(GSC, 8)
            dve.wait_ge(sem("iota_loaded"), 16)
            dve.tensor_tensor(CMPG, other, this, ALU.is_gt)
            link(dve.tensor_tensor(CMPE, other, this, ALU.is_equal))
            lower = LOWER.rearrange("p (a b) -> p a b", b=8).unsqueeze(1).to_broadcast([P, TT, 8, 8])
            link(dve.tensor_tensor(CMPE, CMPE, lower, ALU.mult))
            link(dve.tensor_tensor(CMPG, CMPG, CMPE, ALU.add))
            link(dve.tensor_reduce(GMK, CMPG, AX.X, ALU.add))
            link(dve.tensor_scalar(GMK, GMK, 3.5, None, ALU.is_lt))
            link(dve.tensor_tensor(groups(SEL), groups(SEL), spread(GMK, 8), ALU.mult))
            link(dve.tensor_scalar(GMK, GMK, -1.0, 1e30, ALU.add, ALU.mult))
            link(dve.tensor_tensor(groups(SEL), groups(SEL), spread(GMK, 8), ALU.add))
            for t in range(TT):
                ins = dve.max(DST8[:, t, :], SEL[:, t, :])
            link(ins)
            for t in range(TT):
                ins = dve.match_replace(out=REP[:, t, :], in_to_replace=DST8[:, t, :], in_values=SEL[:, t, :],
                                        imm_value=-3e38)
            link(ins)
            dve.tensor_tensor(MSK, REP, SEL, ALU.not_equal).then_inc(sem("rt_mask"), 1)
            dve.wait_ge(sem("rt_mask"), 1)
            link(dve.tensor_tensor(WTS, SCO, MSK, ALU.mult))
            link(dve.tensor_reduce(WSUM, WTS, AX.X, ALU.add))
            link(dve.reciprocal(WSUM, WSUM))
            link(dve.tensor_scalar(WSUM, WSUM, 2.5, None, ALU.mult))
            link(dve.tensor_tensor(WTS, WTS, WSUM.unsqueeze(2).to_broadcast([P, TT, E_N]), ALU.mult))
            dve.wait_ge(sem("rt_pos"), 1)
            cnt = bank(6, E_N, 256)
            link(dve.tensor_scalar(NB, cnt, 0.0, None, ALU.is_gt))
            for i in range(1, T // P):
                link(dve.scalar_tensor_tensor(NB, cnt, 128.0 * i, NB, ALU.is_gt, ALU.add))
            link(dve.tensor_tensor_scan(INCL, C["ones"][:, 0:E_N], NB, 0.0, ALU.mult, ALU.add))
            link(dve.tensor_tensor(START, INCL, NB, ALU.subtract))
            link(dve.tensor_scalar(START, START, 128.0, 1.0, ALU.mult, ALU.add))
            link(dve.tensor_tensor(KEY, split(bank(7, 256), TT, E_N), START.unsqueeze(1).to_broadcast([P, TT, E_N]),
                                   ALU.add))
            link(dve.tensor_tensor(KEY, KEY, MSK, ALU.mult))
            for t in range(TT):
                ins = dve.max(DST8[:, t, :], KEY[:, t, :])
            link(ins)
            dve.tensor_scalar(DSTI, DST8.rearrange("p a b -> p (a b)"), -1.0, None,
                              ALU.add).then_inc(sem("rt_dest"), 1)
            cmp_in = INCL[0:1, :].unsqueeze(1).to_broadcast([1, MAXBLK, E_N])
            link(dve.tensor_tensor(CMP[0:1], cmp_in, IOTA[0:1, :].unsqueeze(2).to_broadcast([1, MAXBLK, E_N]), ALU.is_le))
            link(dve.tensor_reduce(BEF[0:1, :], CMP[0:1], AX.X, ALU.add))
            dve.tensor_scalar(BEI[0:1, :], BEF[0:1, :], float(E_N - 1), None, ALU.min).then_inc(sem("rt_blocks"), 1)
            link(dve.tensor_scalar(EVEN[0:1, :], IOTA[0:1, 0:MAXBLK:2], INCL[0:1, E_N - 1:E_N], None, ALU.is_lt))
            link(dve.tensor_reduce(NPF[0:1, :], EVEN[0:1, :], AX.X, ALU.add))
            dve.tensor_copy(NPI[0:1, :], NPF[0:1, :]).then_inc(sem("rt_blocks"), 1)
            for t in range(TT):
                for k in range(8):
                    dve.scalar_tensor_tensor(PICK[:, 8 * t + k, :], KEY[:, t, :], DST8[:, t, k:k + 1], WTS[:, t, :],
                                             ALU.is_equal, ALU.mult, accum_out=W8[:, t, k:k + 1])
            dve.wait_ge(sem("sh_silu"), 1)
            dve.wait_ge(sem("chunk_done"), CH_SH + 2)
            dve.tensor_tensor(SHID, SHID, split(acc(1)[:, 0:1024], 2, T), ALU.mult)

        phases.append(dict(tensor=rt_tensor, scalar=rt_scalar, vector=rt_vector, gpsimd=rt_sync_gpsimd))
        MOE_STAGE = len(phases)

        def pairs(eng):
            return eng.value_load(NPI[0:1, 0:1], min_val=T * 8 // P // 2, max_val=MAXBLK // 2)

        def moe_sync(sp):
            sp.wait_ge(sem("rt_blocks"), 2)
            sp.wait_ge(sem("stage_ended"), 4 * MOE_STAGE)
            n = pairs(sp)

            def load(i):
                for s in range(2):
                    e = sp.value_load(BEI[0:1, bass.ds(i * 2 + s, 1)], min_val=0, max_val=E_N - 1)
                    sp.wait_ge(sem("moe_x_used"), i * 2 + (s + 1))
                    sp.dma_start(XB[s], xs[bass.ds(i * 256 + s * P, P), :]).then_inc(sem(f"moe_x{s}"), 16)
                    sp.wait_ge(sem("moe_gu_used"), i * 2 + (s + 1))
                    sp.dma_start(WGU[s].rearrange("p a b -> p (a b)"),
                                 we_gu[bass.ds(e, 1)].rearrange("o p n -> (o p) n")).then_inc(sem(f"moe_wgu{s}"), 16)
                    sp.wait_ge(sem("moe_d_used"), i * 2 + (s + 1))
                    sp.dma_start(WD[s].rearrange("p a b -> p (a b)"),
                                 we_down[bass.ds(e, 1)].rearrange("o p n -> (o p) n")).then_inc(sem(f"moe_wd{s}"), 16)

            def store(i):
                for s in range(2):
                    sp.wait_ge(sem(f"moe_y{s}"), i + 2)
                    sp.dma_start(ys[bass.ds(i * 256 + s * P, P), :], YO[s]).then_inc(sem(f"moe_out{s}"), 16)

            load(0)
            with sp.Fori(1, n) as i:
                load(i)
                store(i - 1)
            store(n - 1)
            for s in range(2):
                sp.wait_ge(sem(f"moe_out{s}"), n * 16 + 16)
                sp.dma_start(BEF[0:1, s:s + 1], IOTA[0:1, s:s + 1]).then_inc(sem("moe_rows_out"), 16)

        def moe_tensor(pe):
            for name in ("moe_x_used", "moe_gu_used", "moe_d_used"):
                pe.sem_inc(sem(name), 2)
            with pe.Fori(0, pairs(pe)) as i:
                for s in range(2):
                    pe.wait_ge(sem(f"moe_x{s}"), i * 16 + 16)
                    pe.wait_ge(sem(f"moe_y{s}"), i + 1)
                    for k in range(KT):
                        mm = pe.transpose(bank(2 * s, P, k * P), XB[s][:, k * P:k * P + P], C["ident"])
                    mm.then_inc(sem("moe_x_used"), 1)
                for s in range(2):
                    pe.wait_ge(sem(f"moe_xt{s}"), i + 1)
                    pe.wait_ge(sem(f"moe_wgu{s}"), i * 16 + 16)
                    for k in range(KT):
                        mm = pe.matmul(bank(4 + s), XBT[s][:, k, :], WGU[s][:, k, :], start=(k == 0), stop=(k == KT - 1))
                    mm.then_inc(sem("moe_gu_used"), 1)
                for s in range(2):
                    pe.wait_ge(sem(f"moe_hid{s}"), i + 1)
                    for k in range(2):
                        mm = pe.transpose(bank(6 + s, P, k * P), HID[s][:, k * P:k * P + P], C["ident"])
                    mm.then_inc(sem("moe_hturn"), 1)
                for s in range(2):
                    pe.wait_ge(sem(f"moe_hidt{s}"), i + 1)
                    pe.wait_ge(sem(f"moe_wd{s}"), i * 16 + 16)
                    for j in range(2):
                        for k in range(2):
                            mm = pe.matmul(bank(2 * s + j), HIDT[s][:, k, :], WD[s][:, k, j * 512:j * 512 + 512],
                                           start=(k == 0), stop=(k == 1))
                    mm.then_inc(sem("moe_d_used"), 1)

        def moe_scalar(act):
            act.sem_inc(sem("moe_y0"), 1)
            act.sem_inc(sem("moe_out0"), 16)
            with act.Fori(0, pairs(act)) as i:
                act.wait_ge(sem("moe_x_used"), i * 2 + 3)
                act.activation(XBT[0].rearrange("p a b -> p (a b)"), pf[:, 0:1024], ACT.Copy).then_inc(sem("moe_xt0"), 1)
                for s in range(2):
                    act.wait_ge(sem("moe_gu_used"), i * 2 + (s + 3))
                    act.activation(SIL[s], bank(4 + s, 256), ACT.Silu).then_inc(sem(f"moe_silu{s}"), 1)
                act.wait_ge(sem("moe_hturn"), i * 2 + 1)
                act.activation(HIDT[0].rearrange("p a b -> p (a b)"), bank(6, 256), ACT.Copy).then_inc(sem("moe_hidt0"), 1)
                act.wait_ge(sem("moe_d_used"), i * 2 + 3)
                act.wait_ge(sem("moe_out0"), i * 16 + 16)
                act.activation(YO[0], pf[:, 0:1024], ACT.Copy).then_inc(sem("moe_y0"), 1)

        def moe_vector(dve):
            dve.sem_inc(sem("moe_y1"), 1)
            dve.sem_inc(sem("moe_out1"), 16)
            with dve.Fori(0, pairs(dve)) as i:
                dve.wait_ge(sem("moe_x_used"), i * 2 + 4)
                dve.tensor_copy(XBT[1].rearrange("p a b -> p (a b)"), pf[:, 1024:2048]).then_inc(sem("moe_xt1"), 1)
                for s in range(2):
                    dve.wait_ge(sem(f"moe_silu{s}"), i + 1)
                    dve.tensor_tensor(HID[s], SIL[s], bank(4 + s, 256, 256), ALU.mult).then_inc(sem(f"moe_hid{s}"), 1)
                dve.wait_ge(sem("moe_hturn"), i * 2 + 2)
                dve.tensor_copy(HIDT[1].rearrange("p a b -> p (a b)"), bank(7, 256)).then_inc(sem("moe_hidt1"), 1)
                dve.wait_ge(sem("moe_d_used"), i * 2 + 4)
                dve.wait_ge(sem("moe_out1"), i * 16 + 16)
                dve.tensor_copy(YO[1], pf[:, 1024:2048]).then_inc(sem("moe_y1"), 1)

        def moe_gpsimd(pool):
            pool.wait_ge(sem("moe_rows_out"), 32)

        phases.append(dict(tensor=moe_tensor, scalar=moe_scalar, vector=moe_vector, gpsimd=moe_gpsimd))

        GB = [view(R + 5120 + 1024 * i, D) for i in range(8)]
        F = view(R + 13312, KT, T)

        def gather_gpsimd(pool):
            for n in range(32):
                if n >= 8:
                    pool.wait_ge(sem("g_used"), n - 7)
                pool.indirect_dma_start(GB[n % 8], None, ys, bass.IndirectOffsetOnAxis(ap=DSTI[:, n:n + 1], axis=0)
                                        ).then_inc(sem(f"gathered{n % 8}"), 16)

        def gather_vector(dve):
            for n in range(32):
                t, k = divmod(n, 8)
                dve.wait_ge(sem(f"gathered{n % 8}"), 16 * (n // 8 + 1))
                if k == 0:
                    dve.tensor_scalar(H2TOK[:, t, :], GB[n % 8], W8[:, t, 0:1], None, ALU.mult).then_inc(sem("g_used"), 1)
                else:
                    dve.wait_ge(sem("g_used"), n)
                    dve.scalar_tensor_tensor(H2TOK[:, t, :], GB[n % 8], W8[:, t, k:k + 1], H2TOK[:, t, :], ALU.mult,
                                             ALU.add).then_inc(sem("g_used"), 1)

        def gather_tensor(pe):
            c = CH_SH + 2
            arrived(pe, c)
            for j in range(KT):
                for k in range(2):
                    pe.matmul(bank(j), ring[:, c % NSLOT, k * D + j * P:k * D + j * P + P], SHID[:, k, :],
                              start=(k == 0), stop=(k == 1))
            pe.wait_ge(sem("g_used"), 32)
            for j in range(KT):
                for t in range(TT):
                    mm = pe.matmul(bank(j, P, t * P), H2TOK[:, t, j * P:j * P + P], C["ident"], start=False,
                                   stop=(t == TT - 1), skip_group_check=True)
                if j == KT - 1:
                    chunk_done(mm)

        def gather_scalar(act):
            act.wait_ge(sem("chunk_done"), CH_SH + 3)
            for j in range(KT):
                act.activation(F[:, j, :], bank(j), ACT.Copy)

        phases.append(dict(tensor=gather_tensor, scalar=gather_scalar, vector=gather_vector, gpsimd=gather_gpsimd))
        norm(F, T, None, lambda k: gain[:, G2 + k:G2 + k + 1], residual=XT)

        BLOCK1_STAGES = len(phases)

        OD = view(R, KT, T)

        def dq(g):
            return view(R + 4096 + 3072 * g, 2, T)

        def dk(g):
            return view(R + 5120 + 3072 * g, 2, T)

        def dv(g):
            return view(R + 6144 + 3072 * g, TT, 256)

        DRAW, DQN, DCO, DSQ, DRS = ([view(R + 13312 + 2048 * b + 1024 * i, 1024) for i in range(2)] for b in range(5))
        DPB = [view(R + 23552 + TA * i, TA) for i in range(2)]
        DPT = [view(R + 25088 + TA * i, AT, P) for i in range(2)]
        dmask = view(R + 26624, 1152).bitcast(BF16)

        def dil_load_gpsimd(pool):
            pool.dma_start(rope[:, :, :], rope_t[1]).then_inc(sem("dil_loaded"), 16)
            pool.dma_start(dmask, dmask_t[:, 0:2304]).then_inc(sem("dil_loaded"), 16)
            pool.dma_start(wdt[:, :, :], w_z).then_inc(sem("dil_loaded"), 16)
            pool.wait_ge(sem("dil_loaded"), 48)

        norm(XT, T, HT, lambda k: v("attn_norm", k, 1))
        phases[-1]["gpsimd"] = dil_load_gpsimd

        def acc2(n):
            return pf[:, (n % 2) * 1024:(n % 2) * 1024 + 1024]

        def dil_items(hq):
            return {3 * g + s: 6 * hq + 2 * g + s for g in range(3) for s in range(2)}

        def dil_units(hq):
            return range(16 * hq, 16 * hq + 16)

        def dil_unit(u):
            return u // 16, (u // 4) % 4, u % 4

        def dil_tensor(pe):
            def project(hq, p):
                m = 9 * hq + p
                c = CH_DIL + m
                g, s = divmod(p, 3)
                arrived(pe, c)
                if m >= 2:
                    pe.wait_ge(sem("dil_evac"), m - 1)
                if s < 2:
                    for j in range(2):
                        for k in range(KT):
                            mm = pe.matmul(acc2(m)[:, j * 512:j * 512 + 512], wtile(c, k, j), HT[:, k, :],
                                           start=(k == 0), stop=(k == KT - 1))
                else:
                    for t in range(TT):
                        for k in range(KT):
                            lhs = HT[:, k, t * P:t * P + P] if g == 0 else HT[:, k, t:T:4]
                            mm = pe.matmul(acc2(m)[:, t * 256:t * 256 + 256], lhs, wtile(c, k, 0, 256),
                                           start=(k == 0), stop=(k == KT - 1))
                chunk_done(mm)

            def pair_sums(m, n):
                pe.wait_ge(sem("dil_evac"), m + 1)
                if n >= 1:
                    pe.wait_ge(sem("dil_ln"), n)
                for j in range(2):
                    mm = pe.matmul(bank(4 + j), C["pair"], DSQ[n % 2][:, 512 * j:512 * j + 512], start=True, stop=True)
                mm.then_inc(sem("dil_ss"), 1)

            def rotate(n):
                pe.wait_ge(sem("dil_qn"), n + 1)
                if n >= 1:
                    pe.wait_ge(sem("dil_out"), n)
                for j in range(2):
                    mm = pe.matmul(bank(6 + j), C["rot"], DQN[n % 2][:, 512 * j:512 * j + 512], start=True, stop=True)
                mm.then_inc(sem("dil_rot"), 1)

            def scores(u):
                _, hl, r = dil_unit(u)
                rows, j, b = slice(64 * (hl % 2), 64 * (hl % 2) + 64), hl // 2, 2 * (u % 2)
                if u >= 2:
                    pe.wait_ge(sem("dil_exp"), u - 1)
                pe.matmul(bank(b), identb[:, :], dmask[:, 512 * r:512 * r + 512], start=True, stop=False)
                pe.matmul(bank(b), dq(0)[rows, j, r:T:4], dk(0)[rows, j, :], start=False, stop=True)
                for g in (1, 2):
                    o = bank(b + 1, P, P * (g - 1))
                    pe.matmul(o, identb[:, :], dmask[:, 1920 + P * g:2048 + P * g], start=True, stop=False)
                    mm = pe.matmul(o, dq(g)[rows, j, r:T:4], dk(g)[rows, j, r:T:4], start=False, stop=True)
                mm.then_inc(sem("dil_scores"), 1)

            def turn(u):
                pe.wait_ge(sem("dil_prob"), u + 1)
                if u >= 1:
                    pe.wait_ge(sem("dil_turned"), u)
                for t in range(AT):
                    mm = pe.transpose(bank(4, P, t * P), DPB[u % 2][:, t * P:t * P + P], C["ident"])
                mm.then_inc(sem("dil_turn"), 1)

            def values(u):
                hq, hl, r = dil_unit(u)
                pe.wait_ge(sem("dil_turned"), u + 1)
                if u % 8 == 0 and u >= 16:
                    pe.wait_ge(sem("dil_o"), u // 8 - 1)
                o = pf[64 * (hl % 2):64 * (hl % 2) + 64, (6 + hl // 2) * 512 + r * P:(6 + hl // 2) * 512 + r * P + P]
                for t in range(AT):
                    val = dv(0)[:, t, 64 * hl:64 * hl + 64] if t < TT else dv(t - TT + 1)[:, r, 64 * hl:64 * hl + 64]
                    mm = pe.matmul(o, val, DPT[u % 2][:, t, :], start=(t == 0), stop=(t == AT - 1))
                mm.then_inc(sem("dil_pv"), 1)

            for hq in range(4):
                items = dil_items(hq)
                for p in range(11):
                    if p < 9:
                        project(hq, p)
                    if p - 1 in items:
                        pair_sums(9 * hq + p - 1, items[p - 1])
                    if p - 2 in items:
                        rotate(items[p - 2])
                pe.wait_ge(sem("dil_out"), 6 * hq + 6)
                pe.wait_ge(sem("dil_evac"), 9 * hq + 9)
                units = dil_units(hq)
                scores(units[0])
                for u in units:
                    if u + 1 in units:
                        scores(u + 1)
                    turn(u)
                    if u - 1 in units:
                        values(u - 1)
                values(units[-1])

        def dil_scalar(act):
            def rstd(n):
                act.wait_ge(sem("dil_ss"), n + 1)
                if n >= 2:
                    act.wait_ge(sem("dil_qn"), n - 1)
                act.activation(DRS[n % 2], pf[:, 2048:3072], ACT.Ln, scale=1.0 / 64,
                               bias=epst[:, :]).then_inc(sem("dil_ln"), 1)
                act.wait_ge(sem("dil_ln"), n + 1)
                act.activation(DRS[n % 2], DRS[n % 2], ACT.Exp, scale=-0.5).then_inc(sem("dil_rstd"), 1)

            def turned(u):
                act.wait_ge(sem("dil_turn"), u + 1)
                if u >= 2:
                    act.wait_ge(sem("dil_pv"), u - 1)
                act.activation(DPT[u % 2].rearrange("p a b -> p (a b)"), bank(4, TA),
                               ACT.Copy).then_inc(sem("dil_turned"), 1)

            for hq in range(4):
                items = dil_items(hq)
                for p in range(10):
                    if p < 9:
                        m = 9 * hq + p
                        act.wait_ge(sem("chunk_done"), CH_DIL + m + 1)
                        if p in items:
                            n = items[p]
                            if n >= 2:
                                act.wait_ge(sem("dil_qn"), n - 1)
                                act.wait_ge(sem("dil_ss"), n - 1)
                            act.activation(DRAW[n % 2], acc2(m), ACT.Copy)
                            act.activation(DSQ[n % 2], acc2(m), ACT.Square).then_inc(sem("dil_evac"), 1)
                        else:
                            act.activation(dv(p // 3).rearrange("p a b -> p (a b)"), acc2(m),
                                           ACT.Copy).then_inc(sem("dil_evac"), 1)
                    if p - 1 in items:
                        rstd(items[p - 1])
                units = dil_units(hq)
                for u in units:
                    s = SC[:, 4 * (u % 2):4 * (u % 2) + 4]
                    act.wait_ge(sem("dil_bias"), u + 1)
                    if u >= 2:
                        act.wait_ge(sem("dil_turn"), u - 1)
                    act.activation(DPB[u % 2], pf[:, 1024 * (u % 2):1024 * (u % 2) + TA], ACT.Exp, scale=0.125,
                                   bias=s[:, 1:2], accum_out=s[:, 2:3]).then_inc(sem("dil_exp"), 1)
                    if u - 1 in units:
                        turned(u - 1)
                turned(units[-1])

        def dil_gpsimd(pool):
            cos = rope[:, 0:1, :].to_broadcast([P, 2, T])
            for n in range(24):
                pool.wait_ge(sem("dil_qn"), n + 1)
                if n >= 2:
                    pool.wait_ge(sem("dil_out"), n - 1)
                pool.tensor_tensor(split(DCO[n % 2], 2, T), split(DQN[n % 2], 2, T), cos,
                                   ALU.mult).then_inc(sem("dil_cos"), 1)

        def dil_vector(dve):
            sin = rope[:, 1:2, :].to_broadcast([P, 2, T])
            rot = split(pf[:, 3072:4096], 2, T)

            def normed(n, m):
                name = ("a_q_norm", "a_k_norm")[n % 2]
                dve.wait_ge(sem("dil_rstd"), n + 1)
                if n >= 2:
                    dve.wait_ge(sem("dil_rot"), n - 1)
                    dve.wait_ge(sem("dil_cos"), n - 1)
                dve.scalar_tensor_tensor(DQN[n % 2], DRAW[n % 2], v(name, (n % 6) // 2, 1), DRS[n % 2], ALU.mult,
                                         ALU.mult).then_inc(sem("dil_qn"), 1)

            def rotated(n):
                dst = (dq, dk)[n % 2]((n % 6) // 2)
                dve.wait_ge(sem("dil_rot"), n + 1)
                dve.tensor_tensor(rot, rot, sin, ALU.mult).then_inc(sem("dil_sin"), 1)
                dve.wait_ge(sem("dil_sin"), n + 1)
                dve.wait_ge(sem("dil_cos"), n + 1)
                dve.tensor_tensor(dst, rot, split(DCO[n % 2], 2, T), ALU.add).then_inc(sem("dil_out"), 1)

            def row_max(u):
                s = SC[:, 4 * (u % 2):4 * (u % 2) + 4]
                dve.wait_ge(sem("dil_scores"), u + 1)
                dve.reduce_max(s[:, 0:1], pf[:, 1024 * (u % 2):1024 * (u % 2) + TA], AX.X).then_inc(sem("dil_max"), 1)
                dve.wait_ge(sem("dil_max"), u + 1)
                dve.tensor_scalar(s[:, 1:2], s[:, 0:1], -0.125, None, ALU.mult).then_inc(sem("dil_bias"), 1)

            def probs(u):
                s = SC[:, 4 * (u % 2):4 * (u % 2) + 4]
                dve.wait_ge(sem("dil_exp"), u + 1)
                dve.reciprocal(s[:, 3:4], s[:, 2:3]).then_inc(sem("dil_recip"), 1)
                dve.wait_ge(sem("dil_recip"), u + 1)
                dve.tensor_scalar(DPB[u % 2], DPB[u % 2], s[:, 3:4], None, ALU.mult).then_inc(sem("dil_prob"), 1)

            def output(q):
                dve.wait_ge(sem("dil_pv"), 8 * q + 8)
                dve.tensor_copy(OD[:, q, :].rearrange("p (u r) -> p r u", r=4),
                                split(bank(6 + q % 2), 4, P)).then_inc(sem("dil_o"), 1)

            for hq in range(4):
                ns = range(6 * hq, 6 * hq + 6)
                for n in ns:
                    normed(n, 0)
                    if n - 1 in ns:
                        rotated(n - 1)
                rotated(ns[-1])
                units = dil_units(hq)
                row_max(units[0])
                for u in units:
                    if u + 1 in units:
                        row_max(u + 1)
                    probs(u)
                    if u % 8 == 2 and u - 8 in units:
                        output(u // 8 - 1)
                output(2 * hq + 1)

        phases.append(dict(tensor=dil_tensor, scalar=dil_scalar, vector=dil_vector, gpsimd=dil_gpsimd))

        def project_out(name, base, src):
            def tensor(pe):
                for n in range(4):
                    arrived(pe, base + n)
                    if n >= 2:
                        pe.wait_ge(sem(name), n - 1)
                    for j in range(2):
                        for k in range(KT):
                            mm = pe.matmul(acc(n)[:, j * 512:j * 512 + 512], wtile(base + n, k, j), src[:, k, :],
                                           start=(k == 0), stop=(k == KT - 1))
                    chunk_done(mm)

            def vector(dve):
                for n in range(4):
                    x = XT[:, 2 * n:2 * n + 2, :]
                    dve.wait_ge(sem("chunk_done"), base + n + 1)
                    dve.tensor_tensor(x, x, split(acc(n)[:, 0:1024], 2, T), ALU.add).then_inc(sem(name), 1)

            phases.append(dict(tensor=tensor, vector=vector))

        project_out("dil_proj", CH_DILO, OD)

        HF = view(R, FF_T, T)
        FS = [view(R + 11264 + 512 * i, T) for i in range(2)]

        def swiglu(f, base):
            silu, hid, down = f"ff{f}_silu", f"ff{f}_hid", f"ff{f}_down"

            def tensor(pe):
                for n in range(FF_T):
                    arrived(pe, base + n)
                    if n >= 2:
                        pe.wait_ge(sem(hid), n - 1)
                    for j in range(2):
                        for k in range(KT):
                            mm = pe.matmul(acc(n)[:, j * 512:j * 512 + 512], wtile(base + n, k, j), HT[:, k, :],
                                           start=(k == 0), stop=(k == KT - 1))
                    chunk_done(mm)
                for b in range(FF_T * KT):
                    o, k = divmod(b, FF_T)
                    c = base + FF_T + b // 16
                    if b % 16 == 0:
                        arrived(pe, c)
                    if b == 0:
                        pe.wait_ge(sem(hid), FF_T)
                    if k == 0 and o >= 2:
                        pe.wait_ge(sem(down), o - 1)
                    mm = pe.matmul(acc(o)[:, 0:512], ring[:, c % NSLOT, (b % 16) * P:(b % 16) * P + P], HF[:, k, :],
                                   start=(k == 0), stop=(k == FF_T - 1))
                    if b % 16 == 15:
                        chunk_done(mm)

            def scalar(act):
                for n in range(FF_T):
                    act.wait_ge(sem("chunk_done"), base + n + 1)
                    if n >= 2:
                        act.wait_ge(sem(hid), n - 1)
                    act.activation(FS[n % 2], acc(n)[:, 0:512], ACT.Silu).then_inc(sem(silu), 1)

            def vector(dve):
                for n in range(FF_T):
                    dve.wait_ge(sem(silu), n + 1)
                    dve.tensor_tensor(HF[:, n, :], acc(n)[:, 512:1024], FS[n % 2], ALU.mult).then_inc(sem(hid), 1)
                for o in range(KT):
                    dve.wait_ge(sem("chunk_done"), base + FF_T + (FF_T * o + FF_T - 1) // 16 + 1)
                    dve.tensor_tensor(XT[:, o, :], XT[:, o, :], acc(o)[:, 0:512], ALU.add).then_inc(sem(down), 1)

            phases.append(dict(tensor=tensor, scalar=scalar, vector=vector))

        norm(XT, T, HT, lambda k: v("ffn_norm", k, 1))
        swiglu(0, CH_FF0)

        norm(XT, T, HT, lambda k: v("attn_norm", 8 + k, 1))
        LQ = view(R, GH, T)
        LK = view(R + 2048, GH, T)
        LV = view(R + 4096, TT, D)
        OG = view(R + 8192, KT, T)
        LA = view(R + 12288, 2, TT, 512)
        LTMP = view(R + 22048, 4096)
        ZT = view(R + 26144, T)
        WG = view(R + 26656, 512)

        def lin_load_gpsimd(pool):
            pool.memset(ZT[0:64, :], 1.0)
            for d in range(2):
                pool.dma_start(WG[32 * d:32 * d + 17, :], w_gate_fb[d]).then_inc(sem("lin_loaded"), 16)
            pool.wait_ge(sem("lin_loaded"), 32)

        phases[-1]["gpsimd"] = lin_load_gpsimd

        def lin_tensor(pe):
            for d in range(2):
                for k in range(KT):
                    mm = pe.matmul(pf[32 * d:32 * d + 16, 3072:3584], wdt[:, k, 16 * d:16 * d + 16], HT[:, k, :],
                                   start=(k == 0), stop=(k == KT - 1))
            mm.then_inc(sem("lin_z"), 1)
            pe.wait_ge(sem("lin_zt"), 1)
            for i in range(8):
                d, t = divmod(i, TT)
                if i >= 2:
                    pe.wait_ge(sem("lin_raw"), i - 1)
                pe.matmul(bank(6 + i % 2), ZT[32 * d:32 * d + 17, t * P:t * P + P], WG[32 * d:32 * d + 17, :],
                          start=True, stop=True).then_inc(sem("lin_gate"), 1)
            for n in range(8):
                c = CH_GLA + n
                arrived(pe, c)
                if n >= 2:
                    pe.wait_ge(sem("lin_evac"), n - 1)
                if n < 4:
                    for j in range(2):
                        for k in range(KT):
                            mm = pe.matmul(acc2(n)[:, j * 512:j * 512 + 512], wtile(c, k, j), HT[:, k, :],
                                           start=(k == 0), stop=(k == KT - 1))
                else:
                    for t in range(TT):
                        for k in range(KT):
                            mm = pe.matmul(acc2(n)[:, t * 256:t * 256 + 256], HT[:, k, t * P:t * P + P],
                                           wtile(c, k, 0, 256), start=(k == 0), stop=(k == KT - 1))
                chunk_done(mm)

        def lin_scalar(act):
            act.wait_ge(sem("lin_z"), 1)
            for d in range(2):
                ins = act.activation(ZT[32 * d:32 * d + 16, :], pf[32 * d:32 * d + 16, 3072:3584], ACT.Copy)
            ins.then_inc(sem("lin_zt"), 1)
            for i in range(8):
                act.wait_ge(sem("lin_gate"), i + 1)
                act.activation(LA[:, i // TT, i % TT, :], bank(6 + i % 2), ACT.Copy).then_inc(sem("lin_raw"), 1)
            act.wait_ge(sem("lin_abs"), 1)
            act.activation(LTMP, LTMP, ACT.Exp).then_inc(sem("lin_exp"), 1)
            act.wait_ge(sem("lin_exp"), 1)
            act.activation(LTMP, LTMP, ACT.Ln, bias=1.0).then_inc(sem("lin_ln"), 1)
            for n in range(8):
                act.wait_ge(sem("chunk_done"), CH_GLA + n + 1)
                if n < 4:
                    dst = (LQ, LK)[n // 2][:, 2 * (n % 2):2 * (n % 2) + 2, :]
                    act.activation(dst, split(acc2(n), 2, T), ACT.Copy).then_inc(sem("lin_evac"), 1)
                else:
                    act.activation(LV[:, :, (n - 4) * 256:(n - 3) * 256], split(acc2(n), TT, 256),
                                   ACT.Copy).then_inc(sem("lin_evac"), 1)

        def lin_vector(dve):
            la = LA.rearrange("p a b c -> p (a b c)")
            dve.wait_ge(sem("lin_raw"), 8)
            dve.scalar_tensor_tensor(LTMP, la, -1.0, la, ALU.mult, ALU.min).then_inc(sem("lin_abs"), 1)
            dve.wait_ge(sem("lin_ln"), 1)
            dve.scalar_tensor_tensor(la, la, 0.0, LTMP, ALU.min, ALU.subtract)

        phases.append(dict(tensor=lin_tensor, scalar=lin_scalar, vector=lin_vector))

        NC = T // GC
        QTL = [view(R + 16384 + 512 * d, T) for d in range(2)]
        KTL = [view(R + 17408 + 512 * d, T) for d in range(2)]
        KEL = [view(R + 18432 + 512 * d, T) for d in range(2)]
        KET = [view(R + 19456 + 512 * d, TT, P) for d in range(2)]
        AM = [view(R + 20480 + 256 * d, TT, GC) for d in range(2)]
        BLS = view(R + 20992, 2, NC)
        DEC = view(R + 21008, 2, NC)
        EBL = [view(R + 21024 + 512 * d, T) for d in range(2)]
        SIN = [view(R + 22048 + 2048 * d, NC, 256) for d in range(2)]
        ORDER = (list(range(NC)), list(range(NC))[::-1])
        KVS = [(d, i) for i in range(NC - 1) for d in range(2)]

        def gla_tensor(pe):
            for h in range(GH):
                for d in range(2):
                    if h >= 1 and d == 0:
                        pe.wait_ge(sem("gla_o"), h)
                    for t in range(TT):
                        mm = pe.matmul(bank(d, P, t * P), LA[:, d, t, h * P:h * P + P],
                                       C[("gtriu", "gtril")[d]], start=True, stop=True)
                    mm.then_inc(sem("gla_b"), 1)
                for d in range(2):
                    i = 2 * h + d
                    pe.wait_ge(sem("gla_q"), i + 1)
                    pe.wait_ge(sem("gla_k"), i + 1)
                    for c in range(NC):
                        o = pf[64 * (c % 2):64 * (c % 2) + 64, (2 + d) * 512 + (c // 2) * GC:(2 + d) * 512 + (c // 2) * GC + GC]
                        mm = pe.matmul(o, KTL[d][:, c * GC:c * GC + GC], QTL[d][:, c * GC:c * GC + GC],
                                       start=True, stop=True)
                    mm.then_inc(sem("gla_attn"), 1)
                    pe.wait_ge(sem("gla_kend"), i + 1)
                    for t in range(TT):
                        mm = pe.transpose(bank(4 + d, P, t * P), KEL[d][:, t * P:t * P + P], C["ident"])
                    mm.then_inc(sem("gla_kturn"), 1)
                pe.wait_ge(sem("gla_kturned"), 2 * h + 2)
                for x, (d, i) in enumerate(KVS):
                    n = len(KVS) * h + x
                    c = ORDER[d][i]
                    rows = slice(64 * (c % 2), 64 * (c % 2) + 64)
                    if n >= 2:
                        pe.wait_ge(sem("gla_state"), n - 1)
                    pe.matmul(bank(6 + x % 2, 256), KET[d][rows, c // 2, :], LV[rows, c // 2, h * 256:h * 256 + 256],
                              start=True, stop=True).then_inc(sem("gla_kv"), 1)
                pe.wait_ge(sem("gla_masked"), 2 * h + 2)
                pe.wait_ge(sem("gla_state"), len(KVS) * (h + 1))
                for e in range(2):
                    for c in range(NC):
                        rows = slice(64 * (c % 2), 64 * (c % 2) + 64)
                        o = bank(e + 2 * (c % 2), GC, (c // 2) * GC)
                        steps = []
                        for d in range(2):
                            steps.append((LV[rows, c // 2, h * 256 + e * P:h * 256 + e * P + P], AM[d][rows, c // 2, :]))
                            if c != ORDER[d][0]:
                                steps.append((SIN[d][:, c, e * P:e * P + P], QTL[d][:, c * GC:c * GC + GC]))
                        for x, (lhs, rhs) in enumerate(steps):
                            mm = pe.matmul(o, lhs, rhs, start=(x == 0), stop=(x == len(steps) - 1))
                mm.then_inc(sem("gla_omm"), 1)

        def gla_vector(dve):
            for d in range(2):
                dve.memset(AM[d].rearrange("p a b -> p (a b)"), 0.0)
                ins = dve.memset(SIN[d][:, ORDER[d][0], :], 0.0)
            ins.then_inc(sem("gla_zeroed"), 1)
            dve.wait_ge(sem("gla_zeroed"), 1)
            for h in range(GH):
                for d in range(2):
                    i = 2 * h + d
                    last = bank(d)[:, 63:T:64] if d == 0 else bank(d)[:, 0:T:64]
                    dve.wait_ge(sem("gla_b"), i + 1)
                    if h >= 1:
                        dve.wait_ge(sem("gla_kturn"), i - 1)
                    dve.tensor_copy(BLS[:, d, :], last).then_inc(sem("gla_last"), 1)
                    dve.wait_ge(sem("gla_last"), i + 1)
                    dve.tensor_tensor(split(KEL[d], NC, GC), BLS[:, d, :].unsqueeze(2).to_broadcast([P, NC, GC]),
                                      split(bank(d), NC, GC), ALU.subtract).then_inc(sem("gla_diff"), 1)
                for d in range(2):
                    i = 2 * h + d
                    dve.wait_ge(sem("gla_eb"), i + 1)
                    dve.scalar_tensor_tensor(QTL[d], LQ[:, h, :], float(P) ** -0.5, EBL[d], ALU.mult,
                                             ALU.mult).then_inc(sem("gla_q"), 1)
                for d in range(2):
                    dve.wait_ge(sem("gla_attn"), 2 * h + d + 1)
                    dve.copy_predicated(AM[d], gmask[:, d:d + 1, :].to_broadcast([P, TT, GC]),
                                        split(bank(2 + d, 256), TT, GC)).then_inc(sem("gla_masked"), 1)
                for x, (d, i) in enumerate(KVS):
                    c, nxt = ORDER[d][i], ORDER[d][i + 1]
                    n = len(KVS) * h + x
                    dve.wait_ge(sem("gla_kv"), n + 1)
                    if i >= 1:
                        dve.wait_ge(sem("gla_state"), n - 1)
                    dve.scalar_tensor_tensor(SIN[d][:, nxt, :], SIN[d][:, c, :], DEC[:, d, c:c + 1],
                                             bank(6 + x % 2, 256), ALU.mult, ALU.add).then_inc(sem("gla_state"), 1)

        def gla_scalar(act):
            for h in range(GH):
                for d in range(2):
                    i = 2 * h + d
                    act.wait_ge(sem("gla_diff"), i + 1)
                    act.activation(KEL[d], KEL[d], ACT.Exp).then_inc(sem("gla_ekend"), 1)
                    act.activation(DEC[:, d, :], BLS[:, d, :], ACT.Exp)
                    if h >= 1:
                        act.wait_ge(sem("gla_attn"), i - 1)
                    act.activation(KTL[d], bank(d), ACT.Exp, scale=-1.0).then_inc(sem("gla_enb"), 1)
                    act.activation(EBL[d], bank(d), ACT.Exp).then_inc(sem("gla_eb"), 1)
                for d in range(2):
                    i = 2 * h + d
                    act.wait_ge(sem("gla_kturn"), i + 1)
                    act.activation(KET[d].rearrange("p a b -> p (a b)"), bank(4 + d), ACT.Copy).then_inc(sem("gla_kturned"), 1)
                act.wait_ge(sem("gla_omm"), h + 1)
                for odd in range(2):
                    dst = OG[:, 2 * h:2 * h + 2, :].rearrange("p a (c o t) -> p a c o t", o=2, t=GC)[:, :, :, odd, :]
                    src = split(pf[:, 1024 * odd:1024 * odd + 1024], 2, 512)[:, :, 0:T // 2]
                    ins = act.activation(dst, src.rearrange("p a (c t) -> p a c t", t=GC), ACT.Copy)
                ins.then_inc(sem("gla_o"), 1)

        def gla_gpsimd(pool):
            for h in range(GH):
                for d in range(2):
                    i = 2 * h + d
                    pool.wait_ge(sem("gla_ekend"), i + 1)
                    pool.tensor_tensor(KEL[d], KEL[d], LK[:, h, :], ALU.mult).then_inc(sem("gla_kend"), 1)
                    pool.wait_ge(sem("gla_enb"), i + 1)
                    pool.tensor_tensor(KTL[d], KTL[d], LK[:, h, :], ALU.mult).then_inc(sem("gla_k"), 1)

        phases.append(dict(tensor=gla_tensor, scalar=gla_scalar, vector=gla_vector, gpsimd=gla_gpsimd))

        LS = [view(R + 1024 * i, 2, T) for i in range(2)]
        LSQ = [view(R + 2048 + 1024 * i, 2, T) for i in range(2)]
        LR = [view(R + 4096 + 512 * i, T) for i in range(2)]

        def lgate_tensor(pe):
            for g in range(GH):
                c = CH_GLAR + g
                arrived(pe, c)
                if g >= 2:
                    pe.wait_ge(sem("lg_silu"), g - 1)
                for j in range(2):
                    for k in range(KT):
                        mm = pe.matmul(acc(g)[:, j * 512:j * 512 + 512], wtile(c, k, j), HT[:, k, :],
                                       start=(k == 0), stop=(k == KT - 1))
                chunk_done(mm)
                pe.wait_ge(sem("lg_sq"), g + 1)
                if g >= 2:
                    pe.wait_ge(sem("lg_ln"), g - 1)
                for j in range(2):
                    mm = pe.matmul(bank(6 + g % 2), C["ones"], LSQ[g % 2][:, j, :], start=(j == 0), stop=(j == 1))
                mm.then_inc(sem("lg_sums"), 1)

        def lgate_scalar(act):
            for g in range(GH):
                if g >= 2:
                    act.wait_ge(sem("lg_sums"), g - 1)
                    act.wait_ge(sem("lg_out"), g - 1)
                act.activation(LSQ[g % 2], OG[:, 2 * g:2 * g + 2, :], ACT.Square).then_inc(sem("lg_sq"), 1)
                act.wait_ge(sem("chunk_done"), CH_GLAR + g + 1)
                act.activation(LS[g % 2], split(acc(g)[:, 0:1024], 2, T), ACT.Silu).then_inc(sem("lg_silu"), 1)
                act.wait_ge(sem("lg_sums"), g + 1)
                act.activation(LR[g % 2], bank(6 + g % 2), ACT.Ln, scale=1.0 / 256, bias=epst[:, :]).then_inc(sem("lg_ln"), 1)
                act.wait_ge(sem("lg_ln"), g + 1)
                act.activation(LR[g % 2], LR[g % 2], ACT.Exp, scale=-0.5).then_inc(sem("lg_rstd"), 1)

        def lgate_vector(dve):
            link = Link(dve, "lg_link")
            for g in range(GH):
                y = OG[:, 2 * g:2 * g + 2, :]
                dve.wait_ge(sem("lg_rstd"), g + 1)
                for j in range(2):
                    ins = dve.scalar_tensor_tensor(y[:, j, :], y[:, j, :], v("b_out_norm", 2 * g + j, 1), LR[g % 2],
                                                   ALU.mult, ALU.mult)
                link(ins)
                dve.wait_ge(sem("lg_silu"), g + 1)
                dve.tensor_tensor(y, y, LS[g % 2], ALU.mult).then_inc(sem("lg_out"), 1)

        phases.append(dict(tensor=lgate_tensor, scalar=lgate_scalar, vector=lgate_vector))
        project_out("gla_proj", CH_GLAO, OG)
        norm(XT, T, HT, lambda k: v("ffn_norm", 8 + k, 1))
        swiglu(1, CH_FF1)

        def meet(eng, n):
            eng.drain().then_inc(sem("stage_ended"), 1)
            eng.wait_ge(sem("stage_ended"), 4 * (n + 1))

        def run(eng, name):
            for n, stage in enumerate(phases[:stop]):
                if name in stage:
                    stage[name](eng)
                meet(eng, n)
                if n == BLOCK1_STAGES - 1:
                    if name == "gpsimd":
                        for old in BLOCK1_SEMS:
                            eng.sem_clear(sem(old))
                        eng.drain().then_inc(sem("semaphores_cleared"), 1)
                    eng.wait_ge(sem("semaphores_cleared"), 1)

        block = ctx.enter_context(nc.Block())

        @block.sync
        def _(sp):
            ada_sync(sp)
            for c in range(CH_END if stop is None else LIMIT):
                if c == CH_SH + 3:
                    moe_sync(sp)
                if c >= NSLOT:
                    sp.wait_ge(sem("chunk_done"), c - NSLOT + 1)
                sp.dma_start(ring[:, c % NSLOT, :], wstream[c]).then_inc(sem(f"slot{c % NSLOT}_full"), 16)
            if stop is None:
                sp.wait_ge(sem("stage_ended"), 4 * len(phases))
                sp.dma_start(out_t, XT).then_inc(sem("out"), 16)
                sp.wait_ge(sem("out"), 16)
            else:
                sp.wait_ge(sem("stage_ended"), 4 * len(phases[:stop]))
                sp.dma_start(dbg, arena[:, :]).then_inc(sem("out"), 16)
                sp.dma_start(out_t, arena[:, 0:4096].rearrange("p (k t) -> p k t", t=T)).then_inc(sem("out"), 16)
                sp.wait_ge(sem("out"), 32)

        @block.tensor
        def _(pe):
            run(pe, "tensor")

        @block.scalar
        def _(act):
            run(act, "scalar")

        @block.vector
        def _(dve):
            run(dve, "vector")

        @block.gpsimd
        def _(pool):
            run(pool, "gpsimd")


def program(nc, a, out_t, dbg=None, stop=None):
    xs = nc.dram_tensor("xs", (MAXBLK * P, D), F32, kind="Internal").ap()
    ys = nc.dram_tensor("ys", (MAXBLK * P, D), F32, kind="Internal").ap()
    two_blocks(nc, a["wstream"], a["x_t"], a["ctx_t"], a["vecs"], a["consts"], a["rope_t"], a["gmask_t"],
               a["dmask_t"], a["iota_t"], a["w_dt"], a["w_router"], a["we_gu"], a["we_down"], a["w_z"],
               a["w_gate_fb"], xs, ys, out_t, dbg, stop)


def _tables(np):
    i = np.arange(P)
    eye = np.eye(P)
    rot = np.zeros((P, P))
    for h in range(2):
        for j in range(32):
            rot[64 * h + 32 + j, 64 * h + j] = -1.0
            rot[64 * h + j, 64 * h + 32 + j] = 1.0
    pair = (i[:, None] // 64 == i[None, :] // 64) * 1.0
    triu = (i[:, None] <= i[None, :]) * 1.0
    mats = [eye, np.ones((P, P)), rot, pair, triu, triu.T, triu - eye, triu * pair / 16.0, triu.T * pair / 16.0]
    consts = np.stack(mats, axis=1).astype(np.float32)

    def cs(ang):
        ang = np.concatenate([ang, ang, ang, ang], axis=-1)
        return np.stack([np.cos(ang).T, np.sin(ang).T], axis=1).astype(np.float32)

    t = np.arange(T, dtype=np.float32)
    inv1 = np.float32(10000.0) ** (-np.arange(0, 32, 2, dtype=np.float32) / np.float32(32))
    ang1 = np.concatenate([np.floor(t / 64)[:, None] * inv1, (t % 64)[:, None] * inv1], axis=-1)
    inv2 = np.float32(10000.0) ** (-np.arange(32, dtype=np.float32) / np.float32(32))
    ang2 = t[:, None] * inv2[None, :]
    s, q = i[:, None] % 64, np.arange(64)[None, :]
    gmask = np.stack([s <= q, s > q], axis=1).astype(np.uint32)
    big = np.float32(-1e30)
    m0 = [np.where(np.abs(np.arange(T)[None, :] - (4 * i + r)[:, None]) <= 64, 0, big) for r in range(4)]
    m1 = np.where(np.abs(i[None, :] - i[:, None]) <= 64, 0, big)
    m2 = np.where((i[None, :] - i[:, None]) % 4 == 0, 0, big)
    dmask = np.concatenate(m0 + [m1, m2, eye], axis=1)
    return consts, cs(ang1), cs(ang2), gmask, dmask


def kernel(**inputs):
    import ml_dtypes
    import numpy as np
    import concourse.bacc as bacc
    from concourse.bass_utils import run_bass_kernel_spmd as launch

    g = {n: np.asarray(a) for n, a in inputs.items()}

    def feat(a):
        return np.ascontiguousarray(a.reshape(a.shape[0], -1, P).transpose(2, 1, 0))

    def vecf(a):
        return a.reshape(-1, P).T

    def chunks(w):
        return w.reshape(KT, P, -1, 256).transpose(2, 1, 0, 3).reshape(-1, P, CHW)

    def blocks(w):
        b = w.reshape(FF_T, P, KT, P).transpose(2, 0, 1, 3).reshape(-1, 16, P, P)
        return b.transpose(0, 2, 1, 3).reshape(-1, P, CHW)

    def gate_up(w):
        return w.reshape(D, 2, -1, P).transpose(0, 2, 1, 3).reshape(D, -1)

    w_in = g["w_in"][0]
    wg, wa, wsd = w_in[:, 6176:8224], g["w_branch_attn"][0], g["w_branch_ssd"][0]
    merge = np.stack([w.reshape(D, 4, 256) for w in (wg[:, :D], wa, wg[:, D:], wsd)], axis=2).reshape(D, -1)
    a_in = g["a_w_in_2"][0].reshape(D, 9, 4, 256).transpose(0, 2, 1, 3).reshape(D, -1)
    b_in = g["b_w_in_2"][0]
    stream = [chunks(g["w_ada"][0]), chunks(w_in[:, :3072]), chunks(w_in[:, 4096:6144]), chunks(w_in[:, 3072:4096]),
              chunks(merge), chunks(g["w_out"][0]), chunks(g["w_sh_gate"][0]), chunks(g["w_sh_up"][0]),
              g["w_sh_down"][0].reshape(2, P, D).transpose(1, 0, 2).reshape(1, P, CHW),
              chunks(a_in), chunks(g["a_w_out_2"][0]),
              chunks(gate_up(g["ffn_w_gate_up_2"][0])), blocks(g["ffn_w_down_2"][0]),
              chunks(b_in[:, 0:2048]), chunks(b_in[:, 2048:3072]), chunks(g["b_w_out_2"][0]),
              chunks(gate_up(g["ffn_w_gate_up_2"][1])), blocks(g["ffn_w_down_2"][1])]
    wstream = np.concatenate(stream, axis=0)
    assert wstream.shape[0] == CH_END

    def row(a):
        return np.broadcast_to(a.reshape(1, -1), (P, a.size))

    cols = {
        "cc": feat(np.stack([g["c"][0], g["c_ctx"]])).reshape(P, 16), "b_ada": vecf(g["b_ada"][0]),
        "g_pre_mix": vecf(g["g_pre_mix"][0]), "g_post_mix": vecf(g["g_post_mix"][0]),
        "g_pre_ffn": vecf(g["g_pre_ffn"][0]), "g_post_ffn": vecf(g["g_post_ffn"][0]),
        "g_subln": g["g_attn_subln"][0][:, None], "conv_w": vecf(g["conv_w"][0].reshape(-1)),
        "conv_b": vecf(g["conv_b"][0]), "d_skip": vecf(np.repeat(g["d_skip"][0], 64)),
        "g_ssd": vecf(g["g_ssd_norm"][0]), "attn_norm": vecf(g["attn_norm_2"].reshape(-1)),
        "ffn_norm": vecf(g["ffn_norm_2"].reshape(-1)), "a_q_norm": np.tile(g["a_q_norm_2"][0], (1, 2)).T,
        "a_k_norm": np.tile(g["a_k_norm_2"][0], (1, 2)).T, "b_out_norm": vecf(g["b_out_norm_2"][0].reshape(-1)),
        "lam": row(np.concatenate([g["lam_q1"][0], g["lam_k1"][0], g["lam_q2"][0], g["lam_k2"][0]])),
        "dt_bias": row(g["dt_bias"][0]), "a_log": row(g["a_log"][0]), "router_bias": row(g["router_bias"][0]),
    }
    vecs = np.concatenate([cols[n] for n in VEC], axis=1).astype(np.float32)
    consts, rope1, rope2, gmask, dmask = _tables(np)
    w_gate_fb = np.stack([np.concatenate([g["b_w_gate_f_2"][0], g["b_gate_bias_f_2"]]),
                          np.concatenate([g["b_w_gate_b_2"][0], g["b_gate_bias_b_2"]])])
    arrays = {
        "wstream": wstream, "x_t": feat(g["x"][0]), "ctx_t": feat(g["ctx"][0]), "vecs": vecs, "consts": consts,
        "rope_t": np.stack([rope1, rope2]), "gmask_t": gmask, "dmask_t": dmask.astype(ml_dtypes.bfloat16),
        "iota_t": np.ascontiguousarray(row(np.concatenate([np.tril(np.ones((8, 8)), -1).reshape(-1), np.arange(MAXBLK)])
                                          .astype(np.float32))),
        "w_dt": np.ascontiguousarray(w_in[:, 6144:6176].reshape(KT, P, 32).transpose(1, 0, 2)),
        "w_router": np.ascontiguousarray(g["w_router"][0].reshape(KT, P, E_N).transpose(1, 0, 2)),
        "we_gu": np.ascontiguousarray(np.concatenate([g["w_e_gate"][0], g["w_e_up"][0]], axis=-1)
                                      .reshape(E_N, KT, P, 512).transpose(0, 2, 1, 3)).reshape(E_N, P, KT * 512),
        "we_down": np.ascontiguousarray(g["w_e_down"][0].reshape(E_N, 2, P, D).transpose(0, 2, 1, 3)).reshape(E_N, P, 2 * D),
        "w_z": np.ascontiguousarray(b_in[:, 3072:3104].reshape(KT, P, 32).transpose(1, 0, 2)),
        "w_gate_fb": w_gate_fb,
    }
    nc = bacc.Bacc("TRN2", target_bir_lowering=False, num_devices=1)
    aps = {n: nc.dram_tensor(n, a.shape, mybir.dt.from_np(a.dtype), kind="ExternalInput").ap()
           for n, a in arrays.items()}
    out_t = nc.dram_tensor("out_t", (P, KT, T), F32, kind="ExternalOutput").ap()
    program(nc, aps, out_t)
    r = launch(nc, [arrays], core_ids=[0])
    got = r.results[0]["out_t"]
    return np.ascontiguousarray(got.transpose(2, 1, 0).reshape(1, T, D))
```

```python
from contextlib import ExitStack

import concourse.bass as bass
from concourse import mybir
from concourse.alu_op_type import AluOpType as ALU

ACT = mybir.ActivationFunctionType
AX = mybir.AxisListType
F32 = mybir.dt.float32
F32R = mybir.dt.float32r
BF16 = mybir.dt.bfloat16
I32 = mybir.dt.int32
U32 = mybir.dt.uint32

P = 128
D = 1024
KT = D // P
T = 512
TC = 256
TA = T + TC
TT = T // P
AT = TA // P
EPS = 1e-6
H1 = 8
SSD_H, SSD_G = 16, 4
E_N, E_F = 64, 256
MAXBLK = T * 8 // P + E_N
FF_T = 2816 // P
FF_PARTS = (12, FF_T - 12)
GH = 4
GC = 64
LAM_INIT = 0.8 - 0.6
NSLOT = 4
ARENA = 40960
CHW = 2048

CH_ADA = 0
CH_QKV = CH_ADA + 2 * D // 256
CH_MOD = CH_QKV + 12
CH_XBC = CH_MOD + 4 * D // 256
CH_Z = CH_XBC + 8
CH_MERGE = CH_Z + 4
CH_OUT = CH_MERGE + 16
CH_SH = CH_OUT + 4
CH_DIL = CH_SH + 3
CH_DILO = CH_DIL + 36
CH_FF0 = CH_DILO + 4
CH_GLA = CH_FF0 + 33
CH_GLAR = CH_GLA + 8
CH_GLAO = CH_GLAR + 4
CH_FF1 = CH_GLAO + 4
CH_END = CH_FF1 + 33

SPLIT = list(range(CH_FF0, CH_FF0 + 33)) + list(range(CH_FF1, CH_FF1 + 33))

VEC = {}


def _cols():
    at = 0
    for name, n in [("cc", 16), ("b_ada", 48), ("g_pre_mix", 8), ("g_post_mix", 8), ("g_pre_ffn", 8),
                    ("g_post_ffn", 8), ("g_subln", 1), ("conv_w", 48), ("conv_b", 16), ("d_skip", 8),
                    ("g_ssd", 8), ("attn_norm", 16), ("ffn_norm", 16), ("a_q_norm", 3), ("a_k_norm", 3),
                    ("b_out_norm", 8), ("lam", 256), ("dt_bias", 32), ("a_log", 32), ("router_bias", 64)]:
        VEC[name] = (at, n)
        at += n
    return at


NVEC = _cols()
CONSTS = ["ident", "ones", "rot", "pair", "triu", "tril", "triu_strict", "gtriu", "gtril"]


BLOCK1_SEMS = (
    "mod", "ada_silu", "lam_exp", "lam_dots", "da_bias", "da_diff", "da_exp", "da_head", "da_ln", "da_max", "da_norm", "da_recip", "da_rstd",
    "da_scores", "da_sq", "da_ss", "da_turn", "da_turned", "da_values", "dt_abs", "dt_diff", "dt_ln",
    "dt_raw", "dt_sums", "dta", "qk_cos", "qk_out", "qk_raw", "qk_rot", "qk_sin", "ssd_btok", "ssd_bturn",
    "ssd_cb", "ssd_cbmm", "ssd_ce", "ssd_decay", "ssd_decayed", "ssd_erow", "ssd_exp", "ssd_rows", "ssd_seg",
    "ssd_state", "ssd_statemm", "ssd_sub", "ssd_tridta", "ssd_xdt", "ssd_xturn", "ssd_xw", "ssd_y", "ssd_ymm",
    "xbc_mid", "xbc_silu", "xbc_taps", "z_gated", "z_ln",
)
BLOCK2_SEMS = (
    "dil_bias", "dil_cos", "dil_evac", "dil_exp", "dil_half", "dil_ln", "dil_max", "dil_o", "dil_out", "dil_prob",
    "dil_pv", "dil_qn", "dil_recip", "dil_rot", "dil_rstd", "dil_scores", "dil_sin", "dil_ss", "dil_turn",
    "dil_turned", "gla_attn", "gla_b", "gla_diff", "gla_eb", "gla_ekend", "gla_enb", "gla_k", "gla_kend",
    "gla_kturn", "gla_kturned", "gla_kv", "gla_last", "gla_masked", "gla_o", "gla_omm", "gla_q", "gla_state",
    "gla_zeroed", "lg_ln", "lg_out", "lg_rstd", "lg_silu", "lg_sq", "lg_sums", "lin_abs", "lin_evac",
    "lin_exp", "lin_gate", "lin_ln", "lin_raw", "lin_z", "lin_zt",
)


def two_blocks(nc, wstream, x_t, ctx_t, vecs, consts, rope_t, gmask_t, dmask_t, iota_t, w_dt, w_router,
               we_gu, we_down, w_z, w_gate_fb, xs, ys, out_t, dbg, stop):
    ctx = ExitStack()
    with ctx:
        def sb(name, shape, dt=F32):
            return ctx.enter_context(nc.sbuf_tensor(name, shape, dt))

        made = {}

        def sem(name):
            if name in BLOCK2_SEMS:
                name = BLOCK1_SEMS[BLOCK2_SEMS.index(name)]
            if name not in made:
                made[name] = ctx.enter_context(nc.semaphore(name))
            return made[name]

        ring = sb("ring", [P, NSLOT, CHW])
        arena_at = (nc.sbuf_base + 31) // 32 * 32
        arena = sb("arena", [P, ARENA])
        arena_r = [nc.alloc_sbuf_tensor_at(f"arena_r{i}", [P, CHW], F32R, offset=arena_at + 4 * CHW * i)
                   for i in range(ARENA // CHW)]
        vec = sb("vec", [P, NVEC])
        cst = sb("cst", [P, len(CONSTS), P])
        rope = sb("rope", [P, 2, T])
        gmask = sb("gmask", [P, 2, 64], U32)
        identb = sb("identb", [P, P], BF16)
        wdt = sb("wdt", [P, KT, 32])
        wrt = sb("wrt", [P, KT, E_N])
        mod = sb("mod", [P, 48, 2])
        cs = sb("cs", [P, KT, 2])
        gain = sb("gain", [P, 40])
        small = sb("small", [P, 64])
        epst = sb("epst", [P, 1])
        ps = ctx.enter_context(nc.psum_tensor("ps", [P, 8, 512], F32))
        pf = ps[:, :, :].rearrange("p b n -> p (b n)")

        def bank(b, n=512, off=0):
            return pf[:, b * 512 + off:b * 512 + off + n]

        def view(at, *dims):
            n = 1
            for d in dims:
                n *= d
            ap = arena[:, at:at + n]
            if len(dims) == 2:
                return ap.rearrange("p (a b) -> p a b", b=dims[1])
            if len(dims) == 3:
                return ap.rearrange("p (a b c) -> p a b c", b=dims[1], c=dims[2])
            return ap

        def rounded(at, n):
            assert at % CHW + n <= CHW
            return arena_r[at // CHW][:, at % CHW:at % CHW + n]

        def rounded_rows(at, rows):
            return [rounded(at + T * i, T) for i in range(rows)]

        def split(ap, *dims):
            if len(dims) == 2:
                return ap.rearrange("p (a b) -> p a b", b=dims[1])
            return ap.rearrange("p (a b c) -> p a b c", b=dims[1], c=dims[2])

        def v(name, a=0, n=None):
            at, m = VEC[name]
            return vec[:, at + a:at + a + (m if n is None else n)]

        C = {name: cst[:, i, :] for i, name in enumerate(CONSTS)}
        XT = view(0, KT, T)
        HT = view(4096, KT, T)
        R = 8192
        WHL = R

        A1, A2, G1, G2 = 0, 16, 24, 32

        phases = []

        class Link:

            def __init__(self, eng, name):
                self.eng, self.sem, self.n = eng, sem(name), 0

            def __call__(self, ins):
                ins.then_inc(self.sem, 1)
                self.n += 1
                self.eng.wait_ge(self.sem, self.n)

        def arrived(pe, c):
            pe.wait_ge(sem(f"slot{c % NSLOT}_full"), 16 * (c // NSLOT + 1))

        def wtile(c, k, j, n=P):
            return ring[:, c % NSLOT, k * 256 + j * P:k * 256 + j * P + n]

        def chunk_done(ins):
            ins.then_inc(sem("chunk_done"), 1)

        def load_exp_ln(act):
            act.preload_act_table_set("natural_log_exp_and_others")

        def whalf(c, part):
            return rounded(WHL + (SPLIT.index(c) % 2) * 2 * CHW + part * CHW, CHW)

        def chunk_hi(act, c):
            i = SPLIT.index(c)
            arrived(act, c)
            if i >= 2:
                act.wait_ge(sem("chunk_done"), SPLIT[i - 2] + 1)
            act.activation(whalf(c, 0), ring[:, c % NSLOT, :], ACT.Copy).then_inc(sem("chunk_hi"), 1)

        def chunk_lo(pool, c):
            pool.wait_ge(sem("chunk_hi"), SPLIT.index(c) + 1)
            pool.tensor_tensor(whalf(c, 1), ring[:, c % NSLOT, :], whalf(c, 0).bitcast(F32),
                               ALU.subtract).then_inc(sem("chunk_lo"), 1)

        def halves_ready(pe, c):
            pe.wait_ge(sem("chunk_lo"), SPLIT.index(c) + 1)

        def product(pe, out, c, at, rhs, start, stop, n=P):
            hi, lo = (whalf(c, part)[:, at:at + n] for part in range(2))
            pe.matmul(out, hi, rhs[0], start=start, stop=False)
            pe.matmul(out, hi, rhs[1], start=False, stop=False)
            return pe.matmul(out, lo, rhs[0], start=False, stop=stop)

        NLOAD = 9

        def ada_sync(sp):
            for dst, src in ((vec[:, :], vecs), (cst[:, :, :], consts), (XT, x_t), (view(R, KT, TC), ctx_t),
                             (rope[:, :, :], rope_t[0]), (gmask[:, :, :], gmask_t),
                             (identb[:, :], dmask_t[:, 2304:2432]), (wdt[:, :, :], w_dt),
                             (wrt[:, :, :], w_router)):
                sp.dma_start(dst, src).then_inc(sem("loaded"), 16)

        def ada_scalar(act):
            act.wait_ge(sem("loaded"), 16 * NLOAD)
            act.activation(cs[:, :, :], split(v("cc"), KT, 2), ACT.Silu).then_inc(sem("ada_silu"), 1)
            act.wait_ge(sem("lam_dots"), 1)
            act.activation(small[:, 2:4], small[:, 0:2], ACT.Exp).then_inc(sem("lam_exp"), 1)

        def modulate(pe, c, j, out):
            if j == 0:
                arrived(pe, c)
            for k in range(KT):
                mm = pe.matmul(out, wtile(c, k, j), cs[:, k, :], start=(k == 0), stop=(k == KT - 1))
            if j == 1:
                chunk_done(mm)

        def ada_tensor(pe):
            pe.wait_ge(sem("ada_silu"), 1)
            for m in range(16):
                modulate(pe, CH_ADA + m // 2, m % 2, bank(7, 2, 2 * m))

        def ada_vector(dve):
            link = Link(dve, "ada_link")
            dve.memset(epst[:, :], EPS)
            dve.wait_ge(sem("loaded"), 16 * NLOAD)
            lam = split(v("lam"), 4, 64)
            prod = split(view(R + 2048, 128), 2, 64)
            link(dve.tensor_tensor(prod, lam[:, 0:4:2, :], lam[:, 1:4:2, :], ALU.mult))
            dve.tensor_reduce(small[:, 0:2], prod, AX.X, ALU.add).then_inc(sem("lam_dots"), 1)
            dve.wait_ge(sem("lam_exp"), 1)
            link(dve.tensor_tensor(small[:, 4:5], small[:, 3:4], small[:, 2:3], ALU.subtract))
            link(dve.tensor_scalar(small[:, 5:6], small[:, 4:5], -LAM_INIT, None, ALU.add))
            link(dve.tensor_scalar(small[:, 6:7], v("g_subln"), 1.0 - LAM_INIT, None, ALU.mult))
            dve.wait_ge(sem("chunk_done"), CH_ADA + 8)
            link(dve.tensor_tensor(mod[:, 0:16, :], split(bank(7, 32), 16, 2),
                                   v("b_ada", 0, 16).unsqueeze(2).to_broadcast([P, 16, 2]), ALU.add))
            for s in range(2):
                dve.scalar_tensor_tensor(gain[:, A1 + 8 * s:A1 + 8 * s + 8], mod[:, 8:16, s], 1.0, v("g_pre_mix"),
                                         ALU.add, ALU.mult)

        def mod_vector(dve):
            dve.wait_ge(sem("chunk_done"), CH_MOD + 16)
            dve.tensor_tensor(mod[:, 16:48, :], split(bank(5, 64, 256), 32, 2),
                              v("b_ada", 16, 32).unsqueeze(2).to_broadcast([P, 32, 2]), ALU.add).then_inc(sem("mod"), 1)
            dve.wait_ge(sem("mod"), 1)
            dve.scalar_tensor_tensor(gain[:, A2:A2 + 8], mod[:, 32:40, 0], 1.0, v("g_pre_ffn"), ALU.add, ALU.mult)
            dve.tensor_tensor(gain[:, G1:G1 + 8], mod[:, 16:24, 0], v("g_post_mix"), ALU.mult)
            dve.tensor_tensor(gain[:, G2:G2 + 8], mod[:, 40:48, 0], v("g_post_ffn"), ALU.mult)

        phases.append(dict(scalar=ada_scalar, tensor=ada_tensor, vector=ada_vector))

        norms = [0]
        halved = [0]
        SQ = R + 32768 - 1024

        def norm(src, n, dst=None, scale=None, shift=None, residual=None, halves=None):
            m = norms[0]
            norms[0] += 1
            low_base = 8 * halved[0]
            halved[0] += halves is not None
            sq = [view(SQ + 512 * i, 512)[:, 0:n] for i in range(2)]
            tmp = [view(SQ - 1024 + 512 * i, 512)[:, 0:n] for i in range(2)]
            ss, rs = bank(6, n), bank(7, n)

            def scalar(act):
                load_exp_ln(act)
                for k in range(KT):
                    if k >= 2:
                        act.wait_ge(sem("norm_summed"), 8 * m + k - 1)
                    act.activation(sq[k % 2], src[:, k, :], ACT.Square).then_inc(sem("norm_sq"), 1)
                act.wait_ge(sem("norm_summed"), 8 * m + 8)
                act.activation(rs, ss, ACT.Ln, scale=1.0 / D, bias=epst[:, :]).then_inc(sem("norm_ln"), 1)
                act.wait_ge(sem("norm_ln"), m + 1)
                act.activation(rs, rs, ACT.Exp, scale=-0.5).then_inc(sem("norm_rstd"), 1)
                if halves is not None:
                    for k in range(KT):
                        act.wait_ge(sem("norm_scaled"), 8 * m + k + 1)
                        act.activation(halves[0][k], tmp[k % 2], ACT.Copy).then_inc(sem("norm_out"), 1)
                elif dst is not None:
                    for k in range(KT):
                        act.wait_ge(sem("norm_scaled"), 8 * m + k + 1)
                        if shift is None:
                            act.activation(dst[:, k, :], tmp[k % 2], ACT.Copy).then_inc(sem("norm_out"), 1)
                        else:
                            act.activation(dst[:, k, :], tmp[k % 2], ACT.Identity, scale=scale(k),
                                           bias=shift(k)).then_inc(sem("norm_out"), 1)
                else:
                    for k in range(KT):
                        act.sem_inc(sem("norm_out"), 1)

            def tensor(pe):
                for k in range(KT):
                    pe.wait_ge(sem("norm_sq"), 8 * m + k + 1)
                    pe.matmul(ss, C["ones"], sq[k % 2], start=(k == 0),
                              stop=(k == KT - 1)).then_inc(sem("norm_summed"), 1)

            def vector(dve):
                def low(k):
                    dve.wait_ge(sem("norm_out"), 8 * m + k + 1)
                    dve.tensor_tensor(halves[1][k], tmp[k % 2], halves[0][k].bitcast(F32),
                                      ALU.subtract).then_inc(sem("norm_lo"), 1)

                dve.wait_ge(sem("norm_rstd"), m + 1)
                if halves is not None:
                    for k in range(KT):
                        if k >= 2:
                            low(k - 2)
                            dve.wait_ge(sem("norm_lo"), low_base + k - 1)
                        dve.scalar_tensor_tensor(tmp[k % 2], src[:, k, :], scale(k), rs, ALU.mult,
                                                 ALU.mult).then_inc(sem("norm_scaled"), 1)
                    low(KT - 2)
                    low(KT - 1)
                    return
                for k in range(KT):
                    if dst is not None:
                        if k >= 2:
                            dve.wait_ge(sem("norm_out"), 8 * m + k - 1)
                        if shift is None:
                            dve.scalar_tensor_tensor(tmp[k % 2], src[:, k, :], scale(k), rs, ALU.mult,
                                                     ALU.mult).then_inc(sem("norm_scaled"), 1)
                        else:
                            dve.tensor_tensor(tmp[k % 2], src[:, k, :], rs, ALU.mult).then_inc(sem("norm_scaled"), 1)
                    else:
                        dve.scalar_tensor_tensor(tmp[k % 2], src[:, k, :], scale(k), rs, ALU.mult,
                                                 ALU.mult).then_inc(sem("norm_scaled"), 1)
                        dve.wait_ge(sem("norm_scaled"), 8 * m + k + 1)
                        dve.tensor_tensor(residual[:, k, :], residual[:, k, :], tmp[k % 2], ALU.add)

            phases.append(dict(scalar=scalar, tensor=tensor, vector=vector))

        HC = view(R, KT, TC)
        norm(XT, T, HT, lambda k: gain[:, A1 + k:A1 + k + 1], lambda k: mod[:, k, 0:1])
        norm(HC, TC, HC, lambda k: gain[:, A1 + 8 + k:A1 + 9 + k], lambda k: mod[:, k, 1:2])

        O1 = view(R + 2048, H1, T)
        Q = view(R + 6144, H1, T)
        K = view(R + 10240, H1, TA)
        V = view(R + 16384, AT, D)
        W0 = R + 22528

        def acc(n):
            return pf[:, (n % 2) * 1536:(n % 2) * 1536 + 1536]

        def qkv_tensor(pe):
            def rotate(ch):
                pe.wait_ge(sem("qk_raw"), ch + 1)
                if ch >= 1:
                    pe.wait_ge(sem("qk_out"), ch)
                for j in range(2):
                    mm = pe.matmul(bank(6 + j), C["rot"], view(W0 + (ch % 2) * 1024 + j * 512, 512),
                                   start=True, stop=True)
                mm.then_inc(sem("qk_rot"), 1)

            for ch in range(12):
                c = CH_QKV + ch
                a = acc(ch)
                arrived(pe, c)
                if ch >= 2:
                    pe.wait_ge(sem("qk_raw"), ch - 1)
                if ch < 8:
                    for j in range(2):
                        for k in range(KT):
                            mm = pe.matmul(a[:, j * 512:j * 512 + 512], wtile(c, k, j), HT[:, k, :],
                                           start=(k == 0), stop=(k == KT - 1))
                        if ch >= 4:
                            for k in range(KT):
                                mm = pe.matmul(a[:, 1024 + j * 256:1280 + j * 256], wtile(c, k, j), HC[:, k, :],
                                               start=(k == 0), stop=(k == KT - 1))
                else:
                    for t in range(AT):
                        for k in range(KT):
                            lhs = HC[:, k, t * P:t * P + P] if t < 2 else HT[:, k, (t - 2) * P:(t - 1) * P]
                            mm = pe.matmul(a[:, t * 256:t * 256 + 256], lhs, wtile(c, k, 0, 256),
                                           start=(k == 0), stop=(k == KT - 1))
                chunk_done(mm)
                if 1 <= ch < 9:
                    rotate(ch - 1)

        def qkv_scalar(act):
            for ch in range(12):
                a = acc(ch)
                act.wait_ge(sem("chunk_done"), CH_QKV + ch + 1)
                if ch < 8:
                    if ch >= 2:
                        act.wait_ge(sem("qk_rot"), ch - 1)
                        act.wait_ge(sem("qk_cos"), ch - 1)
                    if ch >= 4:
                        act.activation(K[:, 2 * (ch - 4):2 * (ch - 4) + 2, 0:TC], split(a[:, 1024:1536], 2, 256),
                                       ACT.Copy)
                    act.activation(view(W0 + (ch % 2) * 1024, 1024), a[:, 0:1024], ACT.Copy).then_inc(sem("qk_raw"), 1)
                else:
                    act.activation(V[:, :, (ch - 8) * 256:(ch - 7) * 256], split(a, AT, 256),
                                   ACT.Copy).then_inc(sem("qk_raw"), 1)

        def qkv_gpsimd(pool):
            cos = rope[:, 0:1, :].to_broadcast([P, 2, T])
            for ch in range(8):
                pool.wait_ge(sem("qk_raw"), ch + 1)
                if ch >= 2:
                    pool.wait_ge(sem("qk_out"), ch - 1)
                pool.tensor_tensor(view(W0 + 2048 + (ch % 2) * 1024, 2, 512), view(W0 + (ch % 2) * 1024, 2, 512),
                                   cos, ALU.mult).then_inc(sem("qk_cos"), 1)

        def qkv_vector(dve):
            sin = rope[:, 1:2, :].to_broadcast([P, 2, T])
            rot = split(pf[:, 3072:4096], 2, 512)
            for ch in range(8):
                dve.wait_ge(sem("qk_rot"), ch + 1)
                dve.tensor_tensor(rot, rot, sin, ALU.mult).then_inc(sem("qk_sin"), 1)
                dve.wait_ge(sem("qk_cos"), ch + 1)
                dve.wait_ge(sem("qk_sin"), ch + 1)
                dst = Q[:, 2 * ch:2 * ch + 2, :] if ch < 4 else K[:, 2 * (ch - 4):2 * (ch - 4) + 2, TC:TA]
                dve.tensor_tensor(dst, rot, view(W0 + 2048 + (ch % 2) * 1024, 2, 512),
                                  ALU.add).then_inc(sem("qk_out"), 1)

        phases.append(dict(tensor=qkv_tensor, scalar=qkv_scalar, gpsimd=qkv_gpsimd, vector=qkv_vector))

        NU = H1 * TT

        def prob(n, c):
            return view(W0 + ((n % 2) * 2 + c) * TA, TA)

        def wT(h):
            return view(W0 + 4 * TA + (h % 2) * AT * T, AT, T)

        SC = small[:, 8:40]

        def da_tensor(pe):
            def scores(n):
                h, qt = divmod(n, TT)
                for c in range(2):
                    if n >= 1:
                        pe.wait_ge(sem("da_exp"), 2 * (n - 1) + c + 1)
                    q = Q[64 * c:64 * c + 64, h, qt * P:qt * P + P]
                    pe.matmul(bank(2 * c), q, K[64 * c:64 * c + 64, h, 0:512], start=True, stop=True)
                    pe.matmul(bank(2 * c + 1, 256), q, K[64 * c:64 * c + 64, h, 512:TA], start=True,
                              stop=True).then_inc(sem("da_scores"), 1)

            def turn(n):
                if n >= 1:
                    pe.wait_ge(sem("da_turned"), n)
                modulate(pe, CH_MOD + n // 2, n % 2, bank(5, 2, 256 + 2 * n))
                pe.wait_ge(sem("da_diff"), n + 1)
                for t in range(AT):
                    mm = pe.transpose(bank(4, P, t * P), prob(n, 0)[:, t * P:t * P + P], C["ident"])
                mm.then_inc(sem("da_turn"), 1)

            def values(h):
                pe.wait_ge(sem("da_turned"), 4 * h + 4)
                if h >= 1:
                    pe.wait_ge(sem("da_head"), h)
                for t in range(AT):
                    mm = pe.matmul(bank(6), V[:, t, h * P:h * P + P], wT(h)[:, t, :], start=(t == 0),
                                   stop=(t == AT - 1))
                mm.then_inc(sem("da_values"), 1)

            def square_sum(h):
                pe.wait_ge(sem("da_sq"), h + 1)
                pe.matmul(bank(7), C["ones"], view(SQ, 512), start=True, stop=True).then_inc(sem("da_ss"), 1)

            scores(0)
            for n in range(NU):
                if n + 1 < NU:
                    scores(n + 1)
                turn(n)
                if n % 4 == 0 and n:
                    values(n // 4 - 1)
                if n % 4 == 1 and n > 4:
                    square_sum(n // 4 - 1)
            values(H1 - 1)
            square_sum(H1 - 1)

        def da_vector(dve):
            def row_max(n):
                s = SC[:, 16 * (n % 2):16 * (n % 2) + 16]
                for c in range(2):
                    dve.wait_ge(sem("da_scores"), 2 * n + c + 1)
                    dve.reduce_max(s[:, c:c + 1], pf[:, 1024 * c:1024 * c + TA], AX.X).then_inc(sem("da_max"), 1)
                    dve.wait_ge(sem("da_max"), 2 * n + c + 1)
                    dve.tensor_scalar(s[:, 2 + c:3 + c], s[:, c:c + 1], -0.125, None,
                                      ALU.mult).then_inc(sem("da_bias"), 1)

            def diff(n):
                s = SC[:, 16 * (n % 2):16 * (n % 2) + 16]
                dve.wait_ge(sem("da_exp"), 2 * n + 2)
                dve.reciprocal(s[:, 6:8], s[:, 4:6]).then_inc(sem("da_recip"), 1)
                dve.wait_ge(sem("da_recip"), n + 1)
                dve.tensor_tensor(s[:, 8:9], s[:, 7:8], small[:, 5:6], ALU.mult)
                dve.tensor_scalar(prob(n, 0), prob(n, 0), s[:, 6:7], None, ALU.mult).then_inc(sem("da_norm"), 1)
                dve.wait_ge(sem("da_norm"), n + 1)
                dve.scalar_tensor_tensor(prob(n, 0), prob(n, 1), s[:, 8:9], prob(n, 0), ALU.mult,
                                         ALU.add).then_inc(sem("da_diff"), 1)

            def head(h):
                dve.wait_ge(sem("da_rstd"), h + 1)
                dve.scalar_tensor_tensor(O1[:, h, :], bank(6), small[:, 6:7], view(SQ + 512, 512), ALU.mult,
                                         ALU.mult).then_inc(sem("da_head"), 1)

            for n in range(NU + 1):
                if n < NU:
                    row_max(n)
                if n >= 1:
                    diff(n - 1)
                if n % 4 == 3 and n > 4:
                    head(n // 4 - 1)
            head(H1 - 1)
            mod_vector(dve)

        def da_scalar(act):
            def turned(n):
                h, qt = divmod(n, TT)
                act.wait_ge(sem("da_turn"), n + 1)
                if h >= 2 and qt == 0:
                    act.wait_ge(sem("da_values"), h - 1)
                act.activation(wT(h)[:, :, qt * P:qt * P + P], split(bank(4, TA), AT, P),
                               ACT.Copy).then_inc(sem("da_turned"), 1)

            def head(h):
                act.wait_ge(sem("da_values"), h + 1)
                act.activation(view(SQ, 512), bank(6), ACT.Square).then_inc(sem("da_sq"), 1)

            def rstd(h):
                act.wait_ge(sem("da_ss"), h + 1)
                if h >= 1:
                    act.wait_ge(sem("da_head"), h)
                act.activation(view(SQ + 512, 512), bank(7), ACT.Ln, scale=1.0 / P,
                               bias=epst[:, :]).then_inc(sem("da_ln"), 1)
                act.wait_ge(sem("da_ln"), h + 1)
                act.activation(view(SQ + 512, 512), view(SQ + 512, 512), ACT.Exp, scale=-0.5).then_inc(sem("da_rstd"), 1)

            for n in range(NU):
                s = SC[:, 16 * (n % 2):16 * (n % 2) + 16]
                for c in range(2):
                    act.wait_ge(sem("da_bias"), 2 * n + c + 1)
                    if n >= 2:
                        act.wait_ge(sem("da_turn"), n - 1)
                    act.activation(prob(n, c), pf[:, 1024 * c:1024 * c + TA], ACT.Exp, scale=0.125,
                                   bias=s[:, 2 + c:3 + c], accum_out=s[:, 4 + c:5 + c]).then_inc(sem("da_exp"), 1)
                if n >= 1:
                    turned(n - 1)
                if n % 4 == 1 and n > 4:
                    head(n // 4 - 1)
                if n % 4 == 2 and n > 4:
                    rstd(n // 4 - 1)
            turned(NU - 1)
            head(H1 - 1)
            rstd(H1 - 1)

        NFILL = 8

        def fill(pool, buf, i):
            src = rope[:, :, :].rearrange("p a b -> p (a b)").unsqueeze(1).to_broadcast([P, NFILL, D])
            pool.dma_start(buf[i * NFILL * P:(i + 1) * NFILL * P, :].rearrange("(b p) d -> p b d", p=P),
                           src).then_inc(sem("filled"), 16)

        def fill_gpsimd(pool):
            for i in range(MAXBLK // NFILL):
                pool.wait_ge(sem("da_exp"), 4 * i + 1)
                fill(pool, xs, i)

        phases.append(dict(tensor=da_tensor, scalar=da_scalar, vector=da_vector, gpsimd=fill_gpsimd))

        XBC = view(R + 6144, 16, TA)
        Y = view(R + 18432, KT, T)
        SEGS = ((0, TC, 1024), (TC, T, 0))

        def xbc_tensor(pe):
            for t in range(AT):
                for k in range(KT):
                    lhs = HC[:, k, t * P:t * P + P] if t < 2 else HT[:, k, (t - 2) * P:(t - 1) * P]
                    mm = pe.matmul(bank(6, 32, t * 32), lhs, wdt[:, k, :], start=(k == 0), stop=(k == KT - 1))
            mm.then_inc(sem("dt_raw"), 1)
            for ch in range(8):
                c = CH_XBC + ch
                a = acc(ch)
                arrived(pe, c)
                if ch >= 2:
                    pe.wait_ge(sem("xbc_taps"), ch - 1)
                for j in range(2):
                    for k in range(KT):
                        pe.matmul(a[:, j * 512:j * 512 + 512], wtile(c, k, j), HT[:, k, :],
                                  start=(k == 0), stop=(k == KT - 1))
                    for k in range(KT):
                        mm = pe.matmul(a[:, 1024 + j * 256:1280 + j * 256], wtile(c, k, j), HC[:, k, :],
                                       start=(k == 0), stop=(k == KT - 1))
                chunk_done(mm)

        def part(a, j, base, n, lo, hi):
            at = base + j * n
            return a[:, at + lo:at + hi]

        def xbc_scalar(act):
            def silu(ch):
                act.wait_ge(sem("xbc_taps"), ch + 1)
                act.activation(XBC[:, 2 * ch:2 * ch + 2, :], XBC[:, 2 * ch:2 * ch + 2, :],
                               ACT.Silu).then_inc(sem("xbc_silu"), 1)

            for ch in range(8):
                act.wait_ge(sem("chunk_done"), CH_XBC + ch + 1)
                for j in range(2):
                    m = 2 * ch + j
                    for first, n, base in SEGS:
                        ins = act.activation(XBC[:, m, first:first + n], part(acc(ch), j, base, n, 0, n), ACT.Identity,
                                             scale=v("conv_w", 16 + m, 1), bias=v("conv_b", m, 1))
                ins.then_inc(sem("xbc_mid"), 1)
                if ch:
                    silu(ch - 1)
            silu(7)

        def xbc_vector(dve):
            link = Link(dve, "xbc_link")
            for ch in range(8):
                dve.wait_ge(sem("xbc_mid"), ch + 1)
                for lo, tap in ((0, 0), (1, 32)):
                    for j in range(2):
                        m = 2 * ch + j
                        for first, n, base in SEGS:
                            o = XBC[:, m, first + 1 - lo:first + n - lo]
                            ins = dve.scalar_tensor_tensor(o, part(acc(ch), j, base, n, lo, n - 1 + lo),
                                                           v("conv_w", tap + m, 1), o, ALU.mult, ALU.add)
                    if lo == 0:
                        link(ins)
                    else:
                        ins.then_inc(sem("xbc_taps"), 1)

        assert MAXBLK // NFILL == 2 * AT

        S0 = R + 22528 + 7168
        DT = view(S0, 2, AT, SSD_H)
        DTA = view(S0 + 192, 2, AT, SSD_H)
        ACOL = view(S0 + 384, 2, AT, SSD_H)
        TOEND = view(S0 + 576, 2, AT, SSD_H)
        DECAY = view(S0 + 768, 2, AT, SSD_H)

        def flat(ap):
            return ap.rearrange("p a b c -> p (a b c)")

        def dt_vector(dve):
            link = Link(dve, "dt_link")
            tmp = view(S0 + 384, AT, 32)
            dve.wait_ge(sem("dt_raw"), 1)
            link(dve.tensor_tensor(tmp, split(bank(6, 192), AT, 32),
                                   v("dt_bias").unsqueeze(1).to_broadcast([P, AT, 32]), ALU.add))
            dve.scalar_tensor_tensor(view(S0 + 576, AT, 32), tmp, -1.0, tmp, ALU.mult, ALU.min).then_inc(sem("dt_abs"), 1)
            dve.wait_ge(sem("dt_ln"), 1)
            for d in range(2):
                ins = dve.scalar_tensor_tensor(DT[:, d], tmp[:, :, 16 * d:16 * d + 16], 0.0,
                                               view(S0 + 576, AT, 32)[:, :, 16 * d:16 * d + 16], ALU.max, ALU.add)
            link(ins)
            for d in range(2):
                ins = dve.scalar_tensor_tensor(
                    DTA[:, d], DT[:, d], -1.0,
                    v("a_log", 16 * d, 16).unsqueeze(1).to_broadcast([P, AT, 16]), ALU.mult, ALU.mult)
            ins.then_inc(sem("dta"), 1)
            dve.wait_ge(sem("dt_sums"), 1)
            link(dve.tensor_copy(flat(ACOL), bank(6, 192)))
            dve.tensor_tensor(flat(TOEND), bank(7, 192), flat(ACOL), ALU.subtract).then_inc(sem("dt_diff"), 1)
            dve.wait_ge(sem("xbc_silu"), 4)
            for j in range(KT):
                dve.tensor_scalar(Y[:, j, :], XBC[:, j, TC:TA], v("d_skip", j, 1), None, ALU.mult)

        def dt_scalar(act):
            link = Link(act, "dt_act_link")
            load_exp_ln(act)
            link(act.activation(v("a_log"), v("a_log"), ACT.Exp))
            act.wait_ge(sem("dt_abs"), 1)
            link(act.activation(flat(TOEND), flat(TOEND), ACT.Exp))
            act.activation(flat(TOEND), flat(TOEND), ACT.Ln, bias=1.0).then_inc(sem("dt_ln"), 1)
            act.wait_ge(sem("dt_diff"), 1)
            act.activation(flat(TOEND), flat(TOEND), ACT.Exp)
            act.activation(flat(DECAY), bank(7, 192), ACT.Exp)

        def dt_tensor(pe):
            pe.wait_ge(sem("dta"), 1)
            pe.matmul(bank(6, 96), C["triu"], DTA[:, 0].rearrange("p a b -> p (a b)"), start=True, stop=True)
            pe.matmul(bank(6, 96, 96), C["tril"], DTA[:, 1].rearrange("p a b -> p (a b)"), start=True, stop=True)
            pe.matmul(bank(7, 192), C["ones"], flat(DTA), start=True, stop=True).then_inc(sem("dt_sums"), 1)

        def xbc_all_tensor(pe):
            xbc_tensor(pe)
            dt_tensor(pe)

        def xbc_all_scalar(act):
            xbc_scalar(act)
            dt_scalar(act)

        def xbc_all_vector(dve):
            xbc_vector(dve)
            dt_vector(dve)

        phases.append(dict(tensor=xbc_all_tensor, scalar=xbc_all_scalar, vector=xbc_all_vector))

        STEPS = [(0, 0), (1, 1), (0, 1), (1, 0), (0, 2), (1, 5), (0, 3), (1, 4), (0, 4), (1, 3), (0, 5), (1, 2)]
        NCTX = 4
        W1 = R + 22528
        DM = view(W1, SSD_H, P)
        EC = view(W1 + 2048, SSD_H, P)
        XDT = view(W1 + 4096, 1024)
        XW = view(W1 + 5120, 1024)
        BTOK = view(W1 + 6144, 512)
        CBM = view(W1 + 6656, SSD_G, P)
        STATE = [view(R + 1024 * d, 1024) for d in range(2)]
        TRI = (C["triu"], C["tril"])

        def hcol(ap):
            return ap.unsqueeze(2).to_broadcast([P, SSD_H, 64])

        def ssd_tensor(pe):
            for n, (d, t) in enumerate(STEPS):
                tok = slice(t * P, t * P + P)
                if n >= 1:
                    pe.wait_ge(sem("ssd_state"), n)
                    pe.wait_ge(sem("ssd_btok"), n)
                for j in range(KT):
                    mm = pe.transpose(bank(0, P, j * P), XBC[:, j, tok], C["ident"])
                mm.then_inc(sem("ssd_xturn"), 1)
                for g in range(SSD_G):
                    mm = pe.transpose(bank(2, P, g * P), XBC[:, 8 + g, tok], C["ident"])
                mm.then_inc(sem("ssd_bturn"), 1)
                if n >= NCTX:
                    m = n - NCTX
                    if m >= 1:
                        pe.wait_ge(sem("ssd_y"), m)
                        pe.wait_ge(sem("ssd_cb"), m)
                    for g in range(SSD_G):
                        mm = pe.matmul(bank(3, P, g * P), XBC[:, 8 + g, tok], XBC[:, 12 + g, tok],
                                       start=True, stop=True)
                    mm.then_inc(sem("ssd_cbmm"), 1)
                    pe.wait_ge(sem("ssd_tridta"), m + 1)
                    for q in range(4):
                        mm = pe.matmul(bank(4 + q), C["ones"], DM[:, 4 * q:4 * q + 4, :], start=True, stop=True)
                    mm.then_inc(sem("ssd_rows"), 1)
                    pe.wait_ge(sem("ssd_decay"), m + 1)
                    pe.wait_ge(sem("ssd_ce"), m + 1)
                    for h in range(SSD_H):
                        o = pf[64 * (h % 2):64 * (h % 2) + 64, 2048 + (h // 2) * P:2048 + (h // 2) * P + P]
                        pe.matmul(o, XDT[:, 64 * h:64 * h + 64], DM[:, h, :], start=True, stop=False)
                        mm = pe.matmul(o, STATE[d][:, 64 * h:64 * h + 64], EC[:, h, :], start=False, stop=True)
                    mm.then_inc(sem("ssd_ymm"), 1)
                pe.wait_ge(sem("ssd_xw"), n + 1)
                pe.wait_ge(sem("ssd_btok"), n + 1)
                for g in range(SSD_G):
                    mm = pe.matmul(bank(g // 2, 256, (g % 2) * 256), BTOK[:, g * P:g * P + P],
                                   XW[:, g * 256:g * 256 + 256], start=True, stop=True)
                mm.then_inc(sem("ssd_statemm"), 1)

        def ssd_vector(dve):
            for n, (d, t) in enumerate(STEPS):
                dve.wait_ge(sem("ssd_xturn"), n + 1)
                if n >= 1:
                    dve.wait_ge(sem("ssd_xw"), n)
                dve.tensor_tensor(split(XDT, SSD_H, 64), split(pf[:, 0:1024], SSD_H, 64), hcol(DT[:, d, t, :]),
                                  ALU.mult).then_inc(sem("ssd_xdt"), 1)
                if n >= NCTX:
                    m = n - NCTX
                    dve.wait_ge(sem("ssd_cbmm"), m + 1)
                    dve.tensor_tensor(CBM, split(bank(3), SSD_G, P), TRI[d].unsqueeze(1).to_broadcast([P, SSD_G, P]),
                                      ALU.mult).then_inc(sem("ssd_cb"), 1)
                    dve.wait_ge(sem("ssd_rows"), m + 1)
                    dve.wait_ge(sem("ssd_erow"), m + 1)
                    dve.tensor_tensor(DM, split(pf[:, 2048:4096], SSD_H, P),
                                      ACOL[:, d, t, :].unsqueeze(2).to_broadcast([P, SSD_H, P]),
                                      ALU.subtract).then_inc(sem("ssd_sub"), 1)
                    dve.wait_ge(sem("ssd_sub"), m + 1)
                    dve.tensor_scalar(DM, DM, 0.0, None, ALU.min).then_inc(sem("ssd_seg"), 1)
                    dve.wait_ge(sem("ssd_exp"), m + 1)
                    dve.wait_ge(sem("ssd_cb"), m + 1)
                    dve.tensor_tensor(DM.rearrange("p (g r) i -> p g r i", r=4),
                                      pf[:, 2048:4096].rearrange("p (g r i) -> p g r i", r=4, i=P),
                                      CBM.unsqueeze(2).to_broadcast([P, SSD_G, 4, P]),
                                      ALU.mult).then_inc(sem("ssd_decay"), 1)
                    dve.wait_ge(sem("ssd_ymm"), m + 1)
                    y = Y[:, :, (t - 2) * P:(t - 1) * P]
                    dve.tensor_tensor(y, y, split(pf[:, 2048:3072], KT, P), ALU.add).then_inc(sem("ssd_y"), 1)
                dve.wait_ge(sem("ssd_statemm"), n + 1)
                if n < 2:
                    dve.tensor_copy(STATE[d], pf[:, 0:1024]).then_inc(sem("ssd_state"), 1)
                else:
                    s = split(STATE[d], SSD_H, 64)
                    dve.tensor_tensor(s, s, hcol(DECAY[:, d, t, :]), ALU.mult).then_inc(sem("ssd_decayed"), 1)
                    dve.wait_ge(sem("ssd_decayed"), n - 1)
                    dve.tensor_tensor(STATE[d], STATE[d], pf[:, 0:1024], ALU.add).then_inc(sem("ssd_state"), 1)

        def ssd_scalar(act):
            for n, (d, t) in enumerate(STEPS):
                act.wait_ge(sem("ssd_bturn"), n + 1)
                if n >= 1:
                    act.wait_ge(sem("ssd_statemm"), n)
                act.activation(BTOK, bank(2), ACT.Copy).then_inc(sem("ssd_btok"), 1)
                if n >= NCTX:
                    m = n - NCTX
                    act.wait_ge(sem("ssd_rows"), m + 1)
                    if m >= 1:
                        act.wait_ge(sem("ssd_ymm"), m)
                    act.activation(EC.rearrange("p h i -> p (h i)"), pf[:, 2048:4096],
                                   ACT.Exp).then_inc(sem("ssd_erow"), 1)
                    act.wait_ge(sem("ssd_seg"), m + 1)
                    act.activation(pf[:, 2048:4096], DM.rearrange("p h i -> p (h i)"),
                                   ACT.Exp).then_inc(sem("ssd_exp"), 1)

        def ssd_gpsimd(pool):
            for n, (d, t) in enumerate(STEPS):
                fill(pool, ys, n)
                if n >= NCTX:
                    m = n - NCTX
                    if m >= 1:
                        pool.wait_ge(sem("ssd_ymm"), m)
                    pool.tensor_tensor(DM, TRI[d].unsqueeze(1).to_broadcast([P, SSD_H, P]),
                                       DTA[:, d, t, :].unsqueeze(2).to_broadcast([P, SSD_H, P]),
                                       ALU.mult).then_inc(sem("ssd_tridta"), 1)
                    pool.wait_ge(sem("ssd_erow"), m + 1)
                    ec = EC.rearrange("p (g r) i -> p g r i", r=4)
                    pool.tensor_tensor(ec, ec, XBC[:, 12:16, t * P:t * P + P].unsqueeze(2).to_broadcast([P, 4, 4, P]),
                                       ALU.mult).then_inc(sem("ssd_ce"), 1)
                pool.wait_ge(sem("ssd_xdt"), n + 1)
                if n >= 1:
                    pool.wait_ge(sem("ssd_statemm"), n)
                pool.tensor_tensor(split(XW, SSD_H, 64), split(XDT, SSD_H, 64), hcol(TOEND[:, d, t, :]),
                                   ALU.mult).then_inc(sem("ssd_xw"), 1)

        phases.append(dict(tensor=ssd_tensor, vector=ssd_vector, scalar=ssd_scalar, gpsimd=ssd_gpsimd))

        ZS = [view(R + 6144 + 1024 * i, 2, T) for i in range(2)]
        ZQ = [view(R + 8192 + 1024 * i, 2, T) for i in range(2)]
        ZR = [view(R + 10240 + 512 * i, T) for i in range(2)]

        def z_tensor(pe):
            def sums(g):
                pe.wait_ge(sem("z_sq"), g + 1)
                if g >= 1:
                    pe.wait_ge(sem("z_ln"), g)
                for j in range(2):
                    mm = pe.matmul(bank(6), C["ones"], ZQ[g % 2][:, j, :], start=(j == 0), stop=(j == 1))
                mm.then_inc(sem("z_sums"), 1)

            for g in range(4):
                c = CH_Z + g
                arrived(pe, c)
                if g >= 2:
                    pe.wait_ge(sem("z_silu"), g - 1)
                for j in range(2):
                    for k in range(KT):
                        mm = pe.matmul(acc(g)[:, j * 512:j * 512 + 512], wtile(c, k, j), HT[:, k, :],
                                       start=(k == 0), stop=(k == KT - 1))
                chunk_done(mm)
                if g:
                    sums(g - 1)
            sums(3)

        def z_scalar(act):
            def rstd(g):
                act.wait_ge(sem("z_gated"), g + 1)
                act.activation(ZQ[g % 2], Y[:, 2 * g:2 * g + 2, :], ACT.Square).then_inc(sem("z_sq"), 1)
                load_exp_ln(act)
                act.wait_ge(sem("z_sums"), g + 1)
                if g >= 2:
                    act.wait_ge(sem("z_out"), g - 1)
                act.activation(ZR[g % 2], bank(6), ACT.Ln, scale=1.0 / 256, bias=epst[:, :]).then_inc(sem("z_ln"), 1)
                act.wait_ge(sem("z_ln"), g + 1)
                act.activation(ZR[g % 2], ZR[g % 2], ACT.Exp, scale=-0.5).then_inc(sem("z_rstd"), 1)

            for g in range(4):
                act.wait_ge(sem("chunk_done"), CH_Z + g + 1)
                if g >= 2:
                    act.wait_ge(sem("z_gated"), g - 1)
                act.activation(ZS[g % 2], split(acc(g)[:, 0:1024], 2, T), ACT.Silu).then_inc(sem("z_silu"), 1)
                if g:
                    rstd(g - 1)
            rstd(3)

        def z_vector(dve):
            for g in range(4):
                y = Y[:, 2 * g:2 * g + 2, :]
                dve.wait_ge(sem("z_silu"), g + 1)
                dve.tensor_tensor(y, y, ZS[g % 2], ALU.mult).then_inc(sem("z_gated"), 1)
                dve.wait_ge(sem("z_rstd"), g + 1)
                for j in range(2):
                    ins = dve.scalar_tensor_tensor(y[:, j, :], y[:, j, :], v("g_ssd", 2 * g + j, 1), ZR[g % 2],
                                                   ALU.mult, ALU.mult)
                ins.then_inc(sem("z_out"), 1)

        def fill_end_gpsimd(pool):
            pool.wait_ge(sem("filled"), 16 * 2 * (MAXBLK // NFILL))

        phases.append(dict(tensor=z_tensor, scalar=z_scalar, vector=z_vector))

        MERGED = view(R + 6144, KT, T)
        MG = [view(R + 10240 + 1024 * i, 1024) for i in range(2)]
        MT = view(R + 12288, 1024)
        MIX = view(R + 13312, KT, T)

        def merge_tensor(pe):
            for n in range(16):
                c = CH_MERGE + n
                src = (HT, O1, HT, Y)[n % 4]
                arrived(pe, c)
                if n >= 2 and n % 2 == 0:
                    pe.wait_ge(sem("merge_gate"), n // 2)
                if n >= 2 and n % 2 == 1:
                    pe.wait_ge(sem("merge_prod"), n // 2)
                for j in range(2):
                    for k in range(KT):
                        mm = pe.matmul(acc(n)[:, j * 512:j * 512 + 512], wtile(c, k, j), src[:, k, :],
                                       start=(k == 0), stop=(k == KT - 1))
                chunk_done(mm)
            for n in range(4):
                c = CH_OUT + n
                arrived(pe, c)
                if n == 0:
                    pe.wait_ge(sem("merge_sum"), 4)
                if n < 2:
                    pe.wait_ge(sem("merge_gate"), 8)
                    pe.wait_ge(sem("merge_prod"), 8)
                else:
                    pe.wait_ge(sem("mix_out"), n - 1)
                for j in range(2):
                    for k in range(KT):
                        mm = pe.matmul(acc(n)[:, j * 512:j * 512 + 512], wtile(c, k, j), MERGED[:, k, :],
                                       start=(k == 0), stop=(k == KT - 1))
                chunk_done(mm)

        def merge_scalar(act):
            for q in range(8):
                act.wait_ge(sem("chunk_done"), CH_MERGE + 2 * q + 1)
                if q >= 2:
                    act.wait_ge(sem("merge_prod"), q - 1)
                act.activation(MG[q % 2], acc(0)[:, 0:1024], ACT.Sigmoid).then_inc(sem("merge_gate"), 1)
            for n in range(4):
                act.wait_ge(sem("chunk_done"), CH_OUT + n + 1)
                act.activation(MIX[:, 2 * n:2 * n + 2, :], split(acc(n)[:, 0:1024], 2, T),
                               ACT.Copy).then_inc(sem("mix_out"), 1)

        def merge_vector(dve):
            for q in range(8):
                m = MERGED[:, 2 * (q // 2):2 * (q // 2) + 2, :].rearrange("p a b -> p (a b)")
                dve.wait_ge(sem("chunk_done"), CH_MERGE + 2 * q + 2)
                dve.wait_ge(sem("merge_gate"), q + 1)
                dst = m if q % 2 == 0 else MT
                dve.tensor_tensor(dst, acc(1)[:, 0:1024], MG[q % 2], ALU.mult).then_inc(sem("merge_prod"), 1)
                if q % 2 == 1:
                    dve.wait_ge(sem("merge_prod"), q + 1)
                    dve.tensor_tensor(m, m, MT, ALU.add).then_inc(sem("merge_sum"), 1)

        phases.append(dict(tensor=merge_tensor, scalar=merge_scalar, vector=merge_vector, gpsimd=fill_end_gpsimd))

        norm(MIX, T, None, lambda k: gain[:, G1 + k:G1 + k + 1], residual=XT)
        norm(XT, T, HT, lambda k: gain[:, A2 + k:A2 + k + 1], lambda k: mod[:, 24 + k, 0:1])

        H2TOK = view(R, TT, D)
        SHID = view(R + 4096, 2, T)
        WGU = [view(R + 5120 + 4096 * s, KT, 512) for s in range(2)]
        WD = [view(R + 13312 + 2048 * s, 2, D) for s in range(2)]
        XB = [view(R + 17408 + 1024 * s, D) for s in range(2)]
        XBT = [view(R + 19456 + 1024 * s, KT, P) for s in range(2)]
        YO = [view(R + 21504 + 1024 * s, D) for s in range(2)]
        HID = [view(R + 23552 + 256 * s, 256) for s in range(2)]
        HIDT = [view(R + 24064 + 256 * s, 2, P) for s in range(2)]
        SIL = [view(R + 24576 + 256 * s, 256) for s in range(2)]
        M0 = R + 25088
        SCO, SEL, MSK, REP, KEY = (view(M0 + 256 * i, TT, E_N) for i in range(5))
        WTS = view(M0 + 1280, TT, E_N)
        GS8 = view(M0 + 1536, TT, 8, 8)
        GSC = view(M0 + 1792, TT, 8)
        GMK = view(M0 + 1824, TT, 8)
        WSUM = view(M0 + 1856, TT)
        NB = view(M0 + 1860, E_N)
        INCL = view(M0 + 1924, E_N)
        START = view(M0 + 1988, E_N)
        DST8 = view(M0 + 2052, TT, 8)
        W8 = view(M0 + 2084, TT, 8)
        DSTI = view(M0 + 2116, 32).bitcast(U32)
        LOWER = view(M0 + 2148, 64)
        IOTA = view(M0 + 2212, MAXBLK)
        BEF = view(M0 + 2308, MAXBLK)
        BEI = view(M0 + 2404, MAXBLK).bitcast(I32)
        NPF = view(M0 + 2500, 1)
        NPI = view(M0 + 2501, 1).bitcast(I32)
        EVEN = view(M0 + 2502, MAXBLK // 2)
        CMP = view(R + 17408, MAXBLK, E_N)
        PICK = view(R + 17408, 32, E_N)
        CMPG = view(M0 + 2560, TT, 8, 8)
        CMPE = view(M0 + 2816, TT, 8, 8)

        def rt_sync_gpsimd(pool):
            pool.dma_start(view(M0 + 2148, 64 + MAXBLK), iota_t).then_inc(sem("iota_loaded"), 16)
            pool.wait_ge(sem("rt_dest"), 1)
            pool.wait_ge(sem("h2_tok"), 8)
            for t in range(TT):
                for k in range(8):
                    pool.indirect_dma_start(xs, bass.IndirectOffsetOnAxis(ap=DSTI[:, 8 * t + k:8 * t + k + 1], axis=0),
                                            H2TOK[:, t, :], None).then_inc(sem("scattered"), 16)
            pool.wait_ge(sem("scattered"), 16 * 32)

        def rt_tensor(pe):
            for t in range(TT):
                for k in range(KT):
                    mm = pe.matmul(bank(6, E_N, t * E_N), HT[:, k, t * P:t * P + P], wrt[:, k, :],
                                   start=(k == 0), stop=(k == KT - 1))
            mm.then_inc(sem("rt_logits"), 1)
            for c in range(2):
                arrived(pe, CH_SH + c)
                for j in range(2):
                    for k in range(KT):
                        mm = pe.matmul(acc(c)[:, j * 512:j * 512 + 512], wtile(CH_SH + c, k, j), HT[:, k, :],
                                       start=(k == 0), stop=(k == KT - 1))
                chunk_done(mm)
            for q in range(8):
                if q >= 2:
                    pe.wait_ge(sem("h2_tok"), q - 1)
                for i in range(4):
                    mm = pe.transpose(bank(2 + 3 * (q % 2), P, i * P), HT[:, 4 * (q % 2) + i, (q // 2) * P:(q // 2) * P + P],
                                      C["ident"])
                mm.then_inc(sem("h2_turn"), 1)
            pe.wait_ge(sem("rt_mask"), 1)
            for t in range(TT):
                for u in range(t + 1):
                    pe.matmul(bank(7, E_N, t * E_N), C["triu_strict"] if u == t else C["ones"], MSK[:, u, :],
                              start=(u == 0), stop=(u == t))
            for u in range(TT):
                mm = pe.matmul(bank(6, E_N, 256), C["ones"], MSK[:, u, :], start=(u == 0), stop=(u == TT - 1))
            mm.then_inc(sem("rt_pos"), 1)

        def rt_scalar(act):
            act.wait_ge(sem("rt_logits"), 1)
            act.activation(SCO.rearrange("p a b -> p (a b)"), bank(6, 256), ACT.Sigmoid).then_inc(sem("rt_scores"), 1)
            act.wait_ge(sem("chunk_done"), CH_SH + 1)
            act.activation(SHID, split(acc(0)[:, 0:1024], 2, T), ACT.Silu).then_inc(sem("sh_silu"), 1)
            for q in range(8):
                act.wait_ge(sem("h2_turn"), q + 1)
                act.activation(H2TOK[:, q // 2, 512 * (q % 2):512 * (q % 2) + 512], bank(2 + 3 * (q % 2)),
                               ACT.Copy).then_inc(sem("h2_tok"), 1)

        def rt_vector(dve):
            link = Link(dve, "rt_link")

            def spread(ap, n):
                return ap.unsqueeze(3).to_broadcast([P, TT, 8, n])

            def groups(ap):
                return ap.rearrange("p t (g e) -> p t g e", e=8)

            dve.wait_ge(sem("rt_scores"), 1)
            link(dve.tensor_tensor(SEL, SCO, v("router_bias").unsqueeze(1).to_broadcast([P, TT, E_N]), ALU.add))
            for t in range(TT):
                for g in range(8):
                    ins = dve.max(GS8[:, t, g, :], SEL[:, t, 8 * g:8 * g + 8])
            link(ins)
            link(dve.tensor_tensor(GSC, GS8[:, :, :, 0], GS8[:, :, :, 1], ALU.add))
            other = GSC.unsqueeze(2).to_broadcast([P, TT, 8, 8])
            this = spread(GSC, 8)
            dve.wait_ge(sem("iota_loaded"), 16)
            dve.tensor_tensor(CMPG, other, this, ALU.is_gt)
            link(dve.tensor_tensor(CMPE, other, this, ALU.is_equal))
            lower = LOWER.rearrange("p (a b) -> p a b", b=8).unsqueeze(1).to_broadcast([P, TT, 8, 8])
            link(dve.tensor_tensor(CMPE, CMPE, lower, ALU.mult))
            link(dve.tensor_tensor(CMPG, CMPG, CMPE, ALU.add))
            link(dve.tensor_reduce(GMK, CMPG, AX.X, ALU.add))
            link(dve.tensor_scalar(GMK, GMK, 3.5, None, ALU.is_lt))
            link(dve.tensor_tensor(groups(SEL), groups(SEL), spread(GMK, 8), ALU.mult))
            link(dve.tensor_scalar(GMK, GMK, -1.0, 1e30, ALU.add, ALU.mult))
            link(dve.tensor_tensor(groups(SEL), groups(SEL), spread(GMK, 8), ALU.add))
            for t in range(TT):
                ins = dve.max(DST8[:, t, :], SEL[:, t, :])
            link(ins)
            for t in range(TT):
                ins = dve.match_replace(out=REP[:, t, :], in_to_replace=DST8[:, t, :], in_values=SEL[:, t, :],
                                        imm_value=-3e38)
            link(ins)
            dve.tensor_tensor(MSK, REP, SEL, ALU.not_equal).then_inc(sem("rt_mask"), 1)
            dve.wait_ge(sem("rt_mask"), 1)
            link(dve.tensor_tensor(WTS, SCO, MSK, ALU.mult))
            link(dve.tensor_reduce(WSUM, WTS, AX.X, ALU.add))
            link(dve.reciprocal(WSUM, WSUM))
            link(dve.tensor_scalar(WSUM, WSUM, 2.5, None, ALU.mult))
            link(dve.tensor_tensor(WTS, WTS, WSUM.unsqueeze(2).to_broadcast([P, TT, E_N]), ALU.mult))
            dve.wait_ge(sem("rt_pos"), 1)
            cnt = bank(6, E_N, 256)
            link(dve.tensor_scalar(NB, cnt, 0.0, None, ALU.is_gt))
            for i in range(1, T // P):
                link(dve.scalar_tensor_tensor(NB, cnt, 128.0 * i, NB, ALU.is_gt, ALU.add))
            link(dve.tensor_tensor_scan(INCL, C["ones"][:, 0:E_N], NB, 0.0, ALU.mult, ALU.add))
            link(dve.tensor_tensor(START, INCL, NB, ALU.subtract))
            link(dve.tensor_scalar(START, START, 128.0, 1.0, ALU.mult, ALU.add))
            link(dve.tensor_tensor(KEY, split(bank(7, 256), TT, E_N), START.unsqueeze(1).to_broadcast([P, TT, E_N]),
                                   ALU.add))
            link(dve.tensor_tensor(KEY, KEY, MSK, ALU.mult))
            for t in range(TT):
                ins = dve.max(DST8[:, t, :], KEY[:, t, :])
            link(ins)
            dve.tensor_scalar(DSTI, DST8.rearrange("p a b -> p (a b)"), -1.0, None,
                              ALU.add).then_inc(sem("rt_dest"), 1)
            cmp_in = INCL[0:1, :].unsqueeze(1).to_broadcast([1, MAXBLK, E_N])
            link(dve.tensor_tensor(CMP[0:1], cmp_in, IOTA[0:1, :].unsqueeze(2).to_broadcast([1, MAXBLK, E_N]), ALU.is_le))
            link(dve.tensor_reduce(BEF[0:1, :], CMP[0:1], AX.X, ALU.add))
            dve.tensor_scalar(BEI[0:1, :], BEF[0:1, :], float(E_N - 1), None, ALU.min).then_inc(sem("rt_blocks"), 1)
            link(dve.tensor_scalar(EVEN[0:1, :], IOTA[0:1, 0:MAXBLK:2], INCL[0:1, E_N - 1:E_N], None, ALU.is_lt))
            link(dve.tensor_reduce(NPF[0:1, :], EVEN[0:1, :], AX.X, ALU.add))
            dve.tensor_copy(NPI[0:1, :], NPF[0:1, :]).then_inc(sem("rt_blocks"), 1)
            for t in range(TT):
                for k in range(8):
                    dve.scalar_tensor_tensor(PICK[:, 8 * t + k, :], KEY[:, t, :], DST8[:, t, k:k + 1], WTS[:, t, :],
                                             ALU.is_equal, ALU.mult, accum_out=W8[:, t, k:k + 1])
            dve.wait_ge(sem("sh_silu"), 1)
            dve.wait_ge(sem("chunk_done"), CH_SH + 2)
            dve.tensor_tensor(SHID, SHID, split(acc(1)[:, 0:1024], 2, T), ALU.mult)

        phases.append(dict(tensor=rt_tensor, scalar=rt_scalar, vector=rt_vector, gpsimd=rt_sync_gpsimd))
        MOE_STAGE = len(phases)

        def pairs(eng):
            return eng.value_load(NPI[0:1, 0:1], min_val=T * 8 // P // 2, max_val=MAXBLK // 2)

        def moe_sync(sp):
            sp.wait_ge(sem("rt_blocks"), 2)
            sp.wait_ge(sem("stage_ended"), 4 * MOE_STAGE)
            n = pairs(sp)

            def load(i):
                for s in range(2):
                    e = sp.value_load(BEI[0:1, bass.ds(i * 2 + s, 1)], min_val=0, max_val=E_N - 1)
                    sp.wait_ge(sem("moe_x_used"), i * 2 + (s + 1))
                    sp.dma_start(XB[s], xs[bass.ds(i * 256 + s * P, P), :]).then_inc(sem(f"moe_x{s}"), 16)
                    sp.wait_ge(sem("moe_gu_used"), i * 2 + (s + 1))
                    sp.dma_start(WGU[s].rearrange("p a b -> p (a b)"),
                                 we_gu[bass.ds(e, 1)].rearrange("o p n -> (o p) n")).then_inc(sem(f"moe_wgu{s}"), 16)
                    sp.wait_ge(sem("moe_d_used"), i * 2 + (s + 1))
                    sp.dma_start(WD[s].rearrange("p a b -> p (a b)"),
                                 we_down[bass.ds(e, 1)].rearrange("o p n -> (o p) n")).then_inc(sem(f"moe_wd{s}"), 16)

            def store(i):
                for s in range(2):
                    sp.wait_ge(sem(f"moe_y{s}"), i + 2)
                    sp.dma_start(ys[bass.ds(i * 256 + s * P, P), :], YO[s]).then_inc(sem(f"moe_out{s}"), 16)

            load(0)
            with sp.Fori(1, n) as i:
                load(i)
                store(i - 1)
            store(n - 1)
            for s in range(2):
                sp.wait_ge(sem(f"moe_out{s}"), n * 16 + 16)
                sp.dma_start(BEF[0:1, s:s + 1], IOTA[0:1, s:s + 1]).then_inc(sem("moe_rows_out"), 16)

        def moe_tensor(pe):
            for name in ("moe_x_used", "moe_gu_used", "moe_d_used"):
                pe.sem_inc(sem(name), 2)
            with pe.Fori(0, pairs(pe)) as i:
                for s in range(2):
                    pe.wait_ge(sem(f"moe_x{s}"), i * 16 + 16)
                    pe.wait_ge(sem(f"moe_y{s}"), i + 1)
                    for k in range(KT):
                        mm = pe.transpose(bank(2 * s, P, k * P), XB[s][:, k * P:k * P + P], C["ident"])
                    mm.then_inc(sem("moe_x_used"), 1)
                for s in range(2):
                    pe.wait_ge(sem(f"moe_xt{s}"), i + 1)
                    pe.wait_ge(sem(f"moe_wgu{s}"), i * 16 + 16)
                    for k in range(KT):
                        mm = pe.matmul(bank(4 + s), XBT[s][:, k, :], WGU[s][:, k, :], start=(k == 0), stop=(k == KT - 1))
                    mm.then_inc(sem("moe_gu_used"), 1)
                for s in range(2):
                    pe.wait_ge(sem(f"moe_hid{s}"), i + 1)
                    for k in range(2):
                        mm = pe.transpose(bank(6 + s, P, k * P), HID[s][:, k * P:k * P + P], C["ident"])
                    mm.then_inc(sem("moe_hturn"), 1)
                for s in range(2):
                    pe.wait_ge(sem(f"moe_hidt{s}"), i + 1)
                    pe.wait_ge(sem(f"moe_wd{s}"), i * 16 + 16)
                    for j in range(2):
                        for k in range(2):
                            mm = pe.matmul(bank(2 * s + j), HIDT[s][:, k, :], WD[s][:, k, j * 512:j * 512 + 512],
                                           start=(k == 0), stop=(k == 1))
                    mm.then_inc(sem("moe_d_used"), 1)

        def moe_scalar(act):
            act.sem_inc(sem("moe_y0"), 1)
            act.sem_inc(sem("moe_out0"), 16)
            with act.Fori(0, pairs(act)) as i:
                act.wait_ge(sem("moe_x_used"), i * 2 + 3)
                act.activation(XBT[0].rearrange("p a b -> p (a b)"), pf[:, 0:1024], ACT.Copy).then_inc(sem("moe_xt0"), 1)
                for s in range(2):
                    act.wait_ge(sem("moe_gu_used"), i * 2 + (s + 3))
                    act.activation(SIL[s], bank(4 + s, 256), ACT.Silu).then_inc(sem(f"moe_silu{s}"), 1)
                act.wait_ge(sem("moe_hturn"), i * 2 + 1)
                act.activation(HIDT[0].rearrange("p a b -> p (a b)"), bank(6, 256), ACT.Copy).then_inc(sem("moe_hidt0"), 1)
                act.wait_ge(sem("moe_d_used"), i * 2 + 3)
                act.wait_ge(sem("moe_out0"), i * 16 + 16)
                act.activation(YO[0], pf[:, 0:1024], ACT.Copy).then_inc(sem("moe_y0"), 1)

        def moe_vector(dve):
            dve.sem_inc(sem("moe_y1"), 1)
            dve.sem_inc(sem("moe_out1"), 16)
            with dve.Fori(0, pairs(dve)) as i:
                dve.wait_ge(sem("moe_x_used"), i * 2 + 4)
                dve.tensor_copy(XBT[1].rearrange("p a b -> p (a b)"), pf[:, 1024:2048]).then_inc(sem("moe_xt1"), 1)
                for s in range(2):
                    dve.wait_ge(sem(f"moe_silu{s}"), i + 1)
                    dve.tensor_tensor(HID[s], SIL[s], bank(4 + s, 256, 256), ALU.mult).then_inc(sem(f"moe_hid{s}"), 1)
                dve.wait_ge(sem("moe_hturn"), i * 2 + 2)
                dve.tensor_copy(HIDT[1].rearrange("p a b -> p (a b)"), bank(7, 256)).then_inc(sem("moe_hidt1"), 1)
                dve.wait_ge(sem("moe_d_used"), i * 2 + 4)
                dve.wait_ge(sem("moe_out1"), i * 16 + 16)
                dve.tensor_copy(YO[1], pf[:, 1024:2048]).then_inc(sem("moe_y1"), 1)

        def moe_gpsimd(pool):
            pool.wait_ge(sem("moe_rows_out"), 32)

        phases.append(dict(tensor=moe_tensor, scalar=moe_scalar, vector=moe_vector, gpsimd=moe_gpsimd))

        GB = [view(R + 5120 + 1024 * i, D) for i in range(8)]
        F = view(R + 13312, KT, T)

        def gather_gpsimd(pool):
            for n in range(32):
                if n >= 8:
                    pool.wait_ge(sem("g_used"), n - 7)
                pool.indirect_dma_start(GB[n % 8], None, ys, bass.IndirectOffsetOnAxis(ap=DSTI[:, n:n + 1], axis=0)
                                        ).then_inc(sem(f"gathered{n % 8}"), 16)

        def gather_vector(dve):
            for n in range(32):
                t, k = divmod(n, 8)
                dve.wait_ge(sem(f"gathered{n % 8}"), 16 * (n // 8 + 1))
                if k == 0:
                    dve.tensor_scalar(H2TOK[:, t, :], GB[n % 8], W8[:, t, 0:1], None, ALU.mult).then_inc(sem("g_used"), 1)
                else:
                    dve.wait_ge(sem("g_used"), n)
                    dve.scalar_tensor_tensor(H2TOK[:, t, :], GB[n % 8], W8[:, t, k:k + 1], H2TOK[:, t, :], ALU.mult,
                                             ALU.add).then_inc(sem("g_used"), 1)

        def gather_tensor(pe):
            c = CH_SH + 2
            arrived(pe, c)
            for j in range(KT):
                for k in range(2):
                    pe.matmul(bank(j), ring[:, c % NSLOT, k * D + j * P:k * D + j * P + P], SHID[:, k, :],
                              start=(k == 0), stop=(k == 1))
            pe.wait_ge(sem("g_used"), 32)
            for j in range(KT):
                for t in range(TT):
                    mm = pe.matmul(bank(j, P, t * P), H2TOK[:, t, j * P:j * P + P], C["ident"], start=False,
                                   stop=(t == TT - 1), skip_group_check=True)
                if j == KT - 1:
                    chunk_done(mm)

        def gather_scalar(act):
            act.wait_ge(sem("chunk_done"), CH_SH + 3)
            for j in range(KT):
                act.activation(F[:, j, :], bank(j), ACT.Copy)

        phases.append(dict(tensor=gather_tensor, scalar=gather_scalar, vector=gather_vector, gpsimd=gather_gpsimd))
        norm(F, T, None, lambda k: gain[:, G2 + k:G2 + k + 1], residual=XT)

        BLOCK1_STAGES = len(phases)

        OD = view(R, KT, T)

        def dq(hq, g):
            return view(R + 4096 + 9216 * (hq % 2) + 3072 * g, 2, T)

        def dk(hq, g):
            return view(R + 5120 + 9216 * (hq % 2) + 3072 * g, 2, T)

        def dv(hq, g):
            return view(R + 6144 + 9216 * (hq % 2) + 3072 * g, TT, 256)

        DRAW, DQN, DCO, DSQ, DRS = ([view(R + 22528 + 1024 * b + 512 * i, T) for i in range(2)] for b in range(5))
        DPB = [view(R + 28800 + TA * i, TA) for i in range(2)]
        DPT = [view(R + 30336 + TA * i, AT, P) for i in range(2)]
        dmask = view(R + 27648, 1152).bitcast(BF16)

        def dil_load_gpsimd(pool):
            pool.dma_start(rope[:, :, :], rope_t[1]).then_inc(sem("dil_loaded"), 16)
            pool.dma_start(dmask, dmask_t[:, 0:2304]).then_inc(sem("dil_loaded"), 16)
            pool.dma_start(wdt[:, :, :], w_z).then_inc(sem("dil_loaded"), 16)
            pool.wait_ge(sem("dil_loaded"), 48)

        norm(XT, T, HT, lambda k: v("attn_norm", k, 1))
        phases[-1]["gpsimd"] = dil_load_gpsimd

        def acc2(n):
            return pf[:, (n % 2) * 1024:(n % 2) * 1024 + 1024]

        NH, NU_Q = 18, 16

        def dil_half(h):
            return h // NH, h % NH // 6, h % 6 // 2, h % 2

        def dil_norm(h):
            hq, g, s, j = dil_half(h)
            return None if s == 2 else 12 * hq + 4 * g + 2 * s + j

        def dil_share(u):
            x = u % NU_Q
            return range(NH * (u // NU_Q + 1) + x * NH // NU_Q, NH * (u // NU_Q + 1) + (x + 1) * NH // NU_Q)

        LAST = 3 * NU_Q
        DU = 4 * NU_Q

        def dil_unit(u):
            return u // NU_Q, (u // 4) % 4, u % 4

        def score_bank(u):
            return 5 if u >= LAST and u % 2 else 0

        def dil_tensor(pe):
            def project(h):
                hq, g, s, j = dil_half(h)
                c = CH_DIL + h // 2
                before = dil_norm(h - 1) if h else None
                if before is not None:
                    pair_sums(before, h - 1)
                if j == 0:
                    arrived(pe, c)
                if h >= 2:
                    pe.wait_ge(sem("dil_evac"), h - 1)
                out = bank(5 + h % 2)
                if s < 2:
                    for k in range(KT):
                        if k == 5 and before is not None:
                            rotate(before)
                        mm = pe.matmul(out, wtile(c, k, j), HT[:, k, :], start=(k == 0), stop=(k == KT - 1))
                else:
                    for x in range(2 * KT):
                        t, k = 2 * j + x // KT, x % KT
                        if x == 10 and before is not None:
                            rotate(before)
                        lhs = HT[:, k, t * P:t * P + P] if g == 0 else HT[:, k, t:T:4]
                        mm = pe.matmul(out[:, (t % 2) * 256:(t % 2) * 256 + 256], lhs, wtile(c, k, 0, 256),
                                       start=(k == 0), stop=(k == KT - 1))
                if j == 0:
                    mm.then_inc(sem("dil_half"), 1)
                else:
                    chunk_done(mm)

            def pair_sums(n, h):
                pe.wait_ge(sem("dil_evac"), h + 1)
                if n >= 1:
                    pe.wait_ge(sem("dil_out"), n)
                pe.matmul(bank(7), C["pair"], DSQ[n % 2], start=True, stop=True).then_inc(sem("dil_ss"), 1)

            def rotate(n):
                pe.wait_ge(sem("dil_qn"), n + 1)
                pe.matmul(bank(7), C["rot"], DQN[n % 2], start=True, stop=True).then_inc(sem("dil_rot"), 1)

            def scores(u):
                hq, hl, r = dil_unit(u)
                rows, j, b = slice(64 * (hl % 2), 64 * (hl % 2) + 64), hl // 2, score_bank(u)
                if u % NU_Q == 0:
                    pe.wait_ge(sem("dil_out"), 12 * hq + 12)
                    pe.wait_ge(sem("dil_evac"), NH * hq + NH)
                if u >= 1:
                    pe.wait_ge(sem("dil_exp"), u if u <= LAST else u - 1)
                pe.matmul(bank(b), identb[:, :], dmask[:, 512 * r:512 * r + 512], start=True, stop=False)
                pe.matmul(bank(b), dq(hq, 0)[rows, j, r:T:4], dk(hq, 0)[rows, j, :], start=False, stop=True)
                for g in (1, 2):
                    o = bank(b + 1, P, P * (g - 1))
                    pe.matmul(o, identb[:, :], dmask[:, 1920 + P * g:2048 + P * g], start=True, stop=False)
                    mm = pe.matmul(o, dq(hq, g)[rows, j, r:T:4], dk(hq, g)[rows, j, r:T:4], start=False, stop=True)
                mm.then_inc(sem("dil_scores"), 1)

            def turn(u):
                pe.wait_ge(sem("dil_prob"), u + 1)
                if u >= 1:
                    pe.wait_ge(sem("dil_turned"), u)
                for t in range(AT):
                    mm = pe.transpose(bank(2, P, t * P), DPB[u % 2][:, t * P:t * P + P], C["ident"])
                mm.then_inc(sem("dil_turn"), 1)

            def values(u):
                hq, hl, r = dil_unit(u)
                pe.wait_ge(sem("dil_turned"), u + 1)
                if u % 8 == 0 and u:
                    pe.wait_ge(sem("dil_o"), u // 8)
                o = pf[64 * (hl % 2):64 * (hl % 2) + 64, 2048 + r * P:2048 + r * P + P]
                for t in range(AT):
                    val = (dv(hq, 0)[:, t, 64 * hl:64 * hl + 64] if t < TT
                           else dv(hq, t - TT + 1)[:, r, 64 * hl:64 * hl + 64])
                    mm = pe.matmul(o, val, DPT[u % 2][:, t, :], start=(t == 0), stop=(t == AT - 1))
                mm.then_inc(sem("dil_pv"), 1)

            for h in range(NH):
                project(h)
            for u in range(LAST):
                scores(u)
                if u:
                    values(u - 1)
                for h in dil_share(u):
                    project(h)
                turn(u)
            values(LAST - 1)
            scores(LAST)
            for u in range(LAST, DU):
                if u + 1 < DU:
                    scores(u + 1)
                turn(u)
                if u > LAST:
                    values(u - 1)
            values(DU - 1)

        def dil_scalar(act):
            def evacuate(h):
                hq, g, s, j = dil_half(h)
                before, n = dil_norm(h - 1) if h else None, dil_norm(h)
                if before is not None:
                    rstd(before)
                if j == 0:
                    act.wait_ge(sem("dil_half"), h // 2 + 1)
                else:
                    act.wait_ge(sem("chunk_done"), CH_DIL + h // 2 + 1)
                if n is None:
                    act.activation(dv(hq, g)[:, 2 * j:2 * j + 2, :].rearrange("p a b -> p (a b)"), bank(5 + h % 2),
                                   ACT.Copy).then_inc(sem("dil_evac"), 1)
                else:
                    if n >= 2:
                        act.wait_ge(sem("dil_qn"), n - 1)
                        act.wait_ge(sem("dil_ss"), n - 1)
                    act.activation(DRAW[n % 2], bank(5 + h % 2), ACT.Copy)
                    act.activation(DSQ[n % 2], bank(5 + h % 2), ACT.Square).then_inc(sem("dil_evac"), 1)

            def rstd(n):
                act.wait_ge(sem("dil_ss"), n + 1)
                if n >= 2:
                    act.wait_ge(sem("dil_qn"), n - 1)
                act.activation(DRS[n % 2], bank(7), ACT.Ln, scale=1.0 / 64, bias=epst[:, :]).then_inc(sem("dil_ln"), 1)
                act.wait_ge(sem("dil_ln"), n + 1)
                act.activation(DRS[n % 2], DRS[n % 2], ACT.Exp, scale=-0.5).then_inc(sem("dil_rstd"), 1)

            def turned(u):
                act.wait_ge(sem("dil_turn"), u + 1)
                if u >= 2:
                    act.wait_ge(sem("dil_pv"), u - 1)
                act.activation(DPT[u % 2].rearrange("p a b -> p (a b)"), bank(2, TA),
                               ACT.Copy).then_inc(sem("dil_turned"), 1)

            def exponent(u):
                s = SC[:, 4 * (u % 2):4 * (u % 2) + 4]
                act.wait_ge(sem("dil_bias"), u + 1)
                if u >= 2:
                    act.wait_ge(sem("dil_turn"), u - 1)
                act.activation(DPB[u % 2], bank(score_bank(u), TA), ACT.Exp, scale=0.125,
                               bias=s[:, 1:2], accum_out=s[:, 2:3]).then_inc(sem("dil_exp"), 1)

            for h in range(NH):
                evacuate(h)
            for u in range(LAST):
                if u:
                    turned(u - 1)
                exponent(u)
                for h in dil_share(u):
                    evacuate(h)
            turned(LAST - 1)
            for u in range(LAST, DU):
                exponent(u)
                if u > LAST:
                    turned(u - 1)
            turned(DU - 1)

        def dil_gpsimd(pool):
            for n in range(48):
                pool.wait_ge(sem("dil_qn"), n + 1)
                if n >= 2:
                    pool.wait_ge(sem("dil_out"), n - 1)
                pool.tensor_tensor(DCO[n % 2], DQN[n % 2], rope[:, 0, :], ALU.mult).then_inc(sem("dil_cos"), 1)

        def dil_vector(dve):
            def rotated(h):
                hq, g, s, j = dil_half(h)
                n = dil_norm(h)
                dve.wait_ge(sem("dil_rstd"), n + 1)
                if n >= 2:
                    dve.wait_ge(sem("dil_rot"), n - 1)
                    dve.wait_ge(sem("dil_cos"), n - 1)
                dve.scalar_tensor_tensor(DQN[n % 2], DRAW[n % 2], v(("a_q_norm", "a_k_norm")[s], g, 1), DRS[n % 2],
                                         ALU.mult, ALU.mult).then_inc(sem("dil_qn"), 1)
                dve.wait_ge(sem("dil_rot"), n + 1)
                dve.tensor_tensor(bank(7), bank(7), rope[:, 1, :], ALU.mult).then_inc(sem("dil_sin"), 1)
                dve.wait_ge(sem("dil_sin"), n + 1)
                dve.wait_ge(sem("dil_cos"), n + 1)
                dve.tensor_tensor((dq, dk)[s](hq, g)[:, j, :], bank(7), DCO[n % 2], ALU.add).then_inc(sem("dil_out"), 1)

            def row_max(u):
                s = SC[:, 4 * (u % 2):4 * (u % 2) + 4]
                dve.wait_ge(sem("dil_scores"), u + 1)
                dve.reduce_max(s[:, 0:1], bank(score_bank(u), TA), AX.X).then_inc(sem("dil_max"), 1)
                dve.wait_ge(sem("dil_max"), u + 1)
                dve.tensor_scalar(s[:, 1:2], s[:, 0:1], -0.125, None, ALU.mult).then_inc(sem("dil_bias"), 1)

            def probs(u):
                s = SC[:, 4 * (u % 2):4 * (u % 2) + 4]
                dve.wait_ge(sem("dil_exp"), u + 1)
                dve.reciprocal(s[:, 3:4], s[:, 2:3]).then_inc(sem("dil_recip"), 1)
                dve.wait_ge(sem("dil_recip"), u + 1)
                dve.tensor_scalar(DPB[u % 2], DPB[u % 2], s[:, 3:4], None, ALU.mult).then_inc(sem("dil_prob"), 1)

            def output(q):
                dve.wait_ge(sem("dil_pv"), 8 * q + 8)
                dve.tensor_copy(OD[:, q, :].rearrange("p (u r) -> p r u", r=4),
                                split(bank(4), 4, P)).then_inc(sem("dil_o"), 1)

            for h in range(1, NH):
                if dil_norm(h - 1) is not None:
                    rotated(h - 1)
            for u in range(LAST):
                row_max(u)
                probs(u)
                if u % 8 == 0 and u:
                    output(u // 8 - 1)
                for h in dil_share(u):
                    if dil_norm(h - 1) is not None:
                        rotated(h - 1)
            output(LAST // 8 - 1)
            row_max(LAST)
            for u in range(LAST, DU):
                if u + 1 < DU:
                    row_max(u + 1)
                probs(u)
                if u % 8 == 0 and u > LAST:
                    output(u // 8 - 1)
            output(DU // 8 - 1)

        phases.append(dict(tensor=dil_tensor, scalar=dil_scalar, vector=dil_vector, gpsimd=dil_gpsimd))

        def project_out(name, base, src):
            def tensor(pe):
                for n in range(4):
                    arrived(pe, base + n)
                    if n >= 2:
                        pe.wait_ge(sem(name), n - 1)
                    for j in range(2):
                        for k in range(KT):
                            mm = pe.matmul(acc(n)[:, j * 512:j * 512 + 512], wtile(base + n, k, j), src[:, k, :],
                                           start=(k == 0), stop=(k == KT - 1))
                    chunk_done(mm)

            def vector(dve):
                for n in range(4):
                    x = XT[:, 2 * n:2 * n + 2, :]
                    dve.wait_ge(sem("chunk_done"), base + n + 1)
                    dve.tensor_tensor(x, x, split(acc(n)[:, 0:1024], 2, T), ALU.add).then_inc(sem(name), 1)

            phases.append(dict(tensor=tensor, vector=vector))

        project_out("dil_proj", CH_DILO, OD)

        HHL = (rounded_rows(R + 20480, KT), rounded_rows(R + 24576, KT))
        FHL = (rounded_rows(R + 8192, FF_PARTS[0]), rounded_rows(R + 8192 + FF_PARTS[0] * T, FF_PARTS[0]))
        FS = [view(R + 28672 + 512 * i, T) for i in range(2)]
        FV = [view(R + 29696 + 512 * i, T) for i in range(2)]

        def swiglu(f, base):
            def S(name):
                return sem(f"ff{f}_{name}")

            def down(o):
                return bank((0, 1, 3, 4)[o % 4])

            parts = [(base, FF_PARTS[0], 0), (base + FF_PARTS[0] * 3 // 2, FF_PARTS[1], FF_PARTS[0])]

            def tensor(pe):
                for part, (first, tiles, t0) in enumerate(parts):
                    for n in range(tiles):
                        c = first + n
                        halves_ready(pe, c)
                        if t0 + n >= 2:
                            pe.wait_ge(S("value"), t0 + n - 1)
                        if part == 1 and n < 2:
                            pe.wait_ge(S("down"), KT - 2 + 2 * n)
                        for j in range(2):
                            for k in range(KT):
                                mm = product(pe, acc(n)[:, j * 512:j * 512 + 512], c, k * 256 + j * P,
                                             (HHL[0][k], HHL[1][k]), k == 0, k == KT - 1)
                        chunk_done(mm)
                    for b in range(tiles * KT):
                        o, k = divmod(b, tiles)
                        c = first + tiles + b // 16
                        if b % 16 == 0:
                            halves_ready(pe, c)
                        if b == 0:
                            pe.wait_ge(S("hid_lo"), t0 + tiles)
                        if k == 0 and o >= 4:
                            pe.wait_ge(S("down"), KT * part + o - 3)
                        mm = product(pe, down(o), c, (b % 16) * P, (FHL[0][k], FHL[1][k]),
                                     k == 0, k == tiles - 1)
                        if b % 16 == 15:
                            chunk_done(mm)

            def scalar(act):
                chunk_hi(act, base)
                chunk_hi(act, base + 1)
                for first, tiles, t0 in parts:
                    for n in range(tiles):
                        c = first + n
                        act.wait_ge(sem("chunk_done"), c + 1)
                        if t0 + n >= 2:
                            act.wait_ge(S("value"), t0 + n - 1)
                        act.activation(FS[n % 2], acc(n)[:, 0:512], ACT.Silu).then_inc(S("silu"), 1)
                        chunk_hi(act, c + 2)
                        act.wait_ge(S("value"), t0 + n + 1)
                        act.activation(FHL[0][n], FV[n % 2], ACT.Copy).then_inc(S("hid_hi"), 1)
                    for c in range(first + tiles, first + tiles * 3 // 2):
                        if c + 2 < base + 33:
                            chunk_hi(act, c + 2)

            def gpsimd(pool):
                for c in range(base, base + 33):
                    chunk_lo(pool, c)

            def vector(dve):
                for part, (first, tiles, t0) in enumerate(parts):
                    def low(n):
                        dve.wait_ge(S("hid_hi"), t0 + n + 1)
                        dve.tensor_tensor(FHL[1][n], FV[n % 2], FHL[0][n].bitcast(F32),
                                          ALU.subtract).then_inc(S("hid_lo"), 1)

                    for n in range(tiles):
                        dve.wait_ge(S("silu"), t0 + n + 1)
                        if t0 + n >= 2:
                            dve.wait_ge(S("hid_lo"), t0 + n - 1)
                        dve.tensor_tensor(FV[n % 2], acc(n)[:, 512:1024], FS[n % 2], ALU.mult).then_inc(S("value"), 1)
                        if n:
                            low(n - 1)
                    low(tiles - 1)
                    for o in range(KT):
                        dve.wait_ge(sem("chunk_done"), first + tiles + (tiles * o + tiles - 1) // 16 + 1)
                        if part == 1:
                            dve.wait_ge(S("down"), o + 1)
                        dve.tensor_tensor(XT[:, o, :], XT[:, o, :], down(o), ALU.add).then_inc(S("down"), 1)

            phases.append(dict(tensor=tensor, scalar=scalar, vector=vector, gpsimd=gpsimd))

        norm(XT, T, None, lambda k: v("ffn_norm", k, 1), halves=HHL)
        swiglu(0, CH_FF0)

        norm(XT, T, HT, lambda k: v("attn_norm", 8 + k, 1))
        LQ = view(R, GH, T)
        LK = view(R + 2048, GH, T)
        LV = view(R + 4096, TT, D)
        OG = view(R + 8192, KT, T)
        LA = view(R + 12288, 2, TT, 512)
        LTMP = view(R + 22048, 4096)
        ZT = view(R + 26144, T)
        WG = view(R + 26656, 512)

        def lin_load_gpsimd(pool):
            pool.memset(ZT[0:64, :], 1.0)
            for d in range(2):
                pool.dma_start(WG[32 * d:32 * d + 17, :], w_gate_fb[d]).then_inc(sem("lin_loaded"), 16)
            pool.wait_ge(sem("lin_loaded"), 32)

        phases[-1]["gpsimd"] = lin_load_gpsimd

        def lin_tensor(pe):
            for d in range(2):
                for k in range(KT):
                    mm = pe.matmul(pf[32 * d:32 * d + 16, 3072:3584], wdt[:, k, 16 * d:16 * d + 16], HT[:, k, :],
                                   start=(k == 0), stop=(k == KT - 1))
            mm.then_inc(sem("lin_z"), 1)
            pe.wait_ge(sem("lin_zt"), 1)
            for i in range(8):
                d, t = divmod(i, TT)
                if i >= 2:
                    pe.wait_ge(sem("lin_raw"), i - 1)
                pe.matmul(bank(6 + i % 2), ZT[32 * d:32 * d + 17, t * P:t * P + P], WG[32 * d:32 * d + 17, :],
                          start=True, stop=True).then_inc(sem("lin_gate"), 1)
            for n in range(8):
                c = CH_GLA + n
                arrived(pe, c)
                if n >= 2:
                    pe.wait_ge(sem("lin_evac"), n - 1)
                if n < 4:
                    for j in range(2):
                        for k in range(KT):
                            mm = pe.matmul(acc2(n)[:, j * 512:j * 512 + 512], wtile(c, k, j), HT[:, k, :],
                                           start=(k == 0), stop=(k == KT - 1))
                else:
                    for t in range(TT):
                        for k in range(KT):
                            mm = pe.matmul(acc2(n)[:, t * 256:t * 256 + 256], HT[:, k, t * P:t * P + P],
                                           wtile(c, k, 0, 256), start=(k == 0), stop=(k == KT - 1))
                chunk_done(mm)

        def lin_scalar(act):
            act.wait_ge(sem("lin_z"), 1)
            for d in range(2):
                ins = act.activation(ZT[32 * d:32 * d + 16, :], pf[32 * d:32 * d + 16, 3072:3584], ACT.Copy)
            ins.then_inc(sem("lin_zt"), 1)
            for i in range(8):
                act.wait_ge(sem("lin_gate"), i + 1)
                act.activation(LA[:, i // TT, i % TT, :], bank(6 + i % 2), ACT.Copy).then_inc(sem("lin_raw"), 1)
            act.wait_ge(sem("lin_abs"), 1)
            act.activation(LTMP, LTMP, ACT.Exp).then_inc(sem("lin_exp"), 1)
            act.wait_ge(sem("lin_exp"), 1)
            act.activation(LTMP, LTMP, ACT.Ln, bias=1.0).then_inc(sem("lin_ln"), 1)
            for n in range(8):
                act.wait_ge(sem("chunk_done"), CH_GLA + n + 1)
                if n < 4:
                    dst = (LQ, LK)[n // 2][:, 2 * (n % 2):2 * (n % 2) + 2, :]
                    act.activation(dst, split(acc2(n), 2, T), ACT.Copy).then_inc(sem("lin_evac"), 1)
                else:
                    act.activation(LV[:, :, (n - 4) * 256:(n - 3) * 256], split(acc2(n), TT, 256),
                                   ACT.Copy).then_inc(sem("lin_evac"), 1)

        def lin_vector(dve):
            la = LA.rearrange("p a b c -> p (a b c)")
            dve.wait_ge(sem("lin_raw"), 8)
            dve.scalar_tensor_tensor(LTMP, la, -1.0, la, ALU.mult, ALU.min).then_inc(sem("lin_abs"), 1)
            dve.wait_ge(sem("lin_ln"), 1)
            dve.scalar_tensor_tensor(la, la, 0.0, LTMP, ALU.min, ALU.subtract)

        phases.append(dict(tensor=lin_tensor, scalar=lin_scalar, vector=lin_vector))

        NC = T // GC
        QTL = [view(R + 16384 + 512 * d, T) for d in range(2)]
        KTL = [view(R + 17408 + 512 * d, T) for d in range(2)]
        KEL = [view(R + 18432 + 512 * d, T) for d in range(2)]
        KET = [view(R + 19456 + 512 * d, TT, P) for d in range(2)]
        AM = [view(R + 20480 + 256 * d, TT, GC) for d in range(2)]
        BLS = view(R + 20992, 2, NC)
        DEC = view(R + 21008, 2, NC)
        EBL = [view(R + 21024 + 512 * d, T) for d in range(2)]
        SIN = [view(R + 22048 + 2048 * d, NC, 256) for d in range(2)]
        ORDER = (list(range(NC)), list(range(NC))[::-1])
        KVS = [(d, i) for i in range(NC - 1) for d in range(2)]

        def gla_tensor(pe):
            for h in range(GH):
                for d in range(2):
                    if h >= 1 and d == 0:
                        pe.wait_ge(sem("gla_o"), h)
                    for t in range(TT):
                        mm = pe.matmul(bank(d, P, t * P), LA[:, d, t, h * P:h * P + P],
                                       C[("gtriu", "gtril")[d]], start=True, stop=True)
                    mm.then_inc(sem("gla_b"), 1)
                for d in range(2):
                    i = 2 * h + d
                    pe.wait_ge(sem("gla_q"), i + 1)
                    pe.wait_ge(sem("gla_k"), i + 1)
                    for c in range(NC):
                        o = pf[64 * (c % 2):64 * (c % 2) + 64, (2 + d) * 512 + (c // 2) * GC:(2 + d) * 512 + (c // 2) * GC + GC]
                        mm = pe.matmul(o, KTL[d][:, c * GC:c * GC + GC], QTL[d][:, c * GC:c * GC + GC],
                                       start=True, stop=True)
                    mm.then_inc(sem("gla_attn"), 1)
                    pe.wait_ge(sem("gla_kend"), i + 1)
                    for t in range(TT):
                        mm = pe.transpose(bank(4 + d, P, t * P), KEL[d][:, t * P:t * P + P], C["ident"])
                    mm.then_inc(sem("gla_kturn"), 1)
                pe.wait_ge(sem("gla_kturned"), 2 * h + 2)
                for x, (d, i) in enumerate(KVS):
                    n = len(KVS) * h + x
                    c = ORDER[d][i]
                    rows = slice(64 * (c % 2), 64 * (c % 2) + 64)
                    if n >= 2:
                        pe.wait_ge(sem("gla_state"), n - 1)
                    pe.matmul(bank(6 + x % 2, 256), KET[d][rows, c // 2, :], LV[rows, c // 2, h * 256:h * 256 + 256],
                              start=True, stop=True).then_inc(sem("gla_kv"), 1)
                pe.wait_ge(sem("gla_masked"), 2 * h + 2)
                pe.wait_ge(sem("gla_state"), len(KVS) * (h + 1))
                for e in range(2):
                    for c in range(NC):
                        rows = slice(64 * (c % 2), 64 * (c % 2) + 64)
                        o = bank(e + 2 * (c % 2), GC, (c // 2) * GC)
                        steps = []
                        for d in range(2):
                            steps.append((LV[rows, c // 2, h * 256 + e * P:h * 256 + e * P + P], AM[d][rows, c // 2, :]))
                            if c != ORDER[d][0]:
                                steps.append((SIN[d][:, c, e * P:e * P + P], QTL[d][:, c * GC:c * GC + GC]))
                        for x, (lhs, rhs) in enumerate(steps):
                            mm = pe.matmul(o, lhs, rhs, start=(x == 0), stop=(x == len(steps) - 1))
                mm.then_inc(sem("gla_omm"), 1)

        def gla_vector(dve):
            for d in range(2):
                dve.memset(AM[d].rearrange("p a b -> p (a b)"), 0.0)
                ins = dve.memset(SIN[d][:, ORDER[d][0], :], 0.0)
            ins.then_inc(sem("gla_zeroed"), 1)
            dve.wait_ge(sem("gla_zeroed"), 1)
            for h in range(GH):
                for d in range(2):
                    i = 2 * h + d
                    last = bank(d)[:, 63:T:64] if d == 0 else bank(d)[:, 0:T:64]
                    dve.wait_ge(sem("gla_b"), i + 1)
                    if h >= 1:
                        dve.wait_ge(sem("gla_kturn"), i - 1)
                    dve.tensor_copy(BLS[:, d, :], last).then_inc(sem("gla_last"), 1)
                    dve.wait_ge(sem("gla_last"), i + 1)
                    dve.tensor_tensor(split(KEL[d], NC, GC), BLS[:, d, :].unsqueeze(2).to_broadcast([P, NC, GC]),
                                      split(bank(d), NC, GC), ALU.subtract).then_inc(sem("gla_diff"), 1)
                for d in range(2):
                    i = 2 * h + d
                    dve.wait_ge(sem("gla_eb"), i + 1)
                    dve.scalar_tensor_tensor(QTL[d], LQ[:, h, :], float(P) ** -0.5, EBL[d], ALU.mult,
                                             ALU.mult).then_inc(sem("gla_q"), 1)
                for d in range(2):
                    dve.wait_ge(sem("gla_attn"), 2 * h + d + 1)
                    dve.copy_predicated(AM[d], gmask[:, d:d + 1, :].to_broadcast([P, TT, GC]),
                                        split(bank(2 + d, 256), TT, GC)).then_inc(sem("gla_masked"), 1)
                for x, (d, i) in enumerate(KVS):
                    c, nxt = ORDER[d][i], ORDER[d][i + 1]
                    n = len(KVS) * h + x
                    dve.wait_ge(sem("gla_kv"), n + 1)
                    if i >= 1:
                        dve.wait_ge(sem("gla_state"), n - 1)
                    dve.scalar_tensor_tensor(SIN[d][:, nxt, :], SIN[d][:, c, :], DEC[:, d, c:c + 1],
                                             bank(6 + x % 2, 256), ALU.mult, ALU.add).then_inc(sem("gla_state"), 1)

        def gla_scalar(act):
            for h in range(GH):
                for d in range(2):
                    i = 2 * h + d
                    act.wait_ge(sem("gla_diff"), i + 1)
                    act.activation(KEL[d], KEL[d], ACT.Exp).then_inc(sem("gla_ekend"), 1)
                    act.activation(DEC[:, d, :], BLS[:, d, :], ACT.Exp)
                    if h >= 1:
                        act.wait_ge(sem("gla_attn"), i - 1)
                    act.activation(KTL[d], bank(d), ACT.Exp, scale=-1.0).then_inc(sem("gla_enb"), 1)
                    act.activation(EBL[d], bank(d), ACT.Exp).then_inc(sem("gla_eb"), 1)
                for d in range(2):
                    i = 2 * h + d
                    act.wait_ge(sem("gla_kturn"), i + 1)
                    act.activation(KET[d].rearrange("p a b -> p (a b)"), bank(4 + d), ACT.Copy).then_inc(sem("gla_kturned"), 1)
                act.wait_ge(sem("gla_omm"), h + 1)
                for odd in range(2):
                    dst = OG[:, 2 * h:2 * h + 2, :].rearrange("p a (c o t) -> p a c o t", o=2, t=GC)[:, :, :, odd, :]
                    src = split(pf[:, 1024 * odd:1024 * odd + 1024], 2, 512)[:, :, 0:T // 2]
                    ins = act.activation(dst, src.rearrange("p a (c t) -> p a c t", t=GC), ACT.Copy)
                ins.then_inc(sem("gla_o"), 1)

        def gla_gpsimd(pool):
            for h in range(GH):
                for d in range(2):
                    i = 2 * h + d
                    pool.wait_ge(sem("gla_ekend"), i + 1)
                    pool.tensor_tensor(KEL[d], KEL[d], LK[:, h, :], ALU.mult).then_inc(sem("gla_kend"), 1)
                    pool.wait_ge(sem("gla_enb"), i + 1)
                    pool.tensor_tensor(KTL[d], KTL[d], LK[:, h, :], ALU.mult).then_inc(sem("gla_k"), 1)

        phases.append(dict(tensor=gla_tensor, scalar=gla_scalar, vector=gla_vector, gpsimd=gla_gpsimd))

        LS = [view(R + 1024 * i, 2, T) for i in range(2)]
        LSQ = [view(R + 2048 + 1024 * i, 2, T) for i in range(2)]
        LR = [view(R + 4096 + 512 * i, T) for i in range(2)]

        def lgate_tensor(pe):
            for g in range(GH):
                c = CH_GLAR + g
                arrived(pe, c)
                if g >= 2:
                    pe.wait_ge(sem("lg_silu"), g - 1)
                for j in range(2):
                    for k in range(KT):
                        mm = pe.matmul(acc(g)[:, j * 512:j * 512 + 512], wtile(c, k, j), HT[:, k, :],
                                       start=(k == 0), stop=(k == KT - 1))
                chunk_done(mm)
                pe.wait_ge(sem("lg_sq"), g + 1)
                if g >= 2:
                    pe.wait_ge(sem("lg_ln"), g - 1)
                for j in range(2):
                    mm = pe.matmul(bank(6 + g % 2), C["ones"], LSQ[g % 2][:, j, :], start=(j == 0), stop=(j == 1))
                mm.then_inc(sem("lg_sums"), 1)

        def lgate_scalar(act):
            for g in range(GH):
                if g >= 2:
                    act.wait_ge(sem("lg_sums"), g - 1)
                    act.wait_ge(sem("lg_out"), g - 1)
                act.activation(LSQ[g % 2], OG[:, 2 * g:2 * g + 2, :], ACT.Square).then_inc(sem("lg_sq"), 1)
                act.wait_ge(sem("chunk_done"), CH_GLAR + g + 1)
                act.activation(LS[g % 2], split(acc(g)[:, 0:1024], 2, T), ACT.Silu).then_inc(sem("lg_silu"), 1)
                load_exp_ln(act)
                act.wait_ge(sem("lg_sums"), g + 1)
                act.activation(LR[g % 2], bank(6 + g % 2), ACT.Ln, scale=1.0 / 256, bias=epst[:, :]).then_inc(sem("lg_ln"), 1)
                act.wait_ge(sem("lg_ln"), g + 1)
                act.activation(LR[g % 2], LR[g % 2], ACT.Exp, scale=-0.5).then_inc(sem("lg_rstd"), 1)

        def lgate_vector(dve):
            link = Link(dve, "lg_link")
            for g in range(GH):
                y = OG[:, 2 * g:2 * g + 2, :]
                dve.wait_ge(sem("lg_rstd"), g + 1)
                for j in range(2):
                    ins = dve.scalar_tensor_tensor(y[:, j, :], y[:, j, :], v("b_out_norm", 2 * g + j, 1), LR[g % 2],
                                                   ALU.mult, ALU.mult)
                link(ins)
                dve.wait_ge(sem("lg_silu"), g + 1)
                dve.tensor_tensor(y, y, LS[g % 2], ALU.mult).then_inc(sem("lg_out"), 1)

        phases.append(dict(tensor=lgate_tensor, scalar=lgate_scalar, vector=lgate_vector))
        project_out("gla_proj", CH_GLAO, OG)
        norm(XT, T, None, lambda k: v("ffn_norm", 8 + k, 1), halves=HHL)
        swiglu(1, CH_FF1)

        def meet(eng, n):
            eng.drain().then_inc(sem("stage_ended"), 1)
            eng.wait_ge(sem("stage_ended"), 4 * (n + 1))

        def run(eng, name):
            for n, stage in enumerate(phases[:stop]):
                if name in stage:
                    stage[name](eng)
                meet(eng, n)
                if n == BLOCK1_STAGES - 1:
                    if name == "gpsimd":
                        for old in BLOCK1_SEMS:
                            eng.sem_clear(sem(old))
                        eng.drain().then_inc(sem("semaphores_cleared"), 1)
                    eng.wait_ge(sem("semaphores_cleared"), 1)

        block = ctx.enter_context(nc.Block())

        @block.sync
        def _(sp):
            ada_sync(sp)
            for c in range(CH_END if stop is None else LIMIT):
                if c == CH_SH + 3:
                    moe_sync(sp)
                last = c - NSLOT
                if last in SPLIT:
                    sp.wait_ge(sem("chunk_lo"), SPLIT.index(last) + 1)
                elif last >= 0:
                    sp.wait_ge(sem("chunk_done"), last + 1)
                sp.dma_start(ring[:, c % NSLOT, :], wstream[c]).then_inc(sem(f"slot{c % NSLOT}_full"), 16)
            if stop is None:
                sp.wait_ge(sem("stage_ended"), 4 * len(phases))
                sp.dma_start(out_t, XT).then_inc(sem("out"), 16)
                sp.wait_ge(sem("out"), 16)
            else:
                sp.wait_ge(sem("stage_ended"), 4 * len(phases[:stop]))
                sp.dma_start(dbg, arena[:, :]).then_inc(sem("out"), 16)
                sp.dma_start(out_t, arena[:, 0:4096].rearrange("p (k t) -> p k t", t=T)).then_inc(sem("out"), 16)
                sp.wait_ge(sem("out"), 32)

        @block.tensor
        def _(pe):
            run(pe, "tensor")

        @block.scalar
        def _(act):
            run(act, "scalar")

        @block.vector
        def _(dve):
            run(dve, "vector")

        @block.gpsimd
        def _(pool):
            run(pool, "gpsimd")


def program(nc, a, out_t, dbg=None, stop=None):
    xs = nc.dram_tensor("xs", (MAXBLK * P, D), F32, kind="Internal").ap()
    ys = nc.dram_tensor("ys", (MAXBLK * P, D), F32, kind="Internal").ap()
    two_blocks(nc, a["wstream"], a["x_t"], a["ctx_t"], a["vecs"], a["consts"], a["rope_t"], a["gmask_t"],
               a["dmask_t"], a["iota_t"], a["w_dt"], a["w_router"], a["we_gu"], a["we_down"], a["w_z"],
               a["w_gate_fb"], xs, ys, out_t, dbg, stop)


def _tables(np):
    i = np.arange(P)
    eye = np.eye(P)
    rot = np.zeros((P, P))
    for h in range(2):
        for j in range(32):
            rot[64 * h + 32 + j, 64 * h + j] = -1.0
            rot[64 * h + j, 64 * h + 32 + j] = 1.0
    pair = (i[:, None] // 64 == i[None, :] // 64) * 1.0
    triu = (i[:, None] <= i[None, :]) * 1.0
    mats = [eye, np.ones((P, P)), rot, pair, triu, triu.T, triu - eye, triu * pair / 16.0, triu.T * pair / 16.0]
    consts = np.stack(mats, axis=1).astype(np.float32)

    def cs(ang):
        ang = np.concatenate([ang, ang, ang, ang], axis=-1)
        return np.stack([np.cos(ang).T, np.sin(ang).T], axis=1).astype(np.float32)

    t = np.arange(T, dtype=np.float32)
    inv1 = np.float32(10000.0) ** (-np.arange(0, 32, 2, dtype=np.float32) / np.float32(32))
    ang1 = np.concatenate([np.floor(t / 64)[:, None] * inv1, (t % 64)[:, None] * inv1], axis=-1)
    inv2 = np.float32(10000.0) ** (-np.arange(32, dtype=np.float32) / np.float32(32))
    ang2 = t[:, None] * inv2[None, :]
    s, q = i[:, None] % 64, np.arange(64)[None, :]
    gmask = np.stack([s <= q, s > q], axis=1).astype(np.uint32)
    big = np.float32(-1e30)
    m0 = [np.where(np.abs(np.arange(T)[None, :] - (4 * i + r)[:, None]) <= 64, 0, big) for r in range(4)]
    m1 = np.where(np.abs(i[None, :] - i[:, None]) <= 64, 0, big)
    m2 = np.where((i[None, :] - i[:, None]) % 4 == 0, 0, big)
    dmask = np.concatenate(m0 + [m1, m2, eye], axis=1)
    return consts, cs(ang1), cs(ang2), gmask, dmask


def kernel(**inputs):
    import ml_dtypes
    import numpy as np
    import concourse.bacc as bacc
    from concourse.bass_utils import run_bass_kernel_spmd as launch

    g = {n: np.asarray(a) for n, a in inputs.items()}

    def feat(a):
        return np.ascontiguousarray(a.reshape(a.shape[0], -1, P).transpose(2, 1, 0))

    def vecf(a):
        return a.reshape(-1, P).T

    def chunks(w):
        return w.reshape(KT, P, -1, 256).transpose(2, 1, 0, 3).reshape(-1, P, CHW)

    def ffn(gu, down):
        gu, out, t0 = chunks(gate_up(gu)), [], 0
        for n in FF_PARTS:
            b = down[t0 * P:(t0 + n) * P].reshape(n, P, KT, P).transpose(2, 0, 1, 3).reshape(-1, 16, P, P)
            out += [gu[t0:t0 + n], b.transpose(0, 2, 1, 3).reshape(-1, P, CHW)]
            t0 += n
        return np.concatenate(out)

    def gate_up(w):
        return w.reshape(D, 2, -1, P).transpose(0, 2, 1, 3).reshape(D, -1)

    w_in = g["w_in"][0]
    wg, wa, wsd = w_in[:, 6176:8224], g["w_branch_attn"][0], g["w_branch_ssd"][0]
    merge = np.stack([w.reshape(D, 4, 256) for w in (wg[:, :D], wa, wg[:, D:], wsd)], axis=2).reshape(D, -1)
    a_in = g["a_w_in_2"][0].reshape(D, 9, 4, 256).transpose(0, 2, 1, 3).reshape(D, -1)
    b_in = g["b_w_in_2"][0]
    w_ada = chunks(g["w_ada"][0])
    stream = [w_ada[:8], chunks(w_in[:, :3072]), w_ada[8:], chunks(w_in[:, 4096:6144]), chunks(w_in[:, 3072:4096]),
              chunks(merge), chunks(g["w_out"][0]), chunks(g["w_sh_gate"][0]), chunks(g["w_sh_up"][0]),
              g["w_sh_down"][0].reshape(2, P, D).transpose(1, 0, 2).reshape(1, P, CHW),
              chunks(a_in), chunks(g["a_w_out_2"][0]),
              ffn(g["ffn_w_gate_up_2"][0], g["ffn_w_down_2"][0]),
              chunks(b_in[:, 0:2048]), chunks(b_in[:, 2048:3072]), chunks(g["b_w_out_2"][0]),
              ffn(g["ffn_w_gate_up_2"][1], g["ffn_w_down_2"][1])]
    wstream = np.concatenate(stream, axis=0)
    assert wstream.shape[0] == CH_END

    def row(a):
        return np.broadcast_to(a.reshape(1, -1), (P, a.size))

    cols = {
        "cc": feat(np.stack([g["c"][0], g["c_ctx"]])).reshape(P, 16), "b_ada": vecf(g["b_ada"][0]),
        "g_pre_mix": vecf(g["g_pre_mix"][0]), "g_post_mix": vecf(g["g_post_mix"][0]),
        "g_pre_ffn": vecf(g["g_pre_ffn"][0]), "g_post_ffn": vecf(g["g_post_ffn"][0]),
        "g_subln": g["g_attn_subln"][0][:, None], "conv_w": vecf(g["conv_w"][0].reshape(-1)),
        "conv_b": vecf(g["conv_b"][0]), "d_skip": vecf(np.repeat(g["d_skip"][0], 64)),
        "g_ssd": vecf(g["g_ssd_norm"][0]), "attn_norm": vecf(g["attn_norm_2"].reshape(-1)),
        "ffn_norm": vecf(g["ffn_norm_2"].reshape(-1)), "a_q_norm": np.tile(g["a_q_norm_2"][0], (1, 2)).T,
        "a_k_norm": np.tile(g["a_k_norm_2"][0], (1, 2)).T, "b_out_norm": vecf(g["b_out_norm_2"][0].reshape(-1)),
        "lam": row(np.concatenate([g["lam_q1"][0], g["lam_k1"][0], g["lam_q2"][0], g["lam_k2"][0]])),
        "dt_bias": row(g["dt_bias"][0]), "a_log": row(g["a_log"][0]), "router_bias": row(g["router_bias"][0]),
    }
    vecs = np.concatenate([cols[n] for n in VEC], axis=1).astype(np.float32)
    consts, rope1, rope2, gmask, dmask = _tables(np)
    w_gate_fb = np.stack([np.concatenate([g["b_w_gate_f_2"][0], g["b_gate_bias_f_2"]]),
                          np.concatenate([g["b_w_gate_b_2"][0], g["b_gate_bias_b_2"]])])
    arrays = {
        "wstream": wstream, "x_t": feat(g["x"][0]), "ctx_t": feat(g["ctx"][0]), "vecs": vecs, "consts": consts,
        "rope_t": np.stack([rope1, rope2]), "gmask_t": gmask, "dmask_t": dmask.astype(ml_dtypes.bfloat16),
        "iota_t": np.ascontiguousarray(row(np.concatenate([np.tril(np.ones((8, 8)), -1).reshape(-1), np.arange(MAXBLK)])
                                          .astype(np.float32))),
        "w_dt": np.ascontiguousarray(w_in[:, 6144:6176].reshape(KT, P, 32).transpose(1, 0, 2)),
        "w_router": np.ascontiguousarray(g["w_router"][0].reshape(KT, P, E_N).transpose(1, 0, 2)),
        "we_gu": np.ascontiguousarray(np.concatenate([g["w_e_gate"][0], g["w_e_up"][0]], axis=-1)
                                      .reshape(E_N, KT, P, 512).transpose(0, 2, 1, 3)).reshape(E_N, P, KT * 512),
        "we_down": np.ascontiguousarray(g["w_e_down"][0].reshape(E_N, 2, P, D).transpose(0, 2, 1, 3)).reshape(E_N, P, 2 * D),
        "w_z": np.ascontiguousarray(b_in[:, 3072:3104].reshape(KT, P, 32).transpose(1, 0, 2)),
        "w_gate_fb": w_gate_fb,
    }
    nc = bacc.Bacc("TRN2", target_bir_lowering=False, num_devices=1)
    aps = {n: nc.dram_tensor(n, a.shape, mybir.dt.from_np(a.dtype), kind="ExternalInput").ap()
           for n, a in arrays.items()}
    out_t = nc.dram_tensor("out_t", (P, KT, T), F32, kind="ExternalOutput").ap()
    program(nc, aps, out_t)
    r = launch(nc, [arrays], core_ids=[0])
    got = r.results[0]["out_t"]
    return np.ascontiguousarray(got.transpose(2, 1, 0).reshape(1, T, D))
```

```python
from contextlib import ExitStack

import concourse.bass as bass
from concourse import mybir
from concourse.alu_op_type import AluOpType as ALU

ACT = mybir.ActivationFunctionType
AX = mybir.AxisListType
F32 = mybir.dt.float32
F32R = mybir.dt.float32r
BF16 = mybir.dt.bfloat16
I32 = mybir.dt.int32
U32 = mybir.dt.uint32

P = 128
D = 1024
KT = D // P
T = 512
TC = 256
TA = T + TC
TT = T // P
AT = TA // P
EPS = 1e-6
H1 = 8
SSD_H, SSD_G = 16, 4
E_N, E_F = 64, 256
MAXBLK = T * 8 // P + E_N
FF_T = 2816 // P
FF_PARTS = (12, FF_T - 12)
GH = 4
GC = 64
LAM_INIT = 0.8 - 0.6
NSLOT = 4
ARENA = 40960
CHW = 2048

CH_ADA = 0
CH_QKV = CH_ADA + 2 * D // 256
CH_MOD = CH_QKV + 12
CH_XBC = CH_MOD + 4 * D // 256
CH_Z = CH_XBC + 8
CH_MERGE = CH_Z + 4
CH_OUT = CH_MERGE + 16
CH_SH = CH_OUT + 4
CH_DIL = CH_SH + 3
CH_DILO = CH_DIL + 36
CH_FF0 = CH_DILO + 4
CH_GLA = CH_FF0 + 33
CH_GLAR = CH_GLA + 8
CH_GLAO = CH_GLAR + 4
CH_FF1 = CH_GLAO + 4
CH_END = CH_FF1 + 33

RUNS = {CH_QKV: 12, CH_XBC: 8, CH_MERGE: 20, CH_DIL: 36, CH_DILO: 4, CH_FF0: 33, CH_GLA: 8, CH_GLAR: 4, CH_GLAO: 4,
        CH_FF1: 33}
SPLIT = [c for first, n in RUNS.items() for c in range(first, first + n)]
LO_APART = (CH_FF0, CH_FF1)

VEC = {}


def _cols():
    at = 0
    for name, n in [("cc", 16), ("b_ada", 48), ("g_pre_mix", 8), ("g_post_mix", 8), ("g_pre_ffn", 8),
                    ("g_post_ffn", 8), ("g_subln", 1), ("conv_w", 48), ("conv_b", 16), ("d_skip", 8),
                    ("g_ssd", 8), ("attn_norm", 16), ("ffn_norm", 16), ("a_q_norm", 3), ("a_k_norm", 3),
                    ("b_out_norm", 8), ("lam", 256), ("dt_bias", 32), ("a_log", 32), ("router_bias", 64)]:
        VEC[name] = (at, n)
        at += n
    return at


NVEC = _cols()
CONSTS = ["ident", "ones", "rot", "pair", "triu", "tril", "triu_strict", "gtriu", "gtril"]


BLOCK1_SEMS = (
    "qkv_hi", "qkv_lo", "xbc_hi", "xbc_lo", "source_hi", "source_lo",
    "mod", "mod_turned", "ada_rows", "ada_turned", "ada_silu", "lam_exp", "lam_dots", "da_bias", "da_diff", "da_exp", "da_head", "da_ln", "da_max", "da_norm", "da_recip", "da_rstd",
    "da_scores", "da_sq", "da_ss", "da_turn", "da_turned", "da_values", "dt_abs", "dt_diff", "dt_ln",
    "dt_raw", "dt_sums", "dta", "qk_cos", "qk_out", "qk_raw", "qk_rot", "qk_sin", "ssd_btok", "ssd_bturn",
    "ssd_cb", "ssd_cbmm", "ssd_ce", "ssd_decay", "ssd_decayed", "ssd_erow", "ssd_exp", "ssd_rows", "ssd_seg",
    "ssd_state", "ssd_statemm", "ssd_sub", "ssd_tridta", "ssd_xdt", "ssd_xturn", "ssd_xw", "ssd_y", "ssd_ymm",
    "xbc_mid", "xbc_silu", "xbc_taps", "z_gated", "z_ln",
)
BLOCK2_SEMS = (
    "dil_proj", "dil_proj_hi", "dil_proj_lo", "gla_proj", "gla_proj_hi", "gla_proj_lo",
    "dil_bias", "dil_cos", "dil_evac", "dil_exp", "dil_half", "dil_ln", "dil_max", "dil_o", "dil_out", "dil_prob",
    "dil_pv", "dil_qn", "dil_recip", "dil_rot", "dil_rstd", "dil_scores", "dil_sin", "dil_ss", "dil_turn",
    "dil_turned", "gla_attn", "gla_b", "gla_diff", "gla_eb", "gla_ekend", "gla_enb", "gla_k", "gla_kend",
    "gla_kturn", "gla_kturned", "gla_kv", "gla_last", "gla_masked", "gla_o", "gla_omm", "gla_q", "gla_state", "gla_summed",
    "gla_zeroed", "lg_ln", "lg_out", "lg_rstd", "lg_silu", "lg_sq", "lg_sums", "lin_abs", "lin_evac",
    "lin_exp", "lin_gate", "lin_ln", "lin_raw", "lin_z", "lin_zt",
)


def two_blocks(nc, wstream, x_t, ctx_t, vecs, consts, rope_t, gmask_t, dmask_t, iota_t, w_dt, w_router,
               we_gu, we_down, w_z, w_gate_fb, xs, ys, x_saved, out_t, dbg, stop):
    ctx = ExitStack()
    with ctx:
        def sb(name, shape, dt=F32):
            return ctx.enter_context(nc.sbuf_tensor(name, shape, dt))

        made = {}

        def sem(name):
            if name in BLOCK2_SEMS:
                name = BLOCK1_SEMS[BLOCK2_SEMS.index(name)]
            if name not in made:
                made[name] = ctx.enter_context(nc.semaphore(name))
            return made[name]

        ring_at = (nc.sbuf_base + 31) // 32 * 32
        ring = sb("ring", [P, NSLOT, CHW])
        ring_r = [nc.alloc_sbuf_tensor_at(f"ring_r{i}", [P, CHW], F32R, offset=ring_at + 4 * CHW * i)
                  for i in range(NSLOT)]
        arena_at = (nc.sbuf_base + 31) // 32 * 32
        arena = sb("arena", [P, ARENA])
        arena_r = [nc.alloc_sbuf_tensor_at(f"arena_r{i}", [P, CHW], F32R, offset=arena_at + 4 * CHW * i)
                   for i in range(ARENA // CHW)]
        vec = sb("vec", [P, NVEC])
        cst = sb("cst", [P, len(CONSTS), P])
        rope = sb("rope", [P, 2, T])
        gmask = sb("gmask", [P, 2, 64], U32)
        identb = sb("identb", [P, P], BF16)
        wdt = sb("wdt", [P, KT, 32])
        wrt = sb("wrt", [P, KT, E_N])
        mod = sb("mod", [P, 48, 2])
        cs = sb("cs", [P, KT, 2])
        gain = sb("gain", [P, 40])
        small = sb("small", [P, 64])
        epst = sb("epst", [P, 1])
        ps = ctx.enter_context(nc.psum_tensor("ps", [P, 8, 512], F32))
        pf = ps[:, :, :].rearrange("p b n -> p (b n)")

        def bank(b, n=512, off=0):
            return pf[:, b * 512 + off:b * 512 + off + n]

        def view(at, *dims):
            n = 1
            for d in dims:
                n *= d
            ap = arena[:, at:at + n]
            if len(dims) == 2:
                return ap.rearrange("p (a b) -> p a b", b=dims[1])
            if len(dims) == 3:
                return ap.rearrange("p (a b c) -> p a b c", b=dims[1], c=dims[2])
            return ap

        def rounded(at, n):
            assert at % CHW + n <= CHW
            return arena_r[at // CHW][:, at % CHW:at % CHW + n]

        def rounded_rows(at, rows):
            return [rounded(at + T * i, T) for i in range(rows)]

        def split(ap, *dims):
            if len(dims) == 2:
                return ap.rearrange("p (a b) -> p a b", b=dims[1])
            return ap.rearrange("p (a b c) -> p a b c", b=dims[1], c=dims[2])

        def v(name, a=0, n=None):
            at, m = VEC[name]
            return vec[:, at + a:at + a + (m if n is None else n)]

        C = {name: cst[:, i, :] for i, name in enumerate(CONSTS)}
        XT = view(0, KT, T)
        HT = view(4096, KT, T)
        R = 8192
        WHL = R
        HI_AT = {CH_QKV: (R + 26624, R + 28672), CH_XBC: (R + 24576, R + 26624), CH_MERGE: (R, R + 30720), CH_DIL: (0, CHW),
                 CH_DILO: (R + 4096, R + 6144), CH_GLA: (R + 8192, R + 10240), CH_GLAR: (R + 12288, R + 14336),
                 CH_GLAO: (R, R + 2048)}

        A1, A2, G1, G2 = 0, 16, 24, 32

        phases = []

        class Link:

            def __init__(self, eng, name):
                self.eng, self.sem, self.n = eng, sem(name), 0

            def __call__(self, ins):
                ins.then_inc(self.sem, 1)
                self.n += 1
                self.eng.wait_ge(self.sem, self.n)

        def arrived(pe, c):
            pe.wait_ge(sem(f"slot{c % NSLOT}_full"), 16 * (c // NSLOT + 1))

        def wtile(c, k, j, n=P):
            return ring[:, c % NSLOT, k * 256 + j * P:k * 256 + j * P + n]

        def chunk_done(ins):
            ins.then_inc(sem("chunk_done"), 1)

        def load_exp_ln(act):
            act.preload_act_table_set("natural_log_exp_and_others")

        def run_of(c):
            return max(first for first in RUNS if first <= c)

        def whalf(c, part):
            first = run_of(c)
            if first in LO_APART:
                return rounded(WHL + (c - first) % 2 * 2 * CHW + part * CHW, CHW)
            return ring_r[c % NSLOT][:, :] if part else rounded(HI_AT[first][(c - first) % 2], CHW)

        def chunk_hi(act, c):
            arrived(act, c)
            if c - 2 >= run_of(c):
                act.wait_ge(sem("chunk_done"), c - 1)
            act.activation(whalf(c, 0), ring[:, c % NSLOT, :], ACT.Copy).then_inc(sem("chunk_hi"), 1)

        def chunk_lo(pool, c):
            pool.wait_ge(sem("chunk_hi"), SPLIT.index(c) + 1)
            pool.tensor_tensor(whalf(c, 1), ring[:, c % NSLOT, :], whalf(c, 0).bitcast(F32),
                               ALU.subtract).then_inc(sem("chunk_lo"), 1)

        def halves_ready(pe, c):
            pe.wait_ge(sem("chunk_lo"), SPLIT.index(c) + 1)

        def product(pe, out, c, at, rhs, start, stop, n=P):
            hi, lo = (whalf(c, part)[:, at:at + n] for part in range(2))
            pe.matmul(out, hi, rhs[0], start=start, stop=False)
            pe.matmul(out, hi, rhs[1], start=False, stop=False)
            return pe.matmul(out, lo, rhs[0], start=False, stop=stop)

        def product3(pe, out, a, b, start, stop):
            pe.matmul(out, a[0], b[0], start=start, stop=False)
            pe.matmul(out, a[0], b[1], start=False, stop=False)
            return pe.matmul(out, a[1], b[0], start=False, stop=stop)

        def weight(c, at, n):
            return [whalf(c, part)[:, at:at + n] for part in range(2)]

        class Halved:

            def __init__(self, name, ht_hi, hc_hi):
                self.name = name
                self.src = [HT[:, k, :] for k in range(KT)] + [view(R, KT, TC)[:, k, :] for k in range(KT)]
                self.hi = rounded_rows(ht_hi, KT) + [rounded(hc_hi + TC * k, TC) for k in range(KT)]
                self.lo = rounded_rows(4096, KT) + [rounded(R + TC * k, TC) for k in range(KT)]

            def high(self, act, i):
                act.activation(self.hi[i], self.src[i], ACT.Copy).then_inc(sem(self.name + "_hi"), 1)

            def low(self, dve, i):
                dve.wait_ge(sem(self.name + "_hi"), i + 1)
                dve.tensor_tensor(self.lo[i], self.src[i], self.hi[i].bitcast(F32),
                                  ALU.subtract).then_inc(sem(self.name + "_lo"), 1)

            def ready(self, pe, i):
                pe.wait_ge(sem(self.name + "_lo"), i + 1)

            def pair(self, i, tokens=slice(None)):
                return self.hi[i][:, tokens], self.lo[i][:, tokens]

            def tile(self, k, t):
                return self.pair(8 + k, slice(t * P, t * P + P)) if t < 2 else self.pair(k, slice((t - 2) * P, (t - 1) * P))

            def rebuild(self, eng, i):
                return eng.tensor_tensor(self.src[i], self.hi[i].bitcast(F32), self.lo[i].bitcast(F32), ALU.add)

        NLOAD = 9

        def ada_sync(sp):
            for dst, src in ((vec[:, :], vecs), (cst[:, :, :], consts), (XT, x_t), (view(R, KT, TC), ctx_t),
                             (rope[:, :, :], rope_t[0]), (gmask[:, :, :], gmask_t),
                             (identb[:, :], dmask_t[:, 2304:2432]), (wdt[:, :, :], w_dt),
                             (wrt[:, :, :], w_router)):
                sp.dma_start(dst, src).then_inc(sem("loaded"), 16)

        def ada_scalar(act):
            act.wait_ge(sem("loaded"), 16 * NLOAD)
            act.activation(cs[:, :, :], split(v("cc"), KT, 2), ACT.Silu).then_inc(sem("ada_silu"), 1)
            act.wait_ge(sem("lam_dots"), 1)
            act.activation(small[:, 2:4], small[:, 0:2], ACT.Exp).then_inc(sem("lam_exp"), 1)
            act.wait_ge(sem("chunk_done"), CH_ADA + 8)
            act.activation(ADA_OUT, ADA_ROWS, ACT.Copy).then_inc(sem("ada_rows"), 1)

        ADA_ROWS, ADA_OUT = pf[0:2, 0:2 * D], HT.rearrange("p a b -> p (a b)")[0:2, 0:2 * D]

        def ada_tensor(pe):
            pe.wait_ge(sem("ada_silu"), 1)
            for n in range(8):
                c = CH_ADA + n
                arrived(pe, c)
                for k in range(KT):
                    mm = pe.matmul(ADA_ROWS[:, n * 256:n * 256 + 256], cs[:, k, :], wtile(c, k, 0, 256),
                                   start=(k == 0), stop=(k == KT - 1))
                chunk_done(mm)
            pe.wait_ge(sem("ada_rows"), 1)
            for m in range(16):
                mm = pe.matmul(bank(7, 2, 2 * m), ADA_OUT[:, m * P:m * P + P], C["ident"][0:2, 0:2],
                               start=True, stop=True)
            mm.then_inc(sem("ada_turned"), 1)

        def ada_vector(dve):
            link = Link(dve, "ada_link")
            dve.memset(epst[:, :], EPS)
            dve.wait_ge(sem("loaded"), 16 * NLOAD)
            lam = split(v("lam"), 4, 64)
            prod = split(view(R + 2048, 128), 2, 64)
            link(dve.tensor_tensor(prod, lam[:, 0:4:2, :], lam[:, 1:4:2, :], ALU.mult))
            dve.tensor_reduce(small[:, 0:2], prod, AX.X, ALU.add).then_inc(sem("lam_dots"), 1)
            dve.wait_ge(sem("lam_exp"), 1)
            link(dve.tensor_tensor(small[:, 4:5], small[:, 3:4], small[:, 2:3], ALU.subtract))
            link(dve.tensor_scalar(small[:, 5:6], small[:, 4:5], -LAM_INIT, None, ALU.add))
            link(dve.tensor_scalar(small[:, 6:7], v("g_subln"), 1.0 - LAM_INIT, None, ALU.mult))
            dve.wait_ge(sem("ada_turned"), 1)
            link(dve.tensor_tensor(mod[:, 0:16, :], split(bank(7, 32), 16, 2),
                                   v("b_ada", 0, 16).unsqueeze(2).to_broadcast([P, 16, 2]), ALU.add))
            for s in range(2):
                dve.scalar_tensor_tensor(gain[:, A1 + 8 * s:A1 + 8 * s + 8], mod[:, 8:16, s], 1.0, v("g_pre_mix"),
                                         ALU.add, ALU.mult)

        def mod_vector(dve):
            dve.wait_ge(sem("mod_turned"), 1)
            dve.tensor_tensor(mod[:, 16:48, :], split(bank(5, 64, 256), 32, 2),
                              v("b_ada", 16, 32).unsqueeze(2).to_broadcast([P, 32, 2]), ALU.add).then_inc(sem("mod"), 1)
            dve.wait_ge(sem("mod"), 1)
            dve.scalar_tensor_tensor(gain[:, A2:A2 + 8], mod[:, 32:40, 0], 1.0, v("g_pre_ffn"), ALU.add, ALU.mult)
            dve.tensor_tensor(gain[:, G1:G1 + 8], mod[:, 16:24, 0], v("g_post_mix"), ALU.mult)
            dve.tensor_tensor(gain[:, G2:G2 + 8], mod[:, 40:48, 0], v("g_post_ffn"), ALU.mult)

        phases.append(dict(scalar=ada_scalar, tensor=ada_tensor, vector=ada_vector))

        norms = [0]
        halved = [0]
        SQ = R + 32768 - 1024

        def norm(src, n, dst=None, scale=None, shift=None, residual=None, halves=None):
            m = norms[0]
            norms[0] += 1
            low_base = 8 * halved[0]
            halved[0] += halves is not None
            sq = [view(SQ + 512 * i, 512)[:, 0:n] for i in range(2)]
            tmp = [view(SQ - 1024 + 512 * i, 512)[:, 0:n] for i in range(2)]
            ss, rs = bank(6, n), bank(7, n)

            def scalar(act):
                load_exp_ln(act)
                for k in range(KT):
                    if k >= 2:
                        act.wait_ge(sem("norm_summed"), 8 * m + k - 1)
                    act.activation(sq[k % 2], src[:, k, :], ACT.Square).then_inc(sem("norm_sq"), 1)
                act.wait_ge(sem("norm_summed"), 8 * m + 8)
                act.activation(rs, ss, ACT.Ln, scale=1.0 / D, bias=epst[:, :]).then_inc(sem("norm_ln"), 1)
                act.wait_ge(sem("norm_ln"), m + 1)
                act.activation(rs, rs, ACT.Exp, scale=-0.5).then_inc(sem("norm_rstd"), 1)
                if halves is not None:
                    for k in range(KT):
                        act.wait_ge(sem("norm_scaled"), 8 * m + k + 1)
                        act.activation(halves[0][k], tmp[k % 2], ACT.Copy).then_inc(sem("norm_out"), 1)
                elif dst is not None:
                    for k in range(KT):
                        act.wait_ge(sem("norm_scaled"), 8 * m + k + 1)
                        if shift is None:
                            act.activation(dst[:, k, :], tmp[k % 2], ACT.Copy).then_inc(sem("norm_out"), 1)
                        else:
                            act.activation(dst[:, k, :], tmp[k % 2], ACT.Identity, scale=scale(k),
                                           bias=shift(k)).then_inc(sem("norm_out"), 1)
                else:
                    for k in range(KT):
                        act.sem_inc(sem("norm_out"), 1)

            def tensor(pe):
                for k in range(KT):
                    pe.wait_ge(sem("norm_sq"), 8 * m + k + 1)
                    pe.matmul(ss, C["ones"], sq[k % 2], start=(k == 0),
                              stop=(k == KT - 1)).then_inc(sem("norm_summed"), 1)

            def vector(dve):
                def low(k):
                    dve.wait_ge(sem("norm_out"), 8 * m + k + 1)
                    dve.tensor_tensor(halves[1][k], tmp[k % 2], halves[0][k].bitcast(F32),
                                      ALU.subtract).then_inc(sem("norm_lo"), 1)

                dve.wait_ge(sem("norm_rstd"), m + 1)
                if halves is not None:
                    for k in range(KT):
                        if k >= 2:
                            low(k - 2)
                            dve.wait_ge(sem("norm_lo"), low_base + k - 1)
                        dve.scalar_tensor_tensor(tmp[k % 2], src[:, k, :], scale(k), rs, ALU.mult,
                                                 ALU.mult).then_inc(sem("norm_scaled"), 1)
                    low(KT - 2)
                    low(KT - 1)
                    return
                for k in range(KT):
                    if dst is not None:
                        if k >= 2:
                            dve.wait_ge(sem("norm_out"), 8 * m + k - 1)
                        if shift is None:
                            dve.scalar_tensor_tensor(tmp[k % 2], src[:, k, :], scale(k), rs, ALU.mult,
                                                     ALU.mult).then_inc(sem("norm_scaled"), 1)
                        else:
                            dve.tensor_tensor(tmp[k % 2], src[:, k, :], rs, ALU.mult).then_inc(sem("norm_scaled"), 1)
                    else:
                        dve.scalar_tensor_tensor(tmp[k % 2], src[:, k, :], scale(k), rs, ALU.mult,
                                                 ALU.mult).then_inc(sem("norm_scaled"), 1)
                        dve.wait_ge(sem("norm_scaled"), 8 * m + k + 1)
                        dve.tensor_tensor(residual[:, k, :], residual[:, k, :], tmp[k % 2], ALU.add)

            phases.append(dict(scalar=scalar, tensor=tensor, vector=vector))

        HC = view(R, KT, TC)
        norm(XT, T, HT, lambda k: gain[:, A1 + k:A1 + k + 1], lambda k: mod[:, k, 0:1])
        norm(HC, TC, HC, lambda k: gain[:, A1 + 8 + k:A1 + 9 + k], lambda k: mod[:, k, 1:2])

        O1 = view(R + 2048, H1, T)
        Q = view(R + 6144, H1, T)
        K = view(R + 10240, H1, TA)
        V = view(R + 16384, AT, D)
        W0 = R + 22528

        def acc(n):
            return pf[:, (n % 2) * 1536:(n % 2) * 1536 + 1536]

        QX = Halved("qkv", R + 2048, R + 30720)

        def qkv_tensor(pe):
            def rotate(ch):
                pe.wait_ge(sem("qk_raw"), ch + 1)
                if ch >= 1:
                    pe.wait_ge(sem("qk_out"), ch)
                for j in range(2):
                    mm = pe.matmul(bank(6 + j), C["rot"], view(W0 + (ch % 2) * 1024 + j * 512, 512),
                                   start=True, stop=True)
                mm.then_inc(sem("qk_rot"), 1)

            for ch in range(12):
                c = CH_QKV + ch
                a = acc(ch)
                halves_ready(pe, c)
                if ch >= 2:
                    pe.wait_ge(sem("qk_raw"), ch - 1)
                if ch < 8:
                    for j in range(2):
                        for k in range(KT):
                            if ch == 0 and j == 0:
                                QX.ready(pe, k)
                            mm = product3(pe, a[:, j * 512:j * 512 + 512], weight(c, k * 256 + j * P, P), QX.pair(k),
                                          k == 0, k == KT - 1)
                        if ch >= 4:
                            for k in range(KT):
                                QX.ready(pe, 8 + k)
                                mm = product3(pe, a[:, 1024 + j * 256:1280 + j * 256], weight(c, k * 256 + j * P, P),
                                              QX.pair(8 + k), k == 0, k == KT - 1)
                else:
                    for t in range(AT):
                        for k in range(KT):
                            mm = product3(pe, a[:, t * 256:t * 256 + 256], QX.tile(k, t), weight(c, k * 256, 256),
                                          k == 0, k == KT - 1)
                chunk_done(mm)
                if 1 <= ch < 9:
                    rotate(ch - 1)

        def qkv_scalar(act):
            chunk_hi(act, CH_QKV)
            for k in range(KT):
                QX.high(act, k)
            chunk_hi(act, CH_QKV + 1)
            for k in range(KT, 2 * KT):
                QX.high(act, k)
            for ch in range(12):
                a = acc(ch)
                act.wait_ge(sem("chunk_done"), CH_QKV + ch + 1)
                if ch < 8:
                    if ch >= 2:
                        act.wait_ge(sem("qk_rot"), ch - 1)
                        act.wait_ge(sem("qk_cos"), ch - 1)
                    if ch >= 4:
                        act.activation(K[:, 2 * (ch - 4):2 * (ch - 4) + 2, 0:TC], split(a[:, 1024:1536], 2, 256),
                                       ACT.Copy)
                    act.activation(view(W0 + (ch % 2) * 1024, 1024), a[:, 0:1024], ACT.Copy).then_inc(sem("qk_raw"), 1)
                else:
                    act.activation(V[:, :, (ch - 8) * 256:(ch - 7) * 256], split(a, AT, 256),
                                   ACT.Copy).then_inc(sem("qk_raw"), 1)
                if ch + 2 < 12:
                    chunk_hi(act, CH_QKV + ch + 2)

        def qkv_gpsimd(pool):
            cos = rope[:, 0:1, :].to_broadcast([P, 2, T])
            chunk_lo(pool, CH_QKV)
            chunk_lo(pool, CH_QKV + 1)
            for ch in range(10):
                if ch < 8:
                    pool.wait_ge(sem("qk_raw"), ch + 1)
                    if ch >= 2:
                        pool.wait_ge(sem("qk_out"), ch - 1)
                    pool.tensor_tensor(view(W0 + 2048 + (ch % 2) * 1024, 2, 512), view(W0 + (ch % 2) * 1024, 2, 512),
                                       cos, ALU.mult).then_inc(sem("qk_cos"), 1)
                chunk_lo(pool, CH_QKV + ch + 2)
            pool.wait_ge(sem("chunk_done"), CH_QKV + 12)
            for k in range(KT):
                QX.rebuild(pool, 8 + k)

        def qkv_vector(dve):
            sin = rope[:, 1:2, :].to_broadcast([P, 2, T])
            rot = split(pf[:, 3072:4096], 2, 512)
            for i in range(2 * KT):
                QX.low(dve, i)
            for ch in range(8):
                dve.wait_ge(sem("qk_rot"), ch + 1)
                dve.tensor_tensor(rot, rot, sin, ALU.mult).then_inc(sem("qk_sin"), 1)
                dve.wait_ge(sem("qk_cos"), ch + 1)
                dve.wait_ge(sem("qk_sin"), ch + 1)
                dst = Q[:, 2 * ch:2 * ch + 2, :] if ch < 4 else K[:, 2 * (ch - 4):2 * (ch - 4) + 2, TC:TA]
                dve.tensor_tensor(dst, rot, view(W0 + 2048 + (ch % 2) * 1024, 2, 512),
                                  ALU.add).then_inc(sem("qk_out"), 1)
            dve.wait_ge(sem("chunk_done"), CH_QKV + 12)
            for k in range(KT):
                QX.rebuild(dve, k)

        phases.append(dict(tensor=qkv_tensor, scalar=qkv_scalar, gpsimd=qkv_gpsimd, vector=qkv_vector))

        NU = H1 * TT

        def prob(n, c):
            return view(W0 + ((n % 2) * 2 + c) * TA, TA)

        def wT(h):
            return view(W0 + 4 * TA + (h % 2) * AT * T, AT, T)

        MOD_ROW = pf[0:2, 5 * 512 + 384:6 * 512]
        MOD_OUT = v("lam", 0, P)[0:2, :]

        SC = small[:, 8:40]

        def da_tensor(pe):
            def scores(n):
                h, qt = divmod(n, TT)
                for c in range(2):
                    if n >= 1:
                        pe.wait_ge(sem("da_exp"), 2 * (n - 1) + c + 1)
                    q = Q[64 * c:64 * c + 64, h, qt * P:qt * P + P]
                    pe.matmul(bank(2 * c), q, K[64 * c:64 * c + 64, h, 0:512], start=True, stop=True)
                    pe.matmul(bank(2 * c + 1, 256), q, K[64 * c:64 * c + 64, h, 512:TA], start=True,
                              stop=True).then_inc(sem("da_scores"), 1)

            def mod_turn(n):
                return pe.matmul(bank(5, 2, 256 + 2 * n), MOD_OUT, C["ident"][0:2, 0:2], start=True, stop=True)

            def turn(n):
                if n >= 1:
                    pe.wait_ge(sem("da_turned"), n)
                    mod_turn(n - 1)
                c, j = CH_MOD + n // 2, n % 2
                if j == 0:
                    arrived(pe, c)
                for k in range(KT):
                    mm = pe.matmul(MOD_ROW, cs[:, k, :], wtile(c, k, j), start=(k == 0), stop=(k == KT - 1))
                if j == 1:
                    chunk_done(mm)
                pe.wait_ge(sem("da_diff"), n + 1)
                for t in range(AT):
                    mm = pe.transpose(bank(4, P, t * P), prob(n, 0)[:, t * P:t * P + P], C["ident"])
                mm.then_inc(sem("da_turn"), 1)

            def values(h):
                pe.wait_ge(sem("da_turned"), 4 * h + 4)
                if h >= 1:
                    pe.wait_ge(sem("da_head"), h)
                for t in range(AT):
                    mm = pe.matmul(bank(6), V[:, t, h * P:h * P + P], wT(h)[:, t, :], start=(t == 0),
                                   stop=(t == AT - 1))
                mm.then_inc(sem("da_values"), 1)

            def square_sum(h):
                pe.wait_ge(sem("da_sq"), h + 1)
                pe.matmul(bank(7), C["ones"], view(SQ, 512), start=True, stop=True).then_inc(sem("da_ss"), 1)

            scores(0)
            for n in range(NU):
                if n + 1 < NU:
                    scores(n + 1)
                turn(n)
                if n % 4 == 0 and n:
                    values(n // 4 - 1)
                if n % 4 == 1 and n > 4:
                    square_sum(n // 4 - 1)
            pe.wait_ge(sem("da_turned"), NU)
            mod_turn(NU - 1).then_inc(sem("mod_turned"), 1)
            values(H1 - 1)
            square_sum(H1 - 1)

        def da_vector(dve):
            def row_max(n):
                s = SC[:, 16 * (n % 2):16 * (n % 2) + 16]
                for c in range(2):
                    dve.wait_ge(sem("da_scores"), 2 * n + c + 1)
                    dve.reduce_max(s[:, c:c + 1], pf[:, 1024 * c:1024 * c + TA], AX.X).then_inc(sem("da_max"), 1)
                    dve.wait_ge(sem("da_max"), 2 * n + c + 1)
                    dve.tensor_scalar(s[:, 2 + c:3 + c], s[:, c:c + 1], -0.125, None,
                                      ALU.mult).then_inc(sem("da_bias"), 1)

            def diff(n):
                s = SC[:, 16 * (n % 2):16 * (n % 2) + 16]
                dve.wait_ge(sem("da_exp"), 2 * n + 2)
                dve.reciprocal(s[:, 6:8], s[:, 4:6]).then_inc(sem("da_recip"), 1)
                dve.wait_ge(sem("da_recip"), n + 1)
                dve.tensor_tensor(s[:, 8:9], s[:, 7:8], small[:, 5:6], ALU.mult)
                dve.tensor_scalar(prob(n, 0), prob(n, 0), s[:, 6:7], None, ALU.mult).then_inc(sem("da_norm"), 1)
                dve.wait_ge(sem("da_norm"), n + 1)
                dve.scalar_tensor_tensor(prob(n, 0), prob(n, 1), s[:, 8:9], prob(n, 0), ALU.mult,
                                         ALU.add).then_inc(sem("da_diff"), 1)

            def head(h):
                dve.wait_ge(sem("da_rstd"), h + 1)
                dve.scalar_tensor_tensor(O1[:, h, :], bank(6), small[:, 6:7], view(SQ + 512, 512), ALU.mult,
                                         ALU.mult).then_inc(sem("da_head"), 1)

            for n in range(NU + 1):
                if n >= 1:
                    diff(n - 1)
                if n < NU:
                    row_max(n)
                if n % 4 == 3 and n > 4:
                    head(n // 4 - 1)
            head(H1 - 1)
            mod_vector(dve)

        def da_scalar(act):
            def turned(n):
                h, qt = divmod(n, TT)
                act.wait_ge(sem("da_turn"), n + 1)
                if h >= 2 and qt == 0:
                    act.wait_ge(sem("da_values"), h - 1)
                act.activation(MOD_OUT, MOD_ROW, ACT.Copy)
                act.activation(wT(h)[:, :, qt * P:qt * P + P], split(bank(4, TA), AT, P),
                               ACT.Copy).then_inc(sem("da_turned"), 1)

            def head(h):
                act.wait_ge(sem("da_values"), h + 1)
                act.activation(view(SQ, 512), bank(6), ACT.Square).then_inc(sem("da_sq"), 1)

            def rstd(h):
                act.wait_ge(sem("da_ss"), h + 1)
                if h >= 1:
                    act.wait_ge(sem("da_head"), h)
                act.activation(view(SQ + 512, 512), bank(7), ACT.Ln, scale=1.0 / P,
                               bias=epst[:, :]).then_inc(sem("da_ln"), 1)
                act.wait_ge(sem("da_ln"), h + 1)
                act.activation(view(SQ + 512, 512), view(SQ + 512, 512), ACT.Exp, scale=-0.5).then_inc(sem("da_rstd"), 1)

            for n in range(NU):
                s = SC[:, 16 * (n % 2):16 * (n % 2) + 16]
                for c in range(2):
                    act.wait_ge(sem("da_bias"), 2 * n + c + 1)
                    if n >= 2:
                        act.wait_ge(sem("da_turn"), n - 1)
                    act.activation(prob(n, c), pf[:, 1024 * c:1024 * c + TA], ACT.Exp, scale=0.125,
                                   bias=s[:, 2 + c:3 + c], accum_out=s[:, 4 + c:5 + c]).then_inc(sem("da_exp"), 1)
                if n >= 1:
                    turned(n - 1)
                if n % 4 == 1 and n > 4:
                    head(n // 4 - 1)
                if n % 4 == 2 and n > 4:
                    rstd(n // 4 - 1)
            turned(NU - 1)
            head(H1 - 1)
            rstd(H1 - 1)

        NFILL = 8

        def fill(pool, buf, i):
            src = rope[:, :, :].rearrange("p a b -> p (a b)").unsqueeze(1).to_broadcast([P, NFILL, D])
            pool.dma_start(buf[i * NFILL * P:(i + 1) * NFILL * P, :].rearrange("(b p) d -> p b d", p=P),
                           src).then_inc(sem("filled"), 16)

        def fill_gpsimd(pool):
            for i in range(MAXBLK // NFILL):
                pool.wait_ge(sem("da_exp"), 4 * i + 1)
                fill(pool, xs, i)

        phases.append(dict(tensor=da_tensor, scalar=da_scalar, vector=da_vector, gpsimd=fill_gpsimd))

        XBC = view(R + 6144, 16, TA)
        Y = view(R + 18432, KT, T)
        SEGS = ((0, TC, 1024), (TC, T, 0))

        XX = Halved("xbc", R + 18432, R + 22528)

        def xbc_tensor(pe):
            for ch in range(8):
                c = CH_XBC + ch
                a = acc(ch)
                halves_ready(pe, c)
                if ch >= 2:
                    pe.wait_ge(sem("xbc_taps"), ch - 1)
                for j in range(2):
                    for k in range(KT):
                        XX.ready(pe, k)
                        product3(pe, a[:, j * 512:j * 512 + 512], weight(c, k * 256 + j * P, P), XX.pair(k),
                                 k == 0, k == KT - 1)
                    for k in range(KT):
                        XX.ready(pe, 8 + k)
                        mm = product3(pe, a[:, 1024 + j * 256:1280 + j * 256], weight(c, k * 256 + j * P, P),
                                      XX.pair(8 + k), k == 0, k == KT - 1)
                chunk_done(mm)
            for t in range(AT):
                for k in range(KT):
                    for i, half in enumerate(XX.tile(k, t)):
                        mm = pe.matmul(bank(6, 32, t * 32), half.bitcast(F32), wdt[:, k, :],
                                       start=(k == 0 and i == 0), stop=(k == KT - 1 and i == 1))
            mm.then_inc(sem("dt_raw"), 1)

        def part(a, j, base, n, lo, hi):
            at = base + j * n
            return a[:, at + lo:at + hi]

        def xbc_scalar(act):
            def silu(ch):
                act.wait_ge(sem("xbc_taps"), ch + 1)
                act.activation(XBC[:, 2 * ch:2 * ch + 2, :], XBC[:, 2 * ch:2 * ch + 2, :],
                               ACT.Silu).then_inc(sem("xbc_silu"), 1)

            chunk_hi(act, CH_XBC)
            for k in range(KT):
                XX.high(act, k)
            chunk_hi(act, CH_XBC + 1)
            for k in range(KT, 2 * KT):
                XX.high(act, k)
            for ch in range(8):
                act.wait_ge(sem("chunk_done"), CH_XBC + ch + 1)
                if ch + 2 < 8:
                    chunk_hi(act, CH_XBC + ch + 2)
                for j in range(2):
                    m = 2 * ch + j
                    for first, n, base in SEGS:
                        ins = act.activation(XBC[:, m, first:first + n], part(acc(ch), j, base, n, 0, n), ACT.Identity,
                                             scale=v("conv_w", 16 + m, 1), bias=v("conv_b", m, 1))
                ins.then_inc(sem("xbc_mid"), 1)
                if ch:
                    silu(ch - 1)
            silu(7)

        def xbc_vector(dve):
            link = Link(dve, "xbc_link")
            for i in range(2 * KT):
                XX.low(dve, i)
            for ch in range(8):
                dve.wait_ge(sem("xbc_mid"), ch + 1)
                for lo, tap in ((0, 0), (1, 32)):
                    for j in range(2):
                        m = 2 * ch + j
                        for first, n, base in SEGS:
                            o = XBC[:, m, first + 1 - lo:first + n - lo]
                            ins = dve.scalar_tensor_tensor(o, part(acc(ch), j, base, n, lo, n - 1 + lo),
                                                           v("conv_w", tap + m, 1), o, ALU.mult, ALU.add)
                    if lo == 0:
                        link(ins)
                    else:
                        ins.then_inc(sem("xbc_taps"), 1)

        assert MAXBLK // NFILL == 2 * AT

        S0 = R + 22528 + 7168
        DT = view(S0, 2, AT, SSD_H)
        DTA = view(S0 + 192, 2, AT, SSD_H)
        ACOL = view(S0 + 384, 2, AT, SSD_H)
        TOEND = view(S0 + 576, 2, AT, SSD_H)
        DECAY = view(S0 + 768, 2, AT, SSD_H)

        def flat(ap):
            return ap.rearrange("p a b c -> p (a b c)")

        def dt_vector(dve):
            link = Link(dve, "dt_link")
            tmp = view(S0 + 384, AT, 32)
            dve.wait_ge(sem("dt_raw"), 1)
            link(dve.tensor_tensor(tmp, split(bank(6, 192), AT, 32),
                                   v("dt_bias").unsqueeze(1).to_broadcast([P, AT, 32]), ALU.add))
            dve.scalar_tensor_tensor(view(S0 + 576, AT, 32), tmp, -1.0, tmp, ALU.mult, ALU.min).then_inc(sem("dt_abs"), 1)
            dve.wait_ge(sem("dt_ln"), 1)
            for d in range(2):
                ins = dve.scalar_tensor_tensor(DT[:, d], tmp[:, :, 16 * d:16 * d + 16], 0.0,
                                               view(S0 + 576, AT, 32)[:, :, 16 * d:16 * d + 16], ALU.max, ALU.add)
            link(ins)
            for d in range(2):
                ins = dve.scalar_tensor_tensor(
                    DTA[:, d], DT[:, d], -1.0,
                    v("a_log", 16 * d, 16).unsqueeze(1).to_broadcast([P, AT, 16]), ALU.mult, ALU.mult)
            ins.then_inc(sem("dta"), 1)
            dve.wait_ge(sem("dt_sums"), 1)
            link(dve.tensor_copy(flat(ACOL), bank(6, 192)))
            dve.tensor_tensor(flat(TOEND), bank(7, 192), flat(ACOL), ALU.subtract).then_inc(sem("dt_diff"), 1)
            for k in range(KT):
                ins = XX.rebuild(dve, k)
            link(ins)
            dve.wait_ge(sem("xbc_silu"), 4)
            for j in range(KT):
                dve.tensor_scalar(Y[:, j, :], XBC[:, j, TC:TA], v("d_skip", j, 1), None, ALU.mult)

        def dt_scalar(act):
            link = Link(act, "dt_act_link")
            load_exp_ln(act)
            link(act.activation(v("a_log"), v("a_log"), ACT.Exp))
            act.wait_ge(sem("dt_abs"), 1)
            link(act.activation(flat(TOEND), flat(TOEND), ACT.Exp))
            act.activation(flat(TOEND), flat(TOEND), ACT.Ln, bias=1.0).then_inc(sem("dt_ln"), 1)
            act.wait_ge(sem("dt_diff"), 1)
            act.activation(flat(TOEND), flat(TOEND), ACT.Exp)
            act.activation(flat(DECAY), bank(7, 192), ACT.Exp)

        def dt_tensor(pe):
            pe.wait_ge(sem("dta"), 1)
            pe.matmul(bank(6, 96), C["triu"], DTA[:, 0].rearrange("p a b -> p (a b)"), start=True, stop=True)
            pe.matmul(bank(6, 96, 96), C["tril"], DTA[:, 1].rearrange("p a b -> p (a b)"), start=True, stop=True)
            pe.matmul(bank(7, 192), C["ones"], flat(DTA), start=True, stop=True).then_inc(sem("dt_sums"), 1)

        def xbc_all_tensor(pe):
            xbc_tensor(pe)
            dt_tensor(pe)

        def xbc_all_scalar(act):
            xbc_scalar(act)
            dt_scalar(act)

        def xbc_all_vector(dve):
            xbc_vector(dve)
            dt_vector(dve)

        def xbc_gpsimd(pool):
            for c in range(CH_XBC, CH_XBC + 8):
                chunk_lo(pool, c)

        phases.append(dict(gpsimd=xbc_gpsimd, tensor=xbc_all_tensor, scalar=xbc_all_scalar, vector=xbc_all_vector))

        STEPS = [(0, 0), (1, 1), (0, 1), (1, 0), (0, 2), (1, 5), (0, 3), (1, 4), (0, 4), (1, 3), (0, 5), (1, 2)]
        NCTX = 4
        W1 = R + 22528
        TD = view(R + 30720, SSD_H, P)
        DM = view(W1, SSD_H, P)
        EC = view(W1 + 2048, SSD_H, P)
        XDT = view(W1 + 4096, 1024)
        XW = view(W1 + 5120, 1024)
        BTOK = view(W1 + 6144, 512)
        CBM = view(W1 + 6656, SSD_G, P)
        STATE = [view(R + 1024 * d, 1024) for d in range(2)]
        TRI = (C["triu"], C["tril"])

        def hcol(ap):
            return ap.unsqueeze(2).to_broadcast([P, SSD_H, 64])

        def ssd_tensor(pe):
            for n, (d, t) in enumerate(STEPS):
                tok = slice(t * P, t * P + P)
                m = n - NCTX
                if n >= NCTX:
                    if m >= 1:
                        pe.wait_ge(sem("ssd_cb"), m)
                    for g in range(SSD_G):
                        mm = pe.matmul(bank(3, P, g * P), XBC[:, 8 + g, tok], XBC[:, 12 + g, tok],
                                       start=True, stop=True)
                    mm.then_inc(sem("ssd_cbmm"), 1)
                    if m >= 1:
                        pe.wait_ge(sem("ssd_y"), m)
                    pe.wait_ge(sem("ssd_tridta"), m + 1)
                    for q in range(4):
                        mm = pe.matmul(bank(4 + q), C["ones"], TD[:, 4 * q:4 * q + 4, :], start=True, stop=True)
                        if q % 2 == 1:
                            mm.then_inc(sem("ssd_rows"), 1)
                if n >= 1:
                    pe.wait_ge(sem("ssd_state"), n)
                    pe.wait_ge(sem("ssd_btok"), n)
                for j in range(KT):
                    mm = pe.transpose(bank(0, P, j * P), XBC[:, j, tok], C["ident"])
                mm.then_inc(sem("ssd_xturn"), 1)
                for g in range(SSD_G):
                    mm = pe.transpose(bank(2, P, g * P), XBC[:, 8 + g, tok], C["ident"])
                mm.then_inc(sem("ssd_bturn"), 1)
                if n >= NCTX:
                    for h in range(SSD_H):
                        if h % 8 == 0:
                            pe.wait_ge(sem("ssd_decay"), 2 * m + h // 8 + 1)
                            pe.wait_ge(sem("ssd_ce"), 2 * m + h // 8 + 1)
                        o = pf[64 * (h % 2):64 * (h % 2) + 64, 2048 + (h // 2) * P:2048 + (h // 2) * P + P]
                        pe.matmul(o, XDT[:, 64 * h:64 * h + 64], DM[:, h, :], start=True, stop=False)
                        mm = pe.matmul(o, STATE[d][:, 64 * h:64 * h + 64], EC[:, h, :], start=False, stop=True)
                    mm.then_inc(sem("ssd_ymm"), 1)
                pe.wait_ge(sem("ssd_xw"), n + 1)
                pe.wait_ge(sem("ssd_btok"), n + 1)
                for g in range(SSD_G):
                    mm = pe.matmul(bank(g // 2, 256, (g % 2) * 256), BTOK[:, g * P:g * P + P],
                                   XW[:, g * 256:g * 256 + 256], start=True, stop=True)
                mm.then_inc(sem("ssd_statemm"), 1)

        def ssd_vector(dve):
            def xdt(n, d, t):
                dve.wait_ge(sem("ssd_xturn"), n + 1)
                if n >= 1:
                    dve.wait_ge(sem("ssd_xw"), n)
                dve.tensor_tensor(split(XDT, SSD_H, 64), split(pf[:, 0:1024], SSD_H, 64), hcol(DT[:, d, t, :]),
                                  ALU.mult).then_inc(sem("ssd_xdt"), 1)

            for n, (d, t) in enumerate(STEPS):
                if n < NCTX:
                    xdt(n, d, t)
                if n >= NCTX:
                    m = n - NCTX
                    dve.wait_ge(sem("ssd_cbmm"), m + 1)
                    dve.tensor_tensor(CBM, split(bank(3), SSD_G, P), TRI[d].unsqueeze(1).to_broadcast([P, SSD_G, P]),
                                      ALU.mult).then_inc(sem("ssd_cb"), 1)
                    halves = [slice(8 * q, 8 * q + 8) for q in range(2)]
                    for q, hs in enumerate(halves):
                        dve.wait_ge(sem("ssd_rows"), 2 * m + q + 1)
                        dve.wait_ge(sem("ssd_erow"), 2 * m + q + 1)
                        dve.tensor_tensor(DM[:, hs, :], split(bank(4 + 2 * q, 1024), 8, P),
                                          ACOL[:, d, t, hs].unsqueeze(2).to_broadcast([P, 8, P]),
                                          ALU.subtract).then_inc(sem("ssd_sub"), 1)
                        dve.wait_ge(sem("ssd_sub"), 2 * m + q + 1)
                        dve.tensor_scalar(DM[:, hs, :], DM[:, hs, :], 0.0, None, ALU.min).then_inc(sem("ssd_seg"), 1)
                    xdt(n, d, t)
                    dve.wait_ge(sem("ssd_cb"), m + 1)
                    for q, hs in enumerate(halves):
                        dve.wait_ge(sem("ssd_exp"), 2 * m + q + 1)
                        dve.tensor_tensor(DM[:, hs, :].rearrange("p (g r) i -> p g r i", r=4),
                                          bank(4 + 2 * q, 1024).rearrange("p (g r i) -> p g r i", r=4, i=P),
                                          CBM[:, 2 * q:2 * q + 2, :].unsqueeze(2).to_broadcast([P, 2, 4, P]),
                                          ALU.mult).then_inc(sem("ssd_decay"), 1)
                    dve.wait_ge(sem("ssd_ymm"), m + 1)
                    y = Y[:, :, (t - 2) * P:(t - 1) * P]
                    dve.tensor_tensor(y, y, split(pf[:, 2048:3072], KT, P), ALU.add).then_inc(sem("ssd_y"), 1)
                dve.wait_ge(sem("ssd_statemm"), n + 1)
                if n < 2:
                    dve.tensor_copy(STATE[d], pf[:, 0:1024]).then_inc(sem("ssd_state"), 1)
                else:
                    s = split(STATE[d], SSD_H, 64)
                    dve.tensor_tensor(s, s, hcol(DECAY[:, d, t, :]), ALU.mult).then_inc(sem("ssd_decayed"), 1)
                    dve.wait_ge(sem("ssd_decayed"), n - 1)
                    dve.tensor_tensor(STATE[d], STATE[d], pf[:, 0:1024], ALU.add).then_inc(sem("ssd_state"), 1)

        def ssd_scalar(act):
            for n, (d, t) in enumerate(STEPS):
                act.wait_ge(sem("ssd_bturn"), n + 1)
                if n >= 1:
                    act.wait_ge(sem("ssd_statemm"), n)
                act.activation(BTOK, bank(2), ACT.Copy).then_inc(sem("ssd_btok"), 1)
                if n >= NCTX:
                    m = n - NCTX
                    if m >= 1:
                        act.wait_ge(sem("ssd_ymm"), m)
                    for q in range(2):
                        act.wait_ge(sem("ssd_rows"), 2 * m + q + 1)
                        act.activation(EC[:, 8 * q:8 * q + 8, :].rearrange("p h i -> p (h i)"), bank(4 + 2 * q, 1024),
                                       ACT.Exp).then_inc(sem("ssd_erow"), 1)
                    for q in range(2):
                        act.wait_ge(sem("ssd_seg"), 2 * m + q + 1)
                        act.activation(bank(4 + 2 * q, 1024), DM[:, 8 * q:8 * q + 8, :].rearrange("p h i -> p (h i)"),
                                       ACT.Exp).then_inc(sem("ssd_exp"), 1)

        def ssd_gpsimd(pool):
            for n, (d, t) in enumerate(STEPS):
                fill(pool, ys, n)
                if n >= NCTX:
                    m = n - NCTX
                    for q in range(2):
                        pool.wait_ge(sem("ssd_erow"), 2 * m + q + 1)
                        ec = EC[:, 8 * q:8 * q + 8, :].rearrange("p (g r) i -> p g r i", r=4)
                        cm = XBC[:, 12 + 2 * q:14 + 2 * q, t * P:t * P + P].unsqueeze(2).to_broadcast([P, 2, 4, P])
                        pool.tensor_tensor(ec, ec, cm, ALU.mult).then_inc(sem("ssd_ce"), 1)
                pool.wait_ge(sem("ssd_xdt"), n + 1)
                if n >= 1:
                    pool.wait_ge(sem("ssd_statemm"), n)
                pool.tensor_tensor(split(XW, SSD_H, 64), split(XDT, SSD_H, 64), hcol(TOEND[:, d, t, :]),
                                   ALU.mult).then_inc(sem("ssd_xw"), 1)
                if NCTX <= n + 1 < len(STEPS):
                    dn, tn = STEPS[n + 1]
                    if n >= NCTX:
                        pool.wait_ge(sem("ssd_rows"), 2 * (n - NCTX) + 2)
                    pool.tensor_tensor(TD, TRI[dn].unsqueeze(1).to_broadcast([P, SSD_H, P]),
                                       DTA[:, dn, tn, :].unsqueeze(2).to_broadcast([P, SSD_H, P]),
                                       ALU.mult).then_inc(sem("ssd_tridta"), 1)

        phases.append(dict(tensor=ssd_tensor, vector=ssd_vector, scalar=ssd_scalar, gpsimd=ssd_gpsimd))

        ZS = [view(R + 6144 + 1024 * i, 2, T) for i in range(2)]
        ZQ = [view(R + 8192 + 1024 * i, 2, T) for i in range(2)]
        ZR = [view(R + 10240 + 512 * i, T) for i in range(2)]

        def z_tensor(pe):
            def sums(g):
                pe.wait_ge(sem("z_sq"), g + 1)
                if g >= 1:
                    pe.wait_ge(sem("z_ln"), g)
                for j in range(2):
                    mm = pe.matmul(bank(6), C["ones"], ZQ[g % 2][:, j, :], start=(j == 0), stop=(j == 1))
                mm.then_inc(sem("z_sums"), 1)

            for g in range(4):
                c = CH_Z + g
                arrived(pe, c)
                if g >= 2:
                    pe.wait_ge(sem("z_silu"), g - 1)
                for j in range(2):
                    for k in range(KT):
                        mm = pe.matmul(acc(g)[:, j * 512:j * 512 + 512], wtile(c, k, j), HT[:, k, :],
                                       start=(k == 0), stop=(k == KT - 1))
                chunk_done(mm)
                if g:
                    sums(g - 1)
            sums(3)

        def z_scalar(act):
            def rstd(g):
                act.wait_ge(sem("z_gated"), g + 1)
                act.activation(ZQ[g % 2], Y[:, 2 * g:2 * g + 2, :], ACT.Square).then_inc(sem("z_sq"), 1)
                load_exp_ln(act)
                act.wait_ge(sem("z_sums"), g + 1)
                if g >= 2:
                    act.wait_ge(sem("z_out"), g - 1)
                act.activation(ZR[g % 2], bank(6), ACT.Ln, scale=1.0 / 256, bias=epst[:, :]).then_inc(sem("z_ln"), 1)
                act.wait_ge(sem("z_ln"), g + 1)
                act.activation(ZR[g % 2], ZR[g % 2], ACT.Exp, scale=-0.5).then_inc(sem("z_rstd"), 1)

            for g in range(4):
                act.wait_ge(sem("chunk_done"), CH_Z + g + 1)
                if g >= 2:
                    act.wait_ge(sem("z_gated"), g - 1)
                act.activation(ZS[g % 2], split(acc(g)[:, 0:1024], 2, T), ACT.Silu).then_inc(sem("z_silu"), 1)
                if g:
                    rstd(g - 1)
            rstd(3)

        def z_vector(dve):
            for g in range(4):
                y = Y[:, 2 * g:2 * g + 2, :]
                dve.wait_ge(sem("z_silu"), g + 1)
                dve.tensor_tensor(y, y, ZS[g % 2], ALU.mult).then_inc(sem("z_gated"), 1)
                dve.wait_ge(sem("z_rstd"), g + 1)
                for j in range(2):
                    ins = dve.scalar_tensor_tensor(y[:, j, :], y[:, j, :], v("g_ssd", 2 * g + j, 1), ZR[g % 2],
                                                   ALU.mult, ALU.mult)
                ins.then_inc(sem("z_out"), 1)

        phases.append(dict(tensor=z_tensor, scalar=z_scalar, vector=z_vector))

        MERGED = view(R + 6144, KT, T)
        MG = [view(R + 10240 + 1024 * i, 1024) for i in range(2)]
        MT = view(R + 12288, 1024)
        MIX = view(R + 13312, KT, T)
        SOURCES = (HT, O1, Y, MERGED)
        HALVES = [(rounded_rows(hi, KT), rounded_rows(at, KT)) for hi, at in
                  ((R + 22528, 4096), (R + 26624, R + 2048), (R + 13312, R + 18432), (R + 22528, R + 6144))]

        def source_hi(act, x, k):
            act.activation(HALVES[x][0][k], SOURCES[x][:, k, :], ACT.Copy).then_inc(sem("source_hi"), 1)

        def source_lo(dve, x, k):
            dve.wait_ge(sem("source_hi"), 8 * x + k + 1)
            dve.tensor_tensor(HALVES[x][1][k], SOURCES[x][:, k, :], HALVES[x][0][k].bitcast(F32),
                              ALU.subtract).then_inc(sem("source_lo"), 1)

        def merge_tensor(pe):
            def products(n, x, fresh):
                c = CH_MERGE + n
                halves_ready(pe, c)
                for j in range(2):
                    for k in range(KT):
                        if fresh and j == 0:
                            pe.wait_ge(sem("source_lo"), 8 * x + k + 1)
                        mm = product(pe, acc(n)[:, j * 512:j * 512 + 512], c, k * 256 + j * P,
                                     (HALVES[x][0][k], HALVES[x][1][k]), k == 0, k == KT - 1)
                chunk_done(mm)

            for n in range(16):
                if n >= 2 and n % 2 == 0:
                    pe.wait_ge(sem("merge_gate"), n // 2)
                if n >= 2 and n % 2 == 1:
                    pe.wait_ge(sem("merge_prod"), n // 2)
                products(n, (0, 1, 0, 2)[n % 4], n in (0, 1, 3))
            for n in range(4):
                if n < 2:
                    pe.wait_ge(sem("merge_gate"), 8)
                    pe.wait_ge(sem("merge_prod"), 8)
                else:
                    pe.wait_ge(sem("mix_out"), n - 1)
                products(16 + n, 3, n == 0)

        def merge_scalar(act):
            chunk_hi(act, CH_MERGE)
            for k in range(KT):
                source_hi(act, 0, k)
            chunk_hi(act, CH_MERGE + 1)
            for x in (1, 2):
                for k in range(KT):
                    source_hi(act, x, k)
            for q in range(8):
                c = CH_MERGE + 2 * q
                act.wait_ge(sem("chunk_done"), c + 1)
                if q >= 2:
                    act.wait_ge(sem("merge_prod"), q - 1)
                act.activation(MG[q % 2], acc(0)[:, 0:1024], ACT.Sigmoid).then_inc(sem("merge_gate"), 1)
                chunk_hi(act, c + 2)
                if q == 7:
                    act.wait_ge(sem("merge_sum"), 3)
                    for k in range(6):
                        source_hi(act, 3, k)
                chunk_hi(act, c + 3)
            act.wait_ge(sem("merge_sum"), 4)
            for k in (6, 7):
                source_hi(act, 3, k)
            for n in range(4):
                act.wait_ge(sem("chunk_done"), CH_OUT + n + 1)
                if n < 2:
                    chunk_hi(act, CH_OUT + n + 2)
                act.activation(MIX[:, 2 * n:2 * n + 2, :], split(acc(n)[:, 0:1024], 2, T),
                               ACT.Copy).then_inc(sem("mix_out"), 1)

        def merge_vector(dve):
            for x in range(3):
                for k in range(KT):
                    source_lo(dve, x, k)
            for q in range(8):
                m = MERGED[:, 2 * (q // 2):2 * (q // 2) + 2, :].rearrange("p a b -> p (a b)")
                if q == 7:
                    for k in range(6):
                        source_lo(dve, 3, k)
                dve.wait_ge(sem("chunk_done"), CH_MERGE + 2 * q + 2)
                dve.wait_ge(sem("merge_gate"), q + 1)
                dst = m if q % 2 == 0 else MT
                dve.tensor_tensor(dst, acc(1)[:, 0:1024], MG[q % 2], ALU.mult).then_inc(sem("merge_prod"), 1)
                if q % 2 == 1:
                    dve.wait_ge(sem("merge_prod"), q + 1)
                    dve.tensor_tensor(m, m, MT, ALU.add).then_inc(sem("merge_sum"), 1)
            for k in (6, 7):
                source_lo(dve, 3, k)

        def merge_gpsimd(pool):
            for c in range(CH_MERGE, CH_MERGE + 20):
                chunk_lo(pool, c)
            pool.wait_ge(sem("filled"), 16 * 2 * (MAXBLK // NFILL))

        phases.append(dict(tensor=merge_tensor, scalar=merge_scalar, vector=merge_vector, gpsimd=merge_gpsimd))

        norm(MIX, T, None, lambda k: gain[:, G1 + k:G1 + k + 1], residual=XT)
        norm(XT, T, HT, lambda k: gain[:, A2 + k:A2 + k + 1], lambda k: mod[:, 24 + k, 0:1])

        H2TOK = view(R, TT, D)
        SHID = view(R + 4096, 2, T)
        WGU = [view(R + 5120 + 4096 * s, KT, 512) for s in range(2)]
        WD = [view(R + 13312 + 2048 * s, 2, D) for s in range(2)]
        XB = [view(R + 17408 + 1024 * s, D) for s in range(2)]
        XBT = [view(R + 19456 + 1024 * s, KT, P) for s in range(2)]
        YO = [view(R + 21504 + 1024 * s, D) for s in range(2)]
        HID = [view(R + 23552 + 256 * s, 256) for s in range(2)]
        HIDT = [view(R + 24064 + 256 * s, 2, P) for s in range(2)]
        SIL = [view(R + 24576 + 256 * s, 256) for s in range(2)]
        M0 = R + 25088
        SCO, SEL, MSK, REP, KEY = (view(M0 + 256 * i, TT, E_N) for i in range(5))
        WTS = view(M0 + 1280, TT, E_N)
        GS8 = view(M0 + 1536, TT, 8, 8)
        GSC = view(M0 + 1792, TT, 8)
        GMK = view(M0 + 1824, TT, 8)
        WSUM = view(M0 + 1856, TT)
        NB = view(M0 + 1860, E_N)
        INCL = view(M0 + 1924, E_N)
        START = view(M0 + 1988, E_N)
        DST8 = view(M0 + 2052, TT, 8)
        W8 = view(M0 + 2084, TT, 8)
        DSTI = view(M0 + 2116, 32).bitcast(U32)
        LOWER = view(M0 + 2148, 64)
        IOTA = view(M0 + 2212, MAXBLK)
        BEF = view(M0 + 2308, MAXBLK)
        BEI = view(M0 + 2404, MAXBLK).bitcast(I32)
        NPF = view(M0 + 2500, 1)
        NPI = view(M0 + 2501, 1).bitcast(I32)
        EVEN = view(M0 + 2502, MAXBLK // 2)
        CMP = view(R + 17408, MAXBLK, E_N)
        PICK = view(R + 17408, 32, E_N)
        CMPG = view(M0 + 2560, TT, 8, 8)
        CMPE = view(M0 + 2816, TT, 8, 8)

        def rt_sync_gpsimd(pool):
            pool.dma_start(view(M0 + 2148, 64 + MAXBLK), iota_t).then_inc(sem("iota_loaded"), 16)
            pool.wait_ge(sem("rt_dest"), 1)
            pool.wait_ge(sem("h2_tok"), 8)
            for t in range(TT):
                for k in range(8):
                    pool.indirect_dma_start(xs, bass.IndirectOffsetOnAxis(ap=DSTI[:, 8 * t + k:8 * t + k + 1], axis=0),
                                            H2TOK[:, t, :], None).then_inc(sem("scattered"), 16)
            pool.wait_ge(sem("scattered"), 16 * 32)

        def rt_tensor(pe):
            for t in range(TT):
                for k in range(KT):
                    mm = pe.matmul(bank(6, E_N, t * E_N), HT[:, k, t * P:t * P + P], wrt[:, k, :],
                                   start=(k == 0), stop=(k == KT - 1))
            mm.then_inc(sem("rt_logits"), 1)
            for c in range(2):
                arrived(pe, CH_SH + c)
                for j in range(2):
                    for k in range(KT):
                        mm = pe.matmul(acc(c)[:, j * 512:j * 512 + 512], wtile(CH_SH + c, k, j), HT[:, k, :],
                                       start=(k == 0), stop=(k == KT - 1))
                chunk_done(mm)
            for q in range(8):
                if q >= 2:
                    pe.wait_ge(sem("h2_tok"), q - 1)
                for i in range(4):
                    mm = pe.transpose(bank(2 + 3 * (q % 2), P, i * P), HT[:, 4 * (q % 2) + i, (q // 2) * P:(q // 2) * P + P],
                                      C["ident"])
                mm.then_inc(sem("h2_turn"), 1)
            pe.wait_ge(sem("rt_mask"), 1)
            for t in range(TT):
                for u in range(t + 1):
                    pe.matmul(bank(7, E_N, t * E_N), C["triu_strict"] if u == t else C["ones"], MSK[:, u, :],
                              start=(u == 0), stop=(u == t))
            for u in range(TT):
                mm = pe.matmul(bank(6, E_N, 256), C["ones"], MSK[:, u, :], start=(u == 0), stop=(u == TT - 1))
            mm.then_inc(sem("rt_pos"), 1)

        def rt_scalar(act):
            act.wait_ge(sem("rt_logits"), 1)
            act.activation(SCO.rearrange("p a b -> p (a b)"), bank(6, 256), ACT.Sigmoid).then_inc(sem("rt_scores"), 1)
            act.wait_ge(sem("chunk_done"), CH_SH + 1)
            act.activation(SHID, split(acc(0)[:, 0:1024], 2, T), ACT.Silu).then_inc(sem("sh_silu"), 1)
            for q in range(8):
                act.wait_ge(sem("h2_turn"), q + 1)
                act.activation(H2TOK[:, q // 2, 512 * (q % 2):512 * (q % 2) + 512], bank(2 + 3 * (q % 2)),
                               ACT.Copy).then_inc(sem("h2_tok"), 1)

        def rt_vector(dve):
            link = Link(dve, "rt_link")

            def spread(ap, n):
                return ap.unsqueeze(3).to_broadcast([P, TT, 8, n])

            def groups(ap):
                return ap.rearrange("p t (g e) -> p t g e", e=8)

            dve.wait_ge(sem("rt_scores"), 1)
            link(dve.tensor_tensor(SEL, SCO, v("router_bias").unsqueeze(1).to_broadcast([P, TT, E_N]), ALU.add))
            for t in range(TT):
                for g in range(8):
                    ins = dve.max(GS8[:, t, g, :], SEL[:, t, 8 * g:8 * g + 8])
            link(ins)
            link(dve.tensor_tensor(GSC, GS8[:, :, :, 0], GS8[:, :, :, 1], ALU.add))
            other = GSC.unsqueeze(2).to_broadcast([P, TT, 8, 8])
            this = spread(GSC, 8)
            dve.wait_ge(sem("iota_loaded"), 16)
            dve.tensor_tensor(CMPG, other, this, ALU.is_gt)
            link(dve.tensor_tensor(CMPE, other, this, ALU.is_equal))
            lower = LOWER.rearrange("p (a b) -> p a b", b=8).unsqueeze(1).to_broadcast([P, TT, 8, 8])
            link(dve.tensor_tensor(CMPE, CMPE, lower, ALU.mult))
            link(dve.tensor_tensor(CMPG, CMPG, CMPE, ALU.add))
            link(dve.tensor_reduce(GMK, CMPG, AX.X, ALU.add))
            link(dve.tensor_scalar(GMK, GMK, 3.5, None, ALU.is_lt))
            link(dve.tensor_tensor(groups(SEL), groups(SEL), spread(GMK, 8), ALU.mult))
            link(dve.tensor_scalar(GMK, GMK, -1.0, 1e30, ALU.add, ALU.mult))
            link(dve.tensor_tensor(groups(SEL), groups(SEL), spread(GMK, 8), ALU.add))
            for t in range(TT):
                ins = dve.max(DST8[:, t, :], SEL[:, t, :])
            link(ins)
            for t in range(TT):
                ins = dve.match_replace(out=REP[:, t, :], in_to_replace=DST8[:, t, :], in_values=SEL[:, t, :],
                                        imm_value=-3e38)
            link(ins)
            dve.tensor_tensor(MSK, REP, SEL, ALU.not_equal).then_inc(sem("rt_mask"), 1)
            dve.wait_ge(sem("rt_mask"), 1)
            link(dve.tensor_tensor(WTS, SCO, MSK, ALU.mult))
            link(dve.tensor_reduce(WSUM, WTS, AX.X, ALU.add))
            link(dve.reciprocal(WSUM, WSUM))
            link(dve.tensor_scalar(WSUM, WSUM, 2.5, None, ALU.mult))
            link(dve.tensor_tensor(WTS, WTS, WSUM.unsqueeze(2).to_broadcast([P, TT, E_N]), ALU.mult))
            dve.wait_ge(sem("rt_pos"), 1)
            cnt = bank(6, E_N, 256)
            link(dve.tensor_scalar(NB, cnt, 0.0, None, ALU.is_gt))
            for i in range(1, T // P):
                link(dve.scalar_tensor_tensor(NB, cnt, 128.0 * i, NB, ALU.is_gt, ALU.add))
            link(dve.tensor_tensor_scan(INCL, C["ones"][:, 0:E_N], NB, 0.0, ALU.mult, ALU.add))
            link(dve.tensor_tensor(START, INCL, NB, ALU.subtract))
            link(dve.tensor_scalar(START, START, 128.0, 1.0, ALU.mult, ALU.add))
            link(dve.tensor_tensor(KEY, split(bank(7, 256), TT, E_N), START.unsqueeze(1).to_broadcast([P, TT, E_N]),
                                   ALU.add))
            link(dve.tensor_tensor(KEY, KEY, MSK, ALU.mult))
            for t in range(TT):
                ins = dve.max(DST8[:, t, :], KEY[:, t, :])
            link(ins)
            dve.tensor_scalar(DSTI, DST8.rearrange("p a b -> p (a b)"), -1.0, None,
                              ALU.add).then_inc(sem("rt_dest"), 1)
            cmp_in = INCL[0:1, :].unsqueeze(1).to_broadcast([1, MAXBLK, E_N])
            link(dve.tensor_tensor(CMP[0:1], cmp_in, IOTA[0:1, :].unsqueeze(2).to_broadcast([1, MAXBLK, E_N]), ALU.is_le))
            link(dve.tensor_reduce(BEF[0:1, :], CMP[0:1], AX.X, ALU.add))
            dve.tensor_scalar(BEI[0:1, :], BEF[0:1, :], float(E_N - 1), None, ALU.min).then_inc(sem("rt_blocks"), 1)
            link(dve.tensor_scalar(EVEN[0:1, :], IOTA[0:1, 0:MAXBLK:2], INCL[0:1, E_N - 1:E_N], None, ALU.is_lt))
            link(dve.tensor_reduce(NPF[0:1, :], EVEN[0:1, :], AX.X, ALU.add))
            dve.tensor_copy(NPI[0:1, :], NPF[0:1, :]).then_inc(sem("rt_blocks"), 1)
            for t in range(TT):
                for k in range(8):
                    dve.scalar_tensor_tensor(PICK[:, 8 * t + k, :], KEY[:, t, :], DST8[:, t, k:k + 1], WTS[:, t, :],
                                             ALU.is_equal, ALU.mult, accum_out=W8[:, t, k:k + 1])
            dve.wait_ge(sem("sh_silu"), 1)
            dve.wait_ge(sem("chunk_done"), CH_SH + 2)
            dve.tensor_tensor(SHID, SHID, split(acc(1)[:, 0:1024], 2, T), ALU.mult)

        phases.append(dict(tensor=rt_tensor, scalar=rt_scalar, vector=rt_vector, gpsimd=rt_sync_gpsimd))
        MOE_STAGE = len(phases)

        def pairs(eng):
            return eng.value_load(NPI[0:1, 0:1], min_val=T * 8 // P // 2, max_val=MAXBLK // 2)

        def moe_sync(sp):
            sp.wait_ge(sem("rt_blocks"), 2)
            sp.wait_ge(sem("stage_ended"), 4 * MOE_STAGE)
            n = pairs(sp)

            def load(i):
                for s in range(2):
                    sp.wait_ge(sem("moe_x_used"), i * 2 + (s + 1))
                    sp.dma_start(XB[s], xs[bass.ds(i * 256 + s * P, P), :]).then_inc(sem(f"moe_x{s}"), 16)
                for s in range(2):
                    e = sp.value_load(BEI[0:1, bass.ds(i * 2 + s, 1)], min_val=0, max_val=E_N - 1)
                    sp.wait_ge(sem("moe_gu_used"), i * 2 + (s + 1))
                    sp.dma_start(WGU[s].rearrange("p a b -> p (a b)"),
                                 we_gu[bass.ds(e, 1)].rearrange("o p n -> (o p) n")).then_inc(sem(f"moe_wgu{s}"), 16)
                for s in range(2):
                    e = sp.value_load(BEI[0:1, bass.ds(i * 2 + s, 1)], min_val=0, max_val=E_N - 1)
                    sp.wait_ge(sem("moe_d_used"), i * 2 + (s + 1))
                    sp.dma_start(WD[s].rearrange("p a b -> p (a b)"),
                                 we_down[bass.ds(e, 1)].rearrange("o p n -> (o p) n")).then_inc(sem(f"moe_wd{s}"), 16)

            def store(i):
                for s in range(2):
                    sp.wait_ge(sem(f"moe_y{s}"), i + 2)
                    sp.dma_start(ys[bass.ds(i * 256 + s * P, P), :], YO[s]).then_inc(sem(f"moe_out{s}"), 16)

            load(0)
            with sp.Fori(1, n) as i:
                load(i)
                store(i - 1)
            store(n - 1)
            for s in range(2):
                sp.wait_ge(sem(f"moe_out{s}"), n * 16 + 16)
                sp.dma_start(BEF[0:1, s:s + 1], IOTA[0:1, s:s + 1]).then_inc(sem("moe_rows_out"), 16)

        def moe_tensor(pe):
            for name in ("moe_x_used", "moe_gu_used", "moe_d_used"):
                pe.sem_inc(sem(name), 2)
            with pe.Fori(0, pairs(pe)) as i:
                for s in range(2):
                    pe.wait_ge(sem(f"moe_x{s}"), i * 16 + 16)
                    pe.wait_ge(sem(f"moe_y{s}"), i + 1)
                    for k in range(KT):
                        mm = pe.transpose(bank(2 * s, P, k * P), XB[s][:, k * P:k * P + P], C["ident"])
                    mm.then_inc(sem("moe_x_used"), 1)
                for s in range(2):
                    pe.wait_ge(sem(f"moe_xt{s}"), i + 1)
                    pe.wait_ge(sem(f"moe_wgu{s}"), i * 16 + 16)
                    for k in range(KT):
                        mm = pe.matmul(bank(4 + s), XBT[s][:, k, :], WGU[s][:, k, :], start=(k == 0), stop=(k == KT - 1))
                    mm.then_inc(sem("moe_gu_used"), 1)
                for s in range(2):
                    pe.wait_ge(sem(f"moe_hid{s}"), i + 1)
                    for k in range(2):
                        mm = pe.transpose(bank(6 + s, P, k * P), HID[s][:, k * P:k * P + P], C["ident"])
                    mm.then_inc(sem("moe_hturn"), 1)
                for s in range(2):
                    pe.wait_ge(sem(f"moe_hidt{s}"), i + 1)
                    pe.wait_ge(sem(f"moe_wd{s}"), i * 16 + 16)
                    for j in range(2):
                        for k in range(2):
                            mm = pe.matmul(bank(2 * s + j), HIDT[s][:, k, :], WD[s][:, k, j * 512:j * 512 + 512],
                                           start=(k == 0), stop=(k == 1))
                    mm.then_inc(sem("moe_d_used"), 1)

        def moe_scalar(act):
            act.sem_inc(sem("moe_y0"), 1)
            act.sem_inc(sem("moe_out0"), 16)
            with act.Fori(0, pairs(act)) as i:
                act.wait_ge(sem("moe_x_used"), i * 2 + 3)
                act.activation(XBT[0].rearrange("p a b -> p (a b)"), pf[:, 0:1024], ACT.Copy).then_inc(sem("moe_xt0"), 1)
                for s in range(2):
                    act.wait_ge(sem("moe_gu_used"), i * 2 + (s + 3))
                    act.activation(SIL[s], bank(4 + s, 256), ACT.Silu).then_inc(sem(f"moe_silu{s}"), 1)
                act.wait_ge(sem("moe_hturn"), i * 2 + 1)
                act.activation(HIDT[0].rearrange("p a b -> p (a b)"), bank(6, 256), ACT.Copy).then_inc(sem("moe_hidt0"), 1)
                act.wait_ge(sem("moe_d_used"), i * 2 + 3)
                act.wait_ge(sem("moe_out0"), i * 16 + 16)
                act.activation(YO[0], pf[:, 0:1024], ACT.Copy).then_inc(sem("moe_y0"), 1)

        def moe_vector(dve):
            dve.sem_inc(sem("moe_y1"), 1)
            dve.sem_inc(sem("moe_out1"), 16)
            with dve.Fori(0, pairs(dve)) as i:
                dve.wait_ge(sem("moe_x_used"), i * 2 + 4)
                dve.tensor_copy(XBT[1].rearrange("p a b -> p (a b)"), pf[:, 1024:2048]).then_inc(sem("moe_xt1"), 1)
                for s in range(2):
                    dve.wait_ge(sem(f"moe_silu{s}"), i + 1)
                    dve.tensor_tensor(HID[s], SIL[s], bank(4 + s, 256, 256), ALU.mult).then_inc(sem(f"moe_hid{s}"), 1)
                dve.wait_ge(sem("moe_hturn"), i * 2 + 2)
                dve.tensor_copy(HIDT[1].rearrange("p a b -> p (a b)"), bank(7, 256)).then_inc(sem("moe_hidt1"), 1)
                dve.wait_ge(sem("moe_d_used"), i * 2 + 4)
                dve.wait_ge(sem("moe_out1"), i * 16 + 16)
                dve.tensor_copy(YO[1], pf[:, 1024:2048]).then_inc(sem("moe_y1"), 1)

        def moe_gpsimd(pool):
            pool.wait_ge(sem("moe_rows_out"), 32)

        phases.append(dict(tensor=moe_tensor, scalar=moe_scalar, vector=moe_vector, gpsimd=moe_gpsimd))

        GB = [view(R + 5120 + 1024 * i, D) for i in range(8)]
        F = view(R + 13312, KT, T)

        def gather_gpsimd(pool):
            for n in range(32):
                if n >= 8:
                    pool.wait_ge(sem("g_used"), n - 7)
                pool.indirect_dma_start(GB[n % 8], None, ys, bass.IndirectOffsetOnAxis(ap=DSTI[:, n:n + 1], axis=0)
                                        ).then_inc(sem(f"gathered{n % 8}"), 16)

        def gather_vector(dve):
            for n in range(32):
                t, k = divmod(n, 8)
                dve.wait_ge(sem(f"gathered{n % 8}"), 16 * (n // 8 + 1))
                if k == 0:
                    dve.tensor_scalar(H2TOK[:, t, :], GB[n % 8], W8[:, t, 0:1], None, ALU.mult).then_inc(sem("g_used"), 1)
                else:
                    dve.wait_ge(sem("g_used"), n)
                    dve.scalar_tensor_tensor(H2TOK[:, t, :], GB[n % 8], W8[:, t, k:k + 1], H2TOK[:, t, :], ALU.mult,
                                             ALU.add).then_inc(sem("g_used"), 1)

        def gather_tensor(pe):
            c = CH_SH + 2
            arrived(pe, c)
            for j in range(KT):
                for k in range(2):
                    pe.matmul(bank(j), ring[:, c % NSLOT, k * D + j * P:k * D + j * P + P], SHID[:, k, :],
                              start=(k == 0), stop=(k == 1))
            pe.wait_ge(sem("g_used"), 32)
            for j in range(KT):
                for t in range(TT):
                    mm = pe.matmul(bank(j, P, t * P), H2TOK[:, t, j * P:j * P + P], C["ident"], start=False,
                                   stop=(t == TT - 1), skip_group_check=True)
                if j == KT - 1:
                    chunk_done(mm)

        def gather_scalar(act):
            act.wait_ge(sem("chunk_done"), CH_SH + 3)
            for j in range(KT):
                act.activation(F[:, j, :], bank(j), ACT.Copy)

        phases.append(dict(tensor=gather_tensor, scalar=gather_scalar, vector=gather_vector, gpsimd=gather_gpsimd))
        norm(F, T, None, lambda k: gain[:, G2 + k:G2 + k + 1], residual=XT)

        BLOCK1_STAGES = len(phases)

        OD = view(R, KT, T)

        def dq(hq, g):
            return view(R + 4096 + 9216 * (hq % 2) + 3072 * g, 2, T)

        def dk(hq, g):
            return view(R + 5120 + 9216 * (hq % 2) + 3072 * g, 2, T)

        def dv(hq, g):
            return view(R + 6144 + 9216 * (hq % 2) + 3072 * g, TT, 256)

        DH = (rounded_rows(R + 22528, KT), rounded_rows(4096, KT))
        DRAW, DQN, DCO, DSQ, DRS = (view(R + 26624 + 512 * b, T) for b in range(5))
        dmask = view(R + 29184, 1152).bitcast(BF16)
        DPB = [view(R + 30336, TA), view(R + 4096, TA)]
        DPT = [view(R + 31104, AT, P), view(R + 4096 + TA, AT, P)]

        def dil_load_gpsimd(pool):
            pool.dma_start(rope[:, :, :], rope_t[1]).then_inc(sem("dil_loaded"), 16)
            pool.dma_start(dmask, dmask_t[:, 0:2304]).then_inc(sem("dil_loaded"), 16)
            pool.dma_start(wdt[:, :, :], w_z).then_inc(sem("dil_loaded"), 16)
            pool.dma_start(x_saved, XT).then_inc(sem("dil_loaded"), 16)
            pool.wait_ge(sem("dil_loaded"), 64)

        norm(XT, T, None, lambda k: v("attn_norm", k, 1), halves=DH)
        phases[-1]["gpsimd"] = dil_load_gpsimd

        def acc2(n):
            return pf[:, (n % 2) * 1024:(n % 2) * 1024 + 1024]

        NH, NU_Q = 18, 16

        def dil_half(h):
            return h // NH, h % NH // 6, h % 6 // 2, h % 2

        def dil_norm(h):
            hq, g, s, j = dil_half(h)
            return None if s == 2 else 12 * hq + 4 * g + 2 * s + j

        def dil_share(u):
            x = u % NU_Q
            return range(NH * (u // NU_Q + 1) + x * NH // NU_Q, NH * (u // NU_Q + 1) + (x + 1) * NH // NU_Q)

        LAST = 3 * NU_Q
        DU = 4 * NU_Q

        def dil_unit(u):
            return u // NU_Q, (u // 4) % 4, u % 4

        def score_bank(u):
            return 5 * score_pair(u)

        def score_pair(u):
            return 1 if u >= LAST and u % 2 else 0

        def dil_tensor(pe):
            def project(h, aside=None):
                hq, g, s, j = dil_half(h)
                c = CH_DIL + h // 2
                before = dil_norm(h - 1) if h else None

                def between(eighth):
                    if eighth == 1 and before is not None:
                        pair_sums(before, h - 1)
                    if eighth == 2 and aside is not None:
                        aside()
                    if eighth == 6 and before is not None:
                        rotate(before)

                if j == 0:
                    halves_ready(pe, c)
                if h >= 2:
                    pe.wait_ge(sem("dil_evac"), h - 1)
                out = bank(5 + h % 2)
                if s < 2:
                    for k in range(KT):
                        between(k)
                        mm = product(pe, out, c, k * 256 + j * P, (DH[0][k], DH[1][k]), k == 0, k == KT - 1)
                else:
                    for x in range(2 * KT):
                        t, k = 2 * j + x // KT, x % KT
                        if x % 2 == 0:
                            between(x // 2)
                        tokens = slice(t * P, t * P + P) if g == 0 else slice(t, T, 4)
                        hi, lo = (half[k][:, tokens] for half in DH)
                        whi, wlo = (whalf(c, part)[:, k * 256:k * 256 + 256] for part in range(2))
                        o = out[:, (t % 2) * 256:(t % 2) * 256 + 256]
                        pe.matmul(o, hi, whi, start=(k == 0), stop=False)
                        pe.matmul(o, hi, wlo, start=False, stop=False)
                        mm = pe.matmul(o, lo, whi, start=False, stop=(k == KT - 1))
                if j == 0:
                    mm.then_inc(sem("dil_half"), 1)
                else:
                    chunk_done(mm)

            def pair_sums(n, h):
                pe.wait_ge(sem("dil_evac"), h + 1)
                if n >= 1:
                    pe.wait_ge(sem("dil_out"), n)
                pe.matmul(bank(7), C["pair"], DSQ, start=True, stop=True).then_inc(sem("dil_ss"), 1)

            def rotate(n):
                pe.wait_ge(sem("dil_qn"), n + 1)
                pe.matmul(bank(7), C["rot"], DQN, start=True, stop=True).then_inc(sem("dil_rot"), 1)

            def scores(u):
                hq, hl, r = dil_unit(u)
                rows, j, b = slice(64 * (hl % 2), 64 * (hl % 2) + 64), hl // 2, score_bank(u)
                if u % NU_Q == 0:
                    pe.wait_ge(sem("dil_out"), 12 * hq + 12)
                    pe.wait_ge(sem("dil_evac"), NH * hq + NH)
                if u >= 1:
                    pe.wait_ge(sem("dil_exp"), u if u <= LAST else u - 1)
                pe.matmul(bank(b), identb[:, :], dmask[:, 512 * r:512 * r + 512], start=True, stop=False)
                pe.matmul(bank(b), dq(hq, 0)[rows, j, r:T:4], dk(hq, 0)[rows, j, :], start=False, stop=True)
                for g in (1, 2):
                    o = bank(b + 1, P, P * (g - 1))
                    pe.matmul(o, identb[:, :], dmask[:, 1920 + P * g:2048 + P * g], start=True, stop=False)
                    mm = pe.matmul(o, dq(hq, g)[rows, j, r:T:4], dk(hq, g)[rows, j, r:T:4], start=False, stop=True)
                mm.then_inc(sem("dil_scores"), 1)

            def turn(u):
                pe.wait_ge(sem("dil_prob"), u + 1)
                if u >= 1:
                    pe.wait_ge(sem("dil_turned"), u)
                for t in range(AT):
                    mm = pe.transpose(bank(2, P, t * P), DPB[score_pair(u)][:, t * P:t * P + P], C["ident"])
                mm.then_inc(sem("dil_turn"), 1)

            def values(u):
                hq, hl, r = dil_unit(u)
                pe.wait_ge(sem("dil_turned"), u + 1)
                if u % 8 == 0 and u:
                    pe.wait_ge(sem("dil_o"), u // 8)
                o = pf[64 * (hl % 2):64 * (hl % 2) + 64, 2048 + r * P:2048 + r * P + P]
                for t in range(AT):
                    val = (dv(hq, 0)[:, t, 64 * hl:64 * hl + 64] if t < TT
                           else dv(hq, t - TT + 1)[:, r, 64 * hl:64 * hl + 64])
                    mm = pe.matmul(o, val, DPT[score_pair(u)][:, t, :], start=(t == 0), stop=(t == AT - 1))
                mm.then_inc(sem("dil_pv"), 1)

            for h in range(NH):
                project(h)
            for u in range(LAST):
                scores(u)
                for i, h in enumerate(dil_share(u)):
                    project(h, (lambda: values(u - 1)) if u and i == 0 else None)
                turn(u)
            values(LAST - 1)
            scores(LAST)
            for u in range(LAST, DU):
                if u + 1 < DU:
                    scores(u + 1)
                if u > LAST:
                    values(u - 1)
                turn(u)
            values(DU - 1)

        def dil_scalar(act):
            def evacuate(h):
                hq, g, s, j = dil_half(h)
                before, n = dil_norm(h - 1) if h else None, dil_norm(h)
                if before is not None:
                    rstd(before)
                if j == 0:
                    act.wait_ge(sem("dil_half"), h // 2 + 1)
                else:
                    act.wait_ge(sem("chunk_done"), CH_DIL + h // 2 + 1)
                    if h // 2 + 2 < 36:
                        chunk_hi(act, CH_DIL + h // 2 + 2)
                if n is None:
                    act.activation(dv(hq, g)[:, 2 * j:2 * j + 2, :].rearrange("p a b -> p (a b)"), bank(5 + h % 2),
                                   ACT.Copy).then_inc(sem("dil_evac"), 1)
                else:
                    if n >= 1:
                        act.wait_ge(sem("dil_qn"), n)
                        act.wait_ge(sem("dil_ss"), n)
                    act.activation(DRAW, bank(5 + h % 2), ACT.Copy)
                    act.activation(DSQ, bank(5 + h % 2), ACT.Square).then_inc(sem("dil_evac"), 1)

            def rstd(n):
                act.wait_ge(sem("dil_ss"), n + 1)
                if n >= 1:
                    act.wait_ge(sem("dil_qn"), n)
                act.activation(DRS, bank(7), ACT.Ln, scale=1.0 / 64, bias=epst[:, :]).then_inc(sem("dil_ln"), 1)
                act.wait_ge(sem("dil_ln"), n + 1)
                act.activation(DRS, DRS, ACT.Exp, scale=-0.5).then_inc(sem("dil_rstd"), 1)

            def turned(u):
                act.wait_ge(sem("dil_turn"), u + 1)
                if u >= 1:
                    act.wait_ge(sem("dil_pv"), u if u <= LAST else u - 1)
                act.activation(DPT[score_pair(u)].rearrange("p a b -> p (a b)"), bank(2, TA),
                               ACT.Copy).then_inc(sem("dil_turned"), 1)

            def exponent(u):
                s = SC[:, 4 * (u % 2):4 * (u % 2) + 4]
                act.wait_ge(sem("dil_bias"), u + 1)
                if u >= 1:
                    act.wait_ge(sem("dil_turn"), u if u <= LAST else u - 1)
                act.activation(DPB[score_pair(u)], bank(score_bank(u), TA), ACT.Exp, scale=0.125,
                               bias=s[:, 1:2], accum_out=s[:, 2:3]).then_inc(sem("dil_exp"), 1)

            chunk_hi(act, CH_DIL)
            chunk_hi(act, CH_DIL + 1)
            for h in range(NH):
                evacuate(h)
            for u in range(LAST):
                if u:
                    turned(u - 1)
                exponent(u)
                for h in dil_share(u):
                    evacuate(h)
            turned(LAST - 1)
            for u in range(LAST, DU):
                exponent(u)
                if u > LAST:
                    turned(u - 1)
            turned(DU - 1)

        def dil_gpsimd(pool):
            chunk_lo(pool, CH_DIL)
            chunk_lo(pool, CH_DIL + 1)
            for h in range(4 * NH):
                n = dil_norm(h)
                if n is not None:
                    pool.wait_ge(sem("dil_qn"), n + 1)
                    if n >= 1:
                        pool.wait_ge(sem("dil_out"), n)
                    pool.tensor_tensor(DCO, DQN, rope[:, 0, :], ALU.mult).then_inc(sem("dil_cos"), 1)
                if h % 2 == 1 and h // 2 + 2 < 36:
                    chunk_lo(pool, CH_DIL + h // 2 + 2)
            pool.wait_ge(sem("chunk_done"), CH_DIL + 36)
            pool.dma_start(XT, x_saved).then_inc(sem("dil_loaded"), 16)
            pool.wait_ge(sem("dil_loaded"), 80)

        def dil_vector(dve):
            def rotated(h):
                hq, g, s, j = dil_half(h)
                n = dil_norm(h)
                dve.wait_ge(sem("dil_rstd"), n + 1)
                if n >= 1:
                    dve.wait_ge(sem("dil_rot"), n)
                    dve.wait_ge(sem("dil_cos"), n)
                dve.scalar_tensor_tensor(DQN, DRAW, v(("a_q_norm", "a_k_norm")[s], g, 1), DRS,
                                         ALU.mult, ALU.mult).then_inc(sem("dil_qn"), 1)
                dve.wait_ge(sem("dil_rot"), n + 1)
                dve.tensor_tensor(bank(7), bank(7), rope[:, 1, :], ALU.mult).then_inc(sem("dil_sin"), 1)
                dve.wait_ge(sem("dil_sin"), n + 1)
                dve.wait_ge(sem("dil_cos"), n + 1)
                dve.tensor_tensor((dq, dk)[s](hq, g)[:, j, :], bank(7), DCO, ALU.add).then_inc(sem("dil_out"), 1)

            def row_max(u):
                s = SC[:, 4 * (u % 2):4 * (u % 2) + 4]
                dve.wait_ge(sem("dil_scores"), u + 1)
                dve.reduce_max(s[:, 0:1], bank(score_bank(u), TA), AX.X).then_inc(sem("dil_max"), 1)
                dve.wait_ge(sem("dil_max"), u + 1)
                dve.tensor_scalar(s[:, 1:2], s[:, 0:1], -0.125, None, ALU.mult).then_inc(sem("dil_bias"), 1)

            def probs(u):
                s = SC[:, 4 * (u % 2):4 * (u % 2) + 4]
                dve.wait_ge(sem("dil_exp"), u + 1)
                dve.reciprocal(s[:, 3:4], s[:, 2:3]).then_inc(sem("dil_recip"), 1)
                dve.wait_ge(sem("dil_recip"), u + 1)
                dve.tensor_scalar(DPB[score_pair(u)], DPB[score_pair(u)], s[:, 3:4], None, ALU.mult).then_inc(sem("dil_prob"), 1)

            def output(q):
                dve.wait_ge(sem("dil_pv"), 8 * q + 8)
                dve.tensor_copy(OD[:, q, :].rearrange("p (u r) -> p r u", r=4),
                                split(bank(4), 4, P)).then_inc(sem("dil_o"), 1)

            for h in range(1, NH):
                if dil_norm(h - 1) is not None:
                    rotated(h - 1)
            for u in range(LAST):
                row_max(u)
                probs(u)
                if u % 8 == 0 and u:
                    output(u // 8 - 1)
                for h in dil_share(u):
                    if dil_norm(h - 1) is not None:
                        rotated(h - 1)
            output(LAST // 8 - 1)
            row_max(LAST)
            for u in range(LAST, DU):
                if u + 1 < DU:
                    row_max(u + 1)
                probs(u)
                if u % 8 == 0 and u > LAST:
                    output(u // 8 - 1)
            output(DU // 8 - 1)

        phases.append(dict(tensor=dil_tensor, scalar=dil_scalar, vector=dil_vector, gpsimd=dil_gpsimd))

        def project_out(name, base, at, hi_at):
            src = view(at, KT, T)
            hi, lo = rounded_rows(hi_at, KT), rounded_rows(at, KT)

            def tensor(pe):
                for n in range(4):
                    c = base + n
                    halves_ready(pe, c)
                    if n >= 2:
                        pe.wait_ge(sem(name), n - 1)
                    for j in range(2):
                        for k in range(KT):
                            if n == 0 and j == 0:
                                pe.wait_ge(sem(name + "_lo"), k + 1)
                            mm = product(pe, acc(n)[:, j * 512:j * 512 + 512], c, k * 256 + j * P, (hi[k], lo[k]),
                                         k == 0, k == KT - 1)
                    chunk_done(mm)

            def scalar(act):
                chunk_hi(act, base)
                for k in range(KT):
                    act.activation(hi[k], src[:, k, :], ACT.Copy).then_inc(sem(name + "_hi"), 1)
                for c in range(base + 1, base + 4):
                    chunk_hi(act, c)

            def gpsimd(pool):
                for c in range(base, base + 4):
                    chunk_lo(pool, c)

            def vector(dve):
                for k in range(KT):
                    dve.wait_ge(sem(name + "_hi"), k + 1)
                    dve.tensor_tensor(lo[k], src[:, k, :], hi[k].bitcast(F32), ALU.subtract).then_inc(sem(name + "_lo"), 1)
                for n in range(4):
                    x = XT[:, 2 * n:2 * n + 2, :]
                    dve.wait_ge(sem("chunk_done"), base + n + 1)
                    dve.tensor_tensor(x, x, split(acc(n)[:, 0:1024], 2, T), ALU.add).then_inc(sem(name), 1)

            phases.append(dict(tensor=tensor, vector=vector, scalar=scalar, gpsimd=gpsimd))

        project_out("dil_proj", CH_DILO, R, R + 8192)

        HHL = (rounded_rows(R + 20480, KT), rounded_rows(R + 24576, KT))
        FHL = (rounded_rows(R + 8192, FF_PARTS[0]), rounded_rows(R + 8192 + FF_PARTS[0] * T, FF_PARTS[0]))
        FS = [view(R + 28672 + 512 * i, T) for i in range(2)]
        FV = [view(R + 29696 + 512 * i, T) for i in range(2)]

        def swiglu(f, base):
            def S(name):
                return sem(f"ff{f}_{name}")

            def down(o):
                return bank((0, 1, 3, 4)[o % 4])

            parts = [(base, FF_PARTS[0], 0), (base + FF_PARTS[0] * 3 // 2, FF_PARTS[1], FF_PARTS[0])]

            def tensor(pe):
                for part, (first, tiles, t0) in enumerate(parts):
                    for n in range(tiles):
                        c = first + n
                        halves_ready(pe, c)
                        if t0 + n >= 2:
                            pe.wait_ge(S("value"), t0 + n - 1)
                        if part == 1 and n < 2:
                            pe.wait_ge(S("down"), KT - 2 + 2 * n)
                        for j in range(2):
                            for k in range(KT):
                                mm = product(pe, acc(n)[:, j * 512:j * 512 + 512], c, k * 256 + j * P,
                                             (HHL[0][k], HHL[1][k]), k == 0, k == KT - 1)
                        chunk_done(mm)
                    for b in range(tiles * KT):
                        o, k = divmod(b, tiles)
                        c = first + tiles + b // 16
                        if b % 16 == 0:
                            halves_ready(pe, c)
                        if b == 0:
                            pe.wait_ge(S("hid_lo"), t0 + tiles)
                        if k == 0 and o >= 4:
                            pe.wait_ge(S("down"), KT * part + o - 3)
                        mm = product(pe, down(o), c, (b % 16) * P, (FHL[0][k], FHL[1][k]),
                                     k == 0, k == tiles - 1)
                        if b % 16 == 15:
                            chunk_done(mm)

            def scalar(act):
                chunk_hi(act, base)
                chunk_hi(act, base + 1)
                for first, tiles, t0 in parts:
                    for n in range(tiles):
                        c = first + n
                        act.wait_ge(sem("chunk_done"), c + 1)
                        if t0 + n >= 2:
                            act.wait_ge(S("value"), t0 + n - 1)
                        act.activation(FS[n % 2], acc(n)[:, 0:512], ACT.Silu).then_inc(S("silu"), 1)
                        chunk_hi(act, c + 2)
                        act.wait_ge(S("value"), t0 + n + 1)
                        act.activation(FHL[0][n], FV[n % 2], ACT.Copy).then_inc(S("hid_hi"), 1)
                    for c in range(first + tiles, first + tiles * 3 // 2):
                        if c + 2 < base + 33:
                            chunk_hi(act, c + 2)

            def gpsimd(pool):
                for c in range(base, base + 33):
                    chunk_lo(pool, c)

            def vector(dve):
                for part, (first, tiles, t0) in enumerate(parts):
                    def low(n):
                        dve.wait_ge(S("hid_hi"), t0 + n + 1)
                        dve.tensor_tensor(FHL[1][n], FV[n % 2], FHL[0][n].bitcast(F32),
                                          ALU.subtract).then_inc(S("hid_lo"), 1)

                    for n in range(tiles):
                        dve.wait_ge(S("silu"), t0 + n + 1)
                        if t0 + n >= 2:
                            dve.wait_ge(S("hid_lo"), t0 + n - 1)
                        dve.tensor_tensor(FV[n % 2], acc(n)[:, 512:1024], FS[n % 2], ALU.mult).then_inc(S("value"), 1)
                        if n:
                            low(n - 1)
                    low(tiles - 1)
                    for o in range(KT):
                        dve.wait_ge(sem("chunk_done"), first + tiles + (tiles * o + tiles - 1) // 16 + 1)
                        if part == 1:
                            dve.wait_ge(S("down"), o + 1)
                        dve.tensor_tensor(XT[:, o, :], XT[:, o, :], down(o), ALU.add).then_inc(S("down"), 1)

            phases.append(dict(tensor=tensor, scalar=scalar, vector=vector, gpsimd=gpsimd))

        norm(XT, T, None, lambda k: v("ffn_norm", k, 1), halves=HHL)
        swiglu(0, CH_FF0)

        LH = (rounded_rows(R + 26624, KT), rounded_rows(4096, KT))
        norm(XT, T, None, lambda k: v("attn_norm", 8 + k, 1), halves=LH)
        LQ = view(R, GH, T)
        LK = view(R + 2048, GH, T)
        LV = view(R + 4096, TT, D)
        OG = view(R + 8192, KT, T)
        LA = view(R + 12288, 2, TT, 512)
        LTMP = view(R + 22048, 4096)
        ZT = view(R + 16384, T)
        WG = view(R + 16896, 512)

        def lin_load_gpsimd(pool):
            pool.memset(ZT[0:64, :], 1.0)
            for d in range(2):
                pool.dma_start(WG[32 * d:32 * d + 17, :], w_gate_fb[d]).then_inc(sem("lin_loaded"), 16)
            pool.wait_ge(sem("lin_loaded"), 32)

        phases[-1]["gpsimd"] = lin_load_gpsimd

        def lin_tensor(pe):
            for d in range(2):
                for k in range(KT):
                    for i in range(2):
                        mm = pe.matmul(pf[32 * d:32 * d + 16, 3072:3584], wdt[:, k, 16 * d:16 * d + 16],
                                       LH[i][k].bitcast(F32), start=(k == 0 and i == 0),
                                       stop=(k == KT - 1 and i == 1))
            mm.then_inc(sem("lin_z"), 1)
            pe.wait_ge(sem("lin_zt"), 1)
            for i in range(8):
                d, t = divmod(i, TT)
                if i >= 2:
                    pe.wait_ge(sem("lin_raw"), i - 1)
                pe.matmul(bank(6 + i % 2), ZT[32 * d:32 * d + 17, t * P:t * P + P], WG[32 * d:32 * d + 17, :],
                          start=True, stop=True).then_inc(sem("lin_gate"), 1)
            for n in range(8):
                c = CH_GLA + n
                halves_ready(pe, c)
                if n >= 2:
                    pe.wait_ge(sem("lin_evac"), n - 1)
                if n < 4:
                    for j in range(2):
                        for k in range(KT):
                            mm = product(pe, acc2(n)[:, j * 512:j * 512 + 512], c, k * 256 + j * P, (LH[0][k], LH[1][k]),
                                         k == 0, k == KT - 1)
                else:
                    for t in range(TT):
                        for k in range(KT):
                            tokens = [half[k][:, t * P:t * P + P] for half in LH]
                            mm = product3(pe, acc2(n)[:, t * 256:t * 256 + 256], tokens, weight(c, k * 256, 256),
                                          k == 0, k == KT - 1)
                chunk_done(mm)

        def lin_scalar(act):
            chunk_hi(act, CH_GLA)
            chunk_hi(act, CH_GLA + 1)
            act.wait_ge(sem("lin_z"), 1)
            for d in range(2):
                ins = act.activation(ZT[32 * d:32 * d + 16, :], pf[32 * d:32 * d + 16, 3072:3584], ACT.Copy)
            ins.then_inc(sem("lin_zt"), 1)
            for i in range(8):
                act.wait_ge(sem("lin_gate"), i + 1)
                act.activation(LA[:, i // TT, i % TT, :], bank(6 + i % 2), ACT.Copy).then_inc(sem("lin_raw"), 1)
            act.wait_ge(sem("lin_abs"), 1)
            act.activation(LTMP, LTMP, ACT.Exp).then_inc(sem("lin_exp"), 1)
            act.wait_ge(sem("lin_exp"), 1)
            act.activation(LTMP, LTMP, ACT.Ln, bias=1.0).then_inc(sem("lin_ln"), 1)
            for n in range(8):
                act.wait_ge(sem("chunk_done"), CH_GLA + n + 1)
                if n + 2 < 8:
                    chunk_hi(act, CH_GLA + n + 2)
                if n < 4:
                    dst = (LQ, LK)[n // 2][:, 2 * (n % 2):2 * (n % 2) + 2, :]
                    act.activation(dst, split(acc2(n), 2, T), ACT.Copy).then_inc(sem("lin_evac"), 1)
                else:
                    act.activation(LV[:, :, (n - 4) * 256:(n - 3) * 256], split(acc2(n), TT, 256),
                                   ACT.Copy).then_inc(sem("lin_evac"), 1)

        def lin_vector(dve):
            la = LA.rearrange("p a b c -> p (a b c)")
            dve.wait_ge(sem("lin_raw"), 8)
            dve.scalar_tensor_tensor(LTMP, la, -1.0, la, ALU.mult, ALU.min).then_inc(sem("lin_abs"), 1)
            dve.wait_ge(sem("lin_ln"), 1)
            dve.scalar_tensor_tensor(la, la, 0.0, LTMP, ALU.min, ALU.subtract)

        def lin_gpsimd(pool):
            for c in range(CH_GLA, CH_GLA + 8):
                chunk_lo(pool, c)

        phases.append(dict(tensor=lin_tensor, scalar=lin_scalar, vector=lin_vector, gpsimd=lin_gpsimd))

        NC = T // GC
        QTL = [view(R + 16384 + 512 * d, T) for d in range(2)]
        KTL = [view(R + 17408 + 512 * d, T) for d in range(2)]
        KEL = [view(R + 18432 + 512 * d, T) for d in range(2)]
        KET = [view(R + 19456 + 512 * d, TT, P) for d in range(2)]
        AM = [view(R + 20480 + 256 * d, TT, GC) for d in range(2)]
        AMS = view(R + 30720, TT, P)
        BLS = view(R + 20992, 2, NC)
        DEC = view(R + 21008, 2, NC)
        EBL = [view(R + 21024 + 512 * d, T) for d in range(2)]
        SIN = [view(R + 22048 + 2048 * d, NC, 256) for d in range(2)]
        ORDER = (list(range(NC)), list(range(NC))[::-1])
        KVS = [(d, i) for i in range(NC - 1) for d in range(2)]

        def gla_tensor(pe):
            for h in range(GH):
                for d in range(2):
                    if h >= 1 and d == 0:
                        pe.wait_ge(sem("gla_o"), h)
                    for t in range(TT):
                        mm = pe.matmul(bank(d, P, t * P), LA[:, d, t, h * P:h * P + P],
                                       C[("gtriu", "gtril")[d]], start=True, stop=True)
                    mm.then_inc(sem("gla_b"), 1)
                for d in range(2):
                    i = 2 * h + d
                    pe.wait_ge(sem("gla_q"), i + 1)
                    pe.wait_ge(sem("gla_k"), i + 1)
                    for c in range(NC):
                        o = pf[64 * (c % 2):64 * (c % 2) + 64, (2 + d) * 512 + (c // 2) * GC:(2 + d) * 512 + (c // 2) * GC + GC]
                        mm = pe.matmul(o, KTL[d][:, c * GC:c * GC + GC], QTL[d][:, c * GC:c * GC + GC],
                                       start=True, stop=True)
                    mm.then_inc(sem("gla_attn"), 1)
                    pe.wait_ge(sem("gla_kend"), i + 1)
                    for t in range(TT):
                        mm = pe.transpose(bank(4 + d, P, t * P), KEL[d][:, t * P:t * P + P], C["ident"])
                    mm.then_inc(sem("gla_kturn"), 1)
                pe.wait_ge(sem("gla_kturned"), 2 * h + 2)
                for x, (d, i) in enumerate(KVS):
                    n = len(KVS) * h + x
                    c = ORDER[d][i]
                    rows = slice(64 * (c % 2), 64 * (c % 2) + 64)
                    if n >= 2:
                        pe.wait_ge(sem("gla_state"), n - 1)
                    pe.matmul(bank(6 + x % 2, 256), KET[d][rows, c // 2, :], LV[rows, c // 2, h * 256:h * 256 + 256],
                              start=True, stop=True).then_inc(sem("gla_kv"), 1)
                pe.wait_ge(sem("gla_summed"), h + 1)
                pe.wait_ge(sem("gla_state"), len(KVS) * (h + 1))
                for e in range(2):
                    for t in range(TT):
                        pe.matmul(bank(e, P, t * P), LV[:, t, h * 256 + e * P:h * 256 + e * P + P], AMS[:, t, :],
                                  start=(t == 0), stop=False, skip_group_check=True)
                        steps = [(c, d) for c in (2 * t, 2 * t + 1) for d in range(2) if c != ORDER[d][0]]
                        for c, d in steps:
                            mm = pe.matmul(bank(e, GC, c * GC), SIN[d][:, c, e * P:e * P + P],
                                           QTL[d][:, c * GC:c * GC + GC], start=False,
                                           stop=(t == TT - 1 and (c, d) == steps[-1]),
                                           skip_group_check=True)
                mm.then_inc(sem("gla_omm"), 1)

        def gla_vector(dve):
            for d in range(2):
                dve.memset(AM[d].rearrange("p a b -> p (a b)"), 0.0)
                dve.memset(AMS.rearrange("p a b -> p (a b)")[:, 256 * d:256 * d + 256], 0.0)
                ins = dve.memset(SIN[d][:, ORDER[d][0], :], 0.0)
            ins.then_inc(sem("gla_zeroed"), 1)
            dve.wait_ge(sem("gla_zeroed"), 1)
            for h in range(GH):
                for d in range(2):
                    i = 2 * h + d
                    last = bank(d)[:, 63:T:64] if d == 0 else bank(d)[:, 0:T:64]
                    dve.wait_ge(sem("gla_b"), i + 1)
                    if h >= 1:
                        dve.wait_ge(sem("gla_kturn"), i - 1)
                    dve.tensor_copy(BLS[:, d, :], last).then_inc(sem("gla_last"), 1)
                    dve.wait_ge(sem("gla_last"), i + 1)
                    dve.tensor_tensor(split(KEL[d], NC, GC), BLS[:, d, :].unsqueeze(2).to_broadcast([P, NC, GC]),
                                      split(bank(d), NC, GC), ALU.subtract).then_inc(sem("gla_diff"), 1)
                for d in range(2):
                    i = 2 * h + d
                    dve.wait_ge(sem("gla_eb"), i + 1)
                    dve.scalar_tensor_tensor(QTL[d], LQ[:, h, :], float(P) ** -0.5, EBL[d], ALU.mult,
                                             ALU.mult).then_inc(sem("gla_q"), 1)
                for d in range(2):
                    dve.wait_ge(sem("gla_attn"), 2 * h + d + 1)
                    dve.copy_predicated(AM[d], gmask[:, d:d + 1, :].to_broadcast([P, TT, GC]),
                                        split(bank(2 + d, 256), TT, GC)).then_inc(sem("gla_masked"), 1)
                dve.wait_ge(sem("gla_masked"), 2 * h + 2)
                if h >= 1:
                    dve.wait_ge(sem("gla_omm"), h)
                for odd in range(2):
                    rows = slice(64 * odd, 64 * odd + 64)
                    ins = dve.tensor_tensor(AMS[rows, :, 64 * odd:64 * odd + 64], AM[0][rows], AM[1][rows], ALU.add)
                ins.then_inc(sem("gla_summed"), 1)
                for x, (d, i) in enumerate(KVS):
                    c, nxt = ORDER[d][i], ORDER[d][i + 1]
                    n = len(KVS) * h + x
                    dve.wait_ge(sem("gla_kv"), n + 1)
                    if i >= 1:
                        dve.wait_ge(sem("gla_state"), n - 1)
                    dve.scalar_tensor_tensor(SIN[d][:, nxt, :], SIN[d][:, c, :], DEC[:, d, c:c + 1],
                                             bank(6 + x % 2, 256), ALU.mult, ALU.add).then_inc(sem("gla_state"), 1)

        def gla_scalar(act):
            for h in range(GH):
                for d in range(2):
                    i = 2 * h + d
                    act.wait_ge(sem("gla_diff"), i + 1)
                    act.activation(KEL[d], KEL[d], ACT.Exp).then_inc(sem("gla_ekend"), 1)
                    act.activation(DEC[:, d, :], BLS[:, d, :], ACT.Exp)
                    if h >= 1:
                        act.wait_ge(sem("gla_attn"), i - 1)
                    act.activation(KTL[d], bank(d), ACT.Exp, scale=-1.0).then_inc(sem("gla_enb"), 1)
                    act.activation(EBL[d], bank(d), ACT.Exp).then_inc(sem("gla_eb"), 1)
                for d in range(2):
                    i = 2 * h + d
                    act.wait_ge(sem("gla_kturn"), i + 1)
                    act.activation(KET[d].rearrange("p a b -> p (a b)"), bank(4 + d), ACT.Copy).then_inc(sem("gla_kturned"), 1)
                act.wait_ge(sem("gla_omm"), h + 1)
                act.activation(OG[:, 2 * h:2 * h + 2, :], split(pf[:, 0:1024], 2, T), ACT.Copy).then_inc(sem("gla_o"), 1)

        def gla_gpsimd(pool):
            for h in range(GH):
                for d in range(2):
                    i = 2 * h + d
                    pool.wait_ge(sem("gla_ekend"), i + 1)
                    pool.tensor_tensor(KEL[d], KEL[d], LK[:, h, :], ALU.mult).then_inc(sem("gla_kend"), 1)
                    pool.wait_ge(sem("gla_enb"), i + 1)
                    pool.tensor_tensor(KTL[d], KTL[d], LK[:, h, :], ALU.mult).then_inc(sem("gla_k"), 1)

        phases.append(dict(tensor=gla_tensor, scalar=gla_scalar, vector=gla_vector, gpsimd=gla_gpsimd))

        LS = [view(R + 1024 * i, 2, T) for i in range(2)]
        LSQ = [view(R + 2048 + 1024 * i, 2, T) for i in range(2)]
        LR = [view(R + 4096 + 512 * i, T) for i in range(2)]

        def lgate_tensor(pe):
            for g in range(GH):
                c = CH_GLAR + g
                halves_ready(pe, c)
                if g >= 2:
                    pe.wait_ge(sem("lg_silu"), g - 1)
                for j in range(2):
                    for k in range(KT):
                        mm = product(pe, acc(g)[:, j * 512:j * 512 + 512], c, k * 256 + j * P, (LH[0][k], LH[1][k]),
                                     k == 0, k == KT - 1)
                chunk_done(mm)
                pe.wait_ge(sem("lg_sq"), g + 1)
                if g >= 2:
                    pe.wait_ge(sem("lg_ln"), g - 1)
                for j in range(2):
                    mm = pe.matmul(bank(6 + g % 2), C["ones"], LSQ[g % 2][:, j, :], start=(j == 0), stop=(j == 1))
                mm.then_inc(sem("lg_sums"), 1)

        def lgate_gpsimd(pool):
            for c in range(CH_GLAR, CH_GLAR + 4):
                chunk_lo(pool, c)

        def lgate_scalar(act):
            chunk_hi(act, CH_GLAR)
            chunk_hi(act, CH_GLAR + 1)
            for g in range(GH):
                if g >= 2:
                    act.wait_ge(sem("lg_sums"), g - 1)
                    act.wait_ge(sem("lg_out"), g - 1)
                act.activation(LSQ[g % 2], OG[:, 2 * g:2 * g + 2, :], ACT.Square).then_inc(sem("lg_sq"), 1)
                act.wait_ge(sem("chunk_done"), CH_GLAR + g + 1)
                if g + 2 < 4:
                    chunk_hi(act, CH_GLAR + g + 2)
                act.activation(LS[g % 2], split(acc(g)[:, 0:1024], 2, T), ACT.Silu).then_inc(sem("lg_silu"), 1)
                load_exp_ln(act)
                act.wait_ge(sem("lg_sums"), g + 1)
                act.activation(LR[g % 2], bank(6 + g % 2), ACT.Ln, scale=1.0 / 256, bias=epst[:, :]).then_inc(sem("lg_ln"), 1)
                act.wait_ge(sem("lg_ln"), g + 1)
                act.activation(LR[g % 2], LR[g % 2], ACT.Exp, scale=-0.5).then_inc(sem("lg_rstd"), 1)

        def lgate_vector(dve):
            link = Link(dve, "lg_link")
            for g in range(GH):
                y = OG[:, 2 * g:2 * g + 2, :]
                dve.wait_ge(sem("lg_rstd"), g + 1)
                for j in range(2):
                    ins = dve.scalar_tensor_tensor(y[:, j, :], y[:, j, :], v("b_out_norm", 2 * g + j, 1), LR[g % 2],
                                                   ALU.mult, ALU.mult)
                link(ins)
                dve.wait_ge(sem("lg_silu"), g + 1)
                dve.tensor_tensor(y, y, LS[g % 2], ALU.mult).then_inc(sem("lg_out"), 1)

        phases.append(dict(tensor=lgate_tensor, scalar=lgate_scalar, vector=lgate_vector, gpsimd=lgate_gpsimd))
        project_out("gla_proj", CH_GLAO, R + 8192, R + 12288)
        norm(XT, T, None, lambda k: v("ffn_norm", 8 + k, 1), halves=HHL)
        swiglu(1, CH_FF1)

        def meet(eng, n):
            eng.drain().then_inc(sem("stage_ended"), 1)
            eng.wait_ge(sem("stage_ended"), 4 * (n + 1))

        def run(eng, name):
            for n, stage in enumerate(phases[:stop]):
                if name in stage:
                    stage[name](eng)
                meet(eng, n)
                if n == BLOCK1_STAGES - 1:
                    if name == "gpsimd":
                        for old in BLOCK1_SEMS:
                            eng.sem_clear(sem(old))
                        eng.drain().then_inc(sem("semaphores_cleared"), 1)
                    eng.wait_ge(sem("semaphores_cleared"), 1)

        block = ctx.enter_context(nc.Block())

        @block.sync
        def _(sp):
            ada_sync(sp)
            for c in range(CH_END if stop is None else LIMIT):
                if c == CH_SH + 3:
                    moe_sync(sp)
                last = c - NSLOT
                if last in SPLIT and run_of(last) in LO_APART:
                    sp.wait_ge(sem("chunk_lo"), SPLIT.index(last) + 1)
                elif last >= 0:
                    sp.wait_ge(sem("chunk_done"), last + 1)
                sp.dma_start(ring[:, c % NSLOT, :], wstream[c]).then_inc(sem(f"slot{c % NSLOT}_full"), 16)
            if stop is None:
                sp.wait_ge(sem("stage_ended"), 4 * len(phases))
                sp.dma_start(out_t, XT).then_inc(sem("out"), 16)
                sp.wait_ge(sem("out"), 16)
            else:
                sp.wait_ge(sem("stage_ended"), 4 * len(phases[:stop]))
                sp.dma_start(dbg, arena[:, :]).then_inc(sem("out"), 16)
                sp.dma_start(out_t, arena[:, 0:4096].rearrange("p (k t) -> p k t", t=T)).then_inc(sem("out"), 16)
                sp.wait_ge(sem("out"), 32)

        @block.tensor
        def _(pe):
            run(pe, "tensor")

        @block.scalar
        def _(act):
            run(act, "scalar")

        @block.vector
        def _(dve):
            run(dve, "vector")

        @block.gpsimd
        def _(pool):
            run(pool, "gpsimd")


def program(nc, a, out_t, dbg=None, stop=None):
    xs = nc.dram_tensor("xs", (MAXBLK * P, D), F32, kind="Internal").ap()
    ys = nc.dram_tensor("ys", (MAXBLK * P, D), F32, kind="Internal").ap()
    x_saved = nc.dram_tensor("x_saved", (P, KT, T), F32, kind="Internal").ap()
    two_blocks(nc, a["wstream"], a["x_t"], a["ctx_t"], a["vecs"], a["consts"], a["rope_t"], a["gmask_t"],
               a["dmask_t"], a["iota_t"], a["w_dt"], a["w_router"], a["we_gu"], a["we_down"], a["w_z"],
               a["w_gate_fb"], xs, ys, x_saved, out_t, dbg, stop)


def _tables(np):
    i = np.arange(P)
    eye = np.eye(P)
    rot = np.zeros((P, P))
    for h in range(2):
        for j in range(32):
            rot[64 * h + 32 + j, 64 * h + j] = -1.0
            rot[64 * h + j, 64 * h + 32 + j] = 1.0
    pair = (i[:, None] // 64 == i[None, :] // 64) * 1.0
    triu = (i[:, None] <= i[None, :]) * 1.0
    mats = [eye, np.ones((P, P)), rot, pair, triu, triu.T, triu - eye, triu * pair / 16.0, triu.T * pair / 16.0]
    consts = np.stack(mats, axis=1).astype(np.float32)

    def cs(ang):
        ang = np.concatenate([ang, ang, ang, ang], axis=-1)
        return np.stack([np.cos(ang).T, np.sin(ang).T], axis=1).astype(np.float32)

    t = np.arange(T, dtype=np.float32)
    inv1 = np.float32(10000.0) ** (-np.arange(0, 32, 2, dtype=np.float32) / np.float32(32))
    ang1 = np.concatenate([np.floor(t / 64)[:, None] * inv1, (t % 64)[:, None] * inv1], axis=-1)
    inv2 = np.float32(10000.0) ** (-np.arange(32, dtype=np.float32) / np.float32(32))
    ang2 = t[:, None] * inv2[None, :]
    s, q = i[:, None] % 64, np.arange(64)[None, :]
    gmask = np.stack([s <= q, s > q], axis=1).astype(np.uint32)
    big = np.float32(-1e30)
    m0 = [np.where(np.abs(np.arange(T)[None, :] - (4 * i + r)[:, None]) <= 64, 0, big) for r in range(4)]
    m1 = np.where(np.abs(i[None, :] - i[:, None]) <= 64, 0, big)
    m2 = np.where((i[None, :] - i[:, None]) % 4 == 0, 0, big)
    dmask = np.concatenate(m0 + [m1, m2, eye], axis=1)
    return consts, cs(ang1), cs(ang2), gmask, dmask


def kernel(**inputs):
    import ml_dtypes
    import numpy as np
    import concourse.bacc as bacc
    from concourse.bass_utils import run_bass_kernel_spmd as launch

    g = {n: np.asarray(a) for n, a in inputs.items()}

    def feat(a):
        return np.ascontiguousarray(a.reshape(a.shape[0], -1, P).transpose(2, 1, 0))

    def vecf(a):
        return a.reshape(-1, P).T

    def chunks(w):
        return w.reshape(KT, P, -1, 256).transpose(2, 1, 0, 3).reshape(-1, P, CHW)

    def ffn(gu, down):
        gu, out, t0 = chunks(gate_up(gu)), [], 0
        for n in FF_PARTS:
            b = down[t0 * P:(t0 + n) * P].reshape(n, P, KT, P).transpose(2, 0, 1, 3).reshape(-1, 16, P, P)
            out += [gu[t0:t0 + n], b.transpose(0, 2, 1, 3).reshape(-1, P, CHW)]
            t0 += n
        return np.concatenate(out)

    def gate_up(w):
        return w.reshape(D, 2, -1, P).transpose(0, 2, 1, 3).reshape(D, -1)

    w_in = g["w_in"][0]
    wg, wa, wsd = w_in[:, 6176:8224], g["w_branch_attn"][0], g["w_branch_ssd"][0]
    merge = np.stack([w.reshape(D, 4, 256) for w in (wg[:, :D], wa, wg[:, D:], wsd)], axis=2).reshape(D, -1)
    a_in = g["a_w_in_2"][0].reshape(D, 9, 4, 256).transpose(0, 2, 1, 3).reshape(D, -1)
    b_in = g["b_w_in_2"][0]
    w_ada = chunks(g["w_ada"][0])
    stream = [w_ada[:8], chunks(w_in[:, :3072]), w_ada[8:], chunks(w_in[:, 4096:6144]), chunks(w_in[:, 3072:4096]),
              chunks(merge), chunks(g["w_out"][0]), chunks(g["w_sh_gate"][0]), chunks(g["w_sh_up"][0]),
              g["w_sh_down"][0].reshape(2, P, D).transpose(1, 0, 2).reshape(1, P, CHW),
              chunks(a_in), chunks(g["a_w_out_2"][0]),
              ffn(g["ffn_w_gate_up_2"][0], g["ffn_w_down_2"][0]),
              chunks(b_in[:, 0:2048]), chunks(b_in[:, 2048:3072]), chunks(g["b_w_out_2"][0]),
              ffn(g["ffn_w_gate_up_2"][1], g["ffn_w_down_2"][1])]
    wstream = np.concatenate(stream, axis=0)
    assert wstream.shape[0] == CH_END

    def row(a):
        return np.broadcast_to(a.reshape(1, -1), (P, a.size))

    cols = {
        "cc": feat(np.stack([g["c"][0], g["c_ctx"]])).reshape(P, 16), "b_ada": vecf(g["b_ada"][0]),
        "g_pre_mix": vecf(g["g_pre_mix"][0]), "g_post_mix": vecf(g["g_post_mix"][0]),
        "g_pre_ffn": vecf(g["g_pre_ffn"][0]), "g_post_ffn": vecf(g["g_post_ffn"][0]),
        "g_subln": g["g_attn_subln"][0][:, None], "conv_w": vecf(g["conv_w"][0].reshape(-1)),
        "conv_b": vecf(g["conv_b"][0]), "d_skip": vecf(np.repeat(g["d_skip"][0], 64)),
        "g_ssd": vecf(g["g_ssd_norm"][0]), "attn_norm": vecf(g["attn_norm_2"].reshape(-1)),
        "ffn_norm": vecf(g["ffn_norm_2"].reshape(-1)), "a_q_norm": np.tile(g["a_q_norm_2"][0], (1, 2)).T,
        "a_k_norm": np.tile(g["a_k_norm_2"][0], (1, 2)).T, "b_out_norm": vecf(g["b_out_norm_2"][0].reshape(-1)),
        "lam": row(np.concatenate([g["lam_q1"][0], g["lam_k1"][0], g["lam_q2"][0], g["lam_k2"][0]])),
        "dt_bias": row(g["dt_bias"][0]), "a_log": row(g["a_log"][0]), "router_bias": row(g["router_bias"][0]),
    }
    vecs = np.concatenate([cols[n] for n in VEC], axis=1).astype(np.float32)
    consts, rope1, rope2, gmask, dmask = _tables(np)
    w_gate_fb = np.stack([np.concatenate([g["b_w_gate_f_2"][0], g["b_gate_bias_f_2"]]),
                          np.concatenate([g["b_w_gate_b_2"][0], g["b_gate_bias_b_2"]])])
    arrays = {
        "wstream": wstream, "x_t": feat(g["x"][0]), "ctx_t": feat(g["ctx"][0]), "vecs": vecs, "consts": consts,
        "rope_t": np.stack([rope1, rope2]), "gmask_t": gmask, "dmask_t": dmask.astype(ml_dtypes.bfloat16),
        "iota_t": np.ascontiguousarray(row(np.concatenate([np.tril(np.ones((8, 8)), -1).reshape(-1), np.arange(MAXBLK)])
                                          .astype(np.float32))),
        "w_dt": np.ascontiguousarray(w_in[:, 6144:6176].reshape(KT, P, 32).transpose(1, 0, 2)),
        "w_router": np.ascontiguousarray(g["w_router"][0].reshape(KT, P, E_N).transpose(1, 0, 2)),
        "we_gu": np.ascontiguousarray(np.concatenate([g["w_e_gate"][0], g["w_e_up"][0]], axis=-1)
                                      .reshape(E_N, KT, P, 512).transpose(0, 2, 1, 3)).reshape(E_N, P, KT * 512),
        "we_down": np.ascontiguousarray(g["w_e_down"][0].reshape(E_N, 2, P, D).transpose(0, 2, 1, 3)).reshape(E_N, P, 2 * D),
        "w_z": np.ascontiguousarray(b_in[:, 3072:3104].reshape(KT, P, 32).transpose(1, 0, 2)),
        "w_gate_fb": w_gate_fb,
    }
    nc = bacc.Bacc("TRN2", target_bir_lowering=False, num_devices=1)
    aps = {n: nc.dram_tensor(n, a.shape, mybir.dt.from_np(a.dtype), kind="ExternalInput").ap()
           for n, a in arrays.items()}
    out_t = nc.dram_tensor("out_t", (P, KT, T), F32, kind="ExternalOutput").ap()
    program(nc, aps, out_t)
    r = launch(nc, [arrays], core_ids=[0])
    got = r.results[0]["out_t"]
    return np.ascontiguousarray(got.transpose(2, 1, 0).reshape(1, T, D))
```
